# Optimizing a Trainium2 kernel written in Bass

```python
import jax
import jax.numpy as jnp
from jax import lax
import numpy as np
import jax, jax.numpy as jnp

D_MODEL = 1024
BATCH = 1
SEQ = 256
DEPTH = 2

N_MIXERS = 2
N_ATTN_LAYERS = (DEPTH + 1) // 2
N_MLSTM_LAYERS = DEPTH // 2

DIL_CONFIGS = ((128, 1), (512, 4), (2048, 16))
N_GROUPS = len(DIL_CONFIGS)
ATTN_HEADS = 8
ATTN_HEAD_DIM = 128
ATTN_WIDTH = ATTN_HEADS * ATTN_HEAD_DIM
ATTN_IN_WIDTH = N_GROUPS * 3 * ATTN_WIDTH
ROT_DIM = ATTN_HEAD_DIM // 4
ROPE_THETA = 500000.0
BLOCK = 128

MLSTM_HEADS = 8
MLSTM_QK_DIM = D_MODEL // 2 // MLSTM_HEADS
MLSTM_V_DIM = D_MODEL // MLSTM_HEADS
QK_WIDTH = MLSTM_HEADS * MLSTM_QK_DIM
MLSTM_IN_WIDTH = 2 * QK_WIDTH + 2 * D_MODEL + 2 * MLSTM_HEADS
MLSTM_CHUNK = 64
CONV_WIDTH = 4

D_FF = -(-8 * D_MODEL // (3 * 256)) * 256

RMS_EPS = 1e-6


def rms_norm(x, g):
    xf = x.astype(jnp.float32)
    y = xf * lax.rsqrt(jnp.mean(xf * xf, axis=-1, keepdims=True) + RMS_EPS)
    return y.astype(x.dtype) * g.astype(x.dtype)

def apply_partial_rope(t, positions):
    half = ROT_DIM // 2
    inv_freq = ROPE_THETA ** (-jnp.arange(half, dtype=jnp.float32) * 2.0 / ROT_DIM)
    ang = positions.astype(jnp.float32)[..., None] * inv_freq
    cos = jnp.cos(ang)[:, :, None, :]
    sin = jnp.sin(ang)[:, :, None, :]
    tf = t.astype(jnp.float32)
    x1 = tf[..., :half]
    x2 = tf[..., half:ROT_DIM]
    out = jnp.concatenate([x1 * cos - x2 * sin, x2 * cos + x1 * sin, tf[..., ROT_DIM:]], axis=-1)
    return out.astype(t.dtype)

def banded_window_attention(q, k, v, window):
    *lead, L, hd = q.shape
    nb = -(-L // BLOCK)
    Lp = nb * BLOCK
    pad = [(0, 0)] * len(lead) + [(0, Lp - L), (0, 0)]

    def blocks(t):
        return jnp.pad(t, pad).reshape(*lead, nb, BLOCK, hd)

    def with_prev(t):
        prev = jnp.concatenate([jnp.zeros_like(t[..., :1, :, :]), t[..., :-1, :, :]], axis=-3)
        return jnp.concatenate([prev, t], axis=-2)

    qb = blocks(q)
    kk = with_prev(blocks(k))
    vv = with_prev(blocks(v))
    s = jnp.einsum('...iqd,...ikd->...iqk', qb, kk).astype(jnp.float32)
    blk = jnp.arange(nb)[:, None, None]
    a = jnp.arange(BLOCK)[None, :, None]
    c = jnp.arange(2 * BLOCK)[None, None, :]
    dist = a + BLOCK - c
    valid = (dist >= 0) & (dist <= window) & ((blk - 1) * BLOCK + c >= 0)
    s = jnp.where(valid, s, -jnp.inf)
    m = jnp.max(s, axis=-1, keepdims=True)
    p = jnp.exp(s - m)
    den = jnp.sum(p, axis=-1, keepdims=True)
    o = jnp.einsum('...iqk,...ikd->...iqd', (p / den).astype(v.dtype), vv)
    lse = (m + jnp.log(den))[..., 0]
    o = o.reshape(*lead, Lp, hd)[..., :L, :]
    lse = lse.reshape(*lead, Lp)[..., :L]
    return o, lse

def dilated_window_attention(q, k, v, window, dilation):
    B, S, H, hd = q.shape
    L = S // dilation

    def to_sub(t):
        return t.reshape(B, L, dilation, H, hd).transpose(0, 2, 3, 1, 4)

    o, lse = banded_window_attention(to_sub(q), to_sub(k), to_sub(v), window // dilation)
    o = o.transpose(0, 3, 1, 2, 4).reshape(B, S, H, hd)
    lse = lse.transpose(0, 3, 1, 2).reshape(B, S, H)
    return o, lse

def dilated_attention_mixer(xn, positions, w_in, w_out):
    B, S, _ = xn.shape
    proj = (xn @ w_in).reshape(B, S, N_GROUPS, 3, ATTN_HEADS, ATTN_HEAD_DIM)
    scale = ATTN_HEAD_DIM ** -0.5
    outs = []
    lses = []
    for g, (window, dilation) in enumerate(DIL_CONFIGS):
        q = apply_partial_rope(proj[:, :, g, 0], positions) * scale
        k = apply_partial_rope(proj[:, :, g, 1], positions)
        v = proj[:, :, g, 2]
        o, lse = dilated_window_attention(q, k, v, window, dilation)
        outs.append(o)
        lses.append(lse)
    wts = jax.nn.softmax(jnp.stack(lses), axis=0)
    o = jnp.einsum('gbsh,gbshd->bshd', wts.astype(xn.dtype), jnp.stack(outs))
    return o.reshape(B, S, ATTN_WIDTH) @ w_out

def causal_depthwise_conv(t, w, b):
    out = lax.conv_general_dilated(
        t, w[:, None, :].astype(t.dtype), window_strides=(1,),
        padding=[(CONV_WIDTH - 1, 0)], dimension_numbers=('NWC', 'WIO', 'NWC'),
        feature_group_count=t.shape[-1])
    return out + b.astype(t.dtype)

def mlstm_chunk_step(carry, xs):
    C, n, m = carry
    q, k, v, ig, lf = xs
    L = q.shape[2]
    b = jnp.cumsum(lf, axis=-1)
    causal = jnp.tril(jnp.ones((L, L), dtype=bool))
    dmat = jnp.where(causal, b[..., :, None] - b[..., None, :] + ig[..., None, :], -jnp.inf)
    inter = b + m[..., None]
    m_t = jnp.maximum(inter, jnp.max(dmat, axis=-1))
    w_intra = jnp.exp(dmat - m_t[..., None])
    w_inter = jnp.exp(inter - m_t)
    sm = w_intra * jnp.einsum('bhtd,bhsd->bhts', q, k)
    num = jnp.einsum('bhts,bhsv->bhtv', sm, v) + w_inter[..., None] * jnp.einsum('bhtd,bhdv->bhtv', q, C)
    den = jnp.sum(sm, axis=-1) + w_inter * jnp.einsum('bhtd,bhd->bht', q, n)
    h = num / jnp.maximum(jnp.abs(den), jnp.exp(-m_t))[..., None]
    b_last = b[..., -1]
    decay = b_last[..., None] - b + ig
    m_new = jnp.maximum(b_last + m, jnp.max(decay, axis=-1))
    ws = jnp.exp(decay - m_new[..., None])
    carry_scale = jnp.exp(b_last + m - m_new)
    C_new = carry_scale[..., None, None] * C + jnp.einsum('bhs,bhsd,bhsv->bhdv', ws, k, v)
    n_new = carry_scale[..., None] * n + jnp.einsum('bhs,bhsd->bhd', ws, k)
    return (C_new, n_new, m_new), h

def mlstm_chunkwise(q, k, v, ig, lf):
    B, H, S, dk = q.shape
    dv = v.shape[-1]
    nc = S // MLSTM_CHUNK

    def to_chunks(t):
        return jnp.moveaxis(t.reshape(B, H, nc, MLSTM_CHUNK, *t.shape[3:]), 2, 0)

    init = (jnp.zeros((B, H, dk, dv), jnp.float32), jnp.zeros((B, H, dk), jnp.float32),
            jnp.zeros((B, H), jnp.float32))
    _, h = lax.scan(mlstm_chunk_step, init,
                    (to_chunks(q), to_chunks(k), to_chunks(v), to_chunks(ig), to_chunks(lf)))
    return jnp.moveaxis(h, 0, 2).reshape(B, H, S, dv)

def mlstm_mixer(xn, w_in, conv_w, conv_b, ig_bias, fg_bias, head_gain, w_out):
    B, S, _ = xn.shape
    proj = xn @ w_in
    qk_pre = proj[..., :2 * QK_WIDTH]
    v = proj[..., 2 * QK_WIDTH:2 * QK_WIDTH + D_MODEL]
    o_pre = proj[..., 2 * QK_WIDTH + D_MODEL:2 * QK_WIDTH + 2 * D_MODEL]
    gates = proj[..., 2 * QK_WIDTH + 2 * D_MODEL:].astype(jnp.float32)
    qk = jax.nn.silu(causal_depthwise_conv(qk_pre, conv_w, conv_b))
    ig = gates[..., :MLSTM_HEADS] + ig_bias.astype(jnp.float32)
    lf = jax.nn.log_sigmoid(gates[..., MLSTM_HEADS:] + fg_bias.astype(jnp.float32))

    def heads(t, d):
        return t.reshape(B, S, MLSTM_HEADS, d).transpose(0, 2, 1, 3).astype(jnp.float32)

    q = heads(qk[..., :QK_WIDTH], MLSTM_QK_DIM)
    k = heads(qk[..., QK_WIDTH:], MLSTM_QK_DIM) * (MLSTM_QK_DIM ** -0.5)
    vh = heads(v, MLSTM_V_DIM)
    h = mlstm_chunkwise(q, k, vh, ig.transpose(0, 2, 1), lf.transpose(0, 2, 1))
    h = h.transpose(0, 2, 1, 3)
    h = h * lax.rsqrt(jnp.mean(h * h, axis=-1, keepdims=True) + RMS_EPS)
    h = h.reshape(B, S, D_MODEL).astype(xn.dtype) * head_gain.astype(xn.dtype)
    return (h * jax.nn.sigmoid(o_pre)) @ w_out

def swiglu(xn, w_in, w_out):
    gu = xn @ w_in
    return (jax.nn.silu(gu[..., :D_FF]) * gu[..., D_FF:]) @ w_out

def first_inputs(seed: int = 0) -> dict:
    key = jax.random.key(seed)
    ks = jax.random.split(key, 20)

    def dense(k, shape, fan_in):
        return jax.random.normal(k, shape, jnp.float32) * (fan_in ** -0.5)

    def gain(k, shape):
        return 1.0 + 0.05 * jax.random.normal(k, shape, jnp.float32)

    x = jax.random.normal(ks[0], (BATCH, SEQ, D_MODEL), jnp.float32)
    offset = jax.random.randint(ks[1], (BATCH, 1), 0, 4096, dtype=jnp.int32)
    positions = offset + jnp.arange(SEQ, dtype=jnp.int32)[None, :]
    return {
        'x': x,
        'positions': positions,
        'attn_norm': gain(ks[2], (N_ATTN_LAYERS, D_MODEL)),
        'attn_w_in': dense(ks[3], (N_ATTN_LAYERS, D_MODEL, ATTN_IN_WIDTH), D_MODEL),
        'attn_w_out': dense(ks[4], (N_ATTN_LAYERS, ATTN_WIDTH, D_MODEL), ATTN_WIDTH),
        'mlstm_norm': gain(ks[5], (N_MLSTM_LAYERS, D_MODEL)),
        'mlstm_w_in': dense(ks[6], (N_MLSTM_LAYERS, D_MODEL, MLSTM_IN_WIDTH), D_MODEL),
        'mlstm_conv_w': dense(ks[7], (N_MLSTM_LAYERS, CONV_WIDTH, 2 * QK_WIDTH), CONV_WIDTH),
        'mlstm_conv_b': 0.02 * jax.random.normal(ks[8], (N_MLSTM_LAYERS, 2 * QK_WIDTH), jnp.float32),
        'mlstm_ig_bias': 0.1 * jax.random.normal(ks[9], (N_MLSTM_LAYERS, MLSTM_HEADS), jnp.float32),
        'mlstm_fg_bias': 3.0 + 0.1 * jax.random.normal(ks[10], (N_MLSTM_LAYERS, MLSTM_HEADS), jnp.float32),
        'mlstm_head_gain': gain(ks[11], (N_MLSTM_LAYERS, D_MODEL)),
        'mlstm_w_out': dense(ks[12], (N_MLSTM_LAYERS, D_MODEL, D_MODEL), D_MODEL),
        'ffn_norm': gain(ks[13], (DEPTH, D_MODEL)),
        'ffn_w_in': dense(ks[14], (DEPTH, D_MODEL, 2 * D_FF), D_MODEL),
        'ffn_w_out': dense(ks[15], (DEPTH, D_FF, D_MODEL), D_FF),
        'final_norm': gain(ks[16], (D_MODEL,)),
    }

def first_block(x, positions, attn_norm, attn_w_in, attn_w_out, mlstm_norm, mlstm_w_in,
              mlstm_conv_w, mlstm_conv_b, mlstm_ig_bias, mlstm_fg_bias, mlstm_head_gain,
              mlstm_w_out, ffn_norm, ffn_w_in, ffn_w_out, final_norm):
    h = x
    for i in range(DEPTH):
        j = i // N_MIXERS
        if i % N_MIXERS == 0:
            h = h + dilated_attention_mixer(rms_norm(h, attn_norm[j]), positions,
                                            attn_w_in[j], attn_w_out[j])
        else:
            h = h + mlstm_mixer(rms_norm(h, mlstm_norm[j]), mlstm_w_in[j], mlstm_conv_w[j],
                                mlstm_conv_b[j], mlstm_ig_bias[j], mlstm_fg_bias[j],
                                mlstm_head_gain[j], mlstm_w_out[j])
        h = h + swiglu(rms_norm(h, ffn_norm[i]), ffn_w_in[i], ffn_w_out[i])
    return rms_norm(h, final_norm)


DEPTH_2 = 4

CTX_LEN = 256
GRID_W = 64
N_MIXERS_2 = 3
N_HEADS = 16
HEAD_DIM = D_MODEL // N_HEADS
ATTN_SCALE = HEAD_DIM ** -0.5
WIN_ROWS_MAX = 8
WIN_COLS = 16
RPB_ROWS = 2 * WIN_ROWS_MAX - 1
RPB_COLS = 2 * WIN_COLS - 1
CONF_KERNEL = 31
SHORT_KERNEL = 3
D_FF_2 = 4 * D_MODEL
N_MOD = 6
EPS = 1e-6
N_NA = (DEPTH_2 + 2) // 3
N_CONF = (DEPTH_2 + 1) // 3
N_SC = DEPTH_2 // 3


def rmsnorm(x, g):
    xf = x.astype(jnp.float32)
    y = xf * lax.rsqrt(jnp.mean(xf * xf, axis=-1, keepdims=True) + EPS)
    return (y * g.astype(jnp.float32)).astype(x.dtype)

def layernorm(x, g, b):
    xf = x.astype(jnp.float32)
    mu = jnp.mean(xf, axis=-1, keepdims=True)
    xc = xf - mu
    var = jnp.mean(xc * xc, axis=-1, keepdims=True)
    y = xc * lax.rsqrt(var + EPS) * g.astype(jnp.float32) + b.astype(jnp.float32)
    return y.astype(x.dtype)

def modulate(h, shift, scale):
    return h * (1 + scale) + shift

def dwconv(x, w):
    k = w.shape[0]
    return lax.conv_general_dilated(
        x, w[:, None, :].astype(x.dtype), window_strides=(1,),
        padding=[((k - 1) // 2, k // 2)],
        dimension_numbers=("NWC", "WIO", "NWC"),
        feature_group_count=x.shape[-1])

def split_heads(t, n):
    b, l, _ = t.shape
    return t.reshape(b, l, n, N_HEADS, HEAD_DIM).transpose(2, 0, 3, 1, 4)

def neighbourhood_attention(h_lat, h_ctx, wqkv, wo, rpb, ctx_out):
    b, l, d = h_lat.shape
    rows = l // GRID_W
    kh = min(WIN_ROWS_MAX, rows)
    q, k, v = split_heads(h_lat @ wqkv, 3)
    q = q * ATTN_SCALE
    if ctx_out:
        q_c, k_c, v_c = split_heads(h_ctx @ wqkv, 3)
    else:
        k_c, v_c = split_heads(h_ctx @ wqkv[:, D_MODEL:], 2)
    q_grid = q.reshape(b, N_HEADS, rows, GRID_W, HEAD_DIM)
    k_grid = k.reshape(b, N_HEADS, rows, GRID_W, HEAD_DIM)
    v_grid = v.reshape(b, N_HEADS, rows, GRID_W, HEAD_DIM)

    r_ar = np.arange(rows)
    row_start = np.clip(r_ar - kh // 2, 0, rows - kh)
    row_off = row_start[:, None] + np.arange(kh)[None, :] - r_ar[:, None] + WIN_ROWS_MAX - 1
    c_ar = np.arange(GRID_W)
    col_idx = np.clip(c_ar - WIN_COLS // 2, 0, GRID_W - WIN_COLS)[:, None] + np.arange(WIN_COLS)[None, :]
    col_off = col_idx - c_ar[:, None] + WIN_COLS - 1
    bias_all = rpb[:, row_off[:, :, None, None], col_off[None, None, :, :]]
    bias_all = bias_all.transpose(1, 0, 3, 2, 4)
    n_lat = kh * WIN_COLS

    def row_block(xs):
        q_r, rs, bias_r = xs
        k_rows = lax.dynamic_slice_in_dim(k_grid, rs, kh, axis=2)
        v_rows = lax.dynamic_slice_in_dim(v_grid, rs, kh, axis=2)
        k_nb = k_rows[:, :, :, col_idx, :]
        v_nb = v_rows[:, :, :, col_idx, :]
        s_lat = jnp.einsum("bhqd,bhaqkd->bhqak", q_r, k_nb).astype(jnp.float32)
        s_lat = s_lat + bias_r.astype(jnp.float32)[None]
        s_ctx = jnp.einsum("bhqd,bhcd->bhqc", q_r, k_c).astype(jnp.float32)
        s = jnp.concatenate([s_lat.reshape(b, N_HEADS, GRID_W, n_lat), s_ctx], axis=-1)
        p = jax.nn.softmax(s, axis=-1).astype(v_nb.dtype)
        p_lat = p[..., :n_lat].reshape(b, N_HEADS, GRID_W, kh, WIN_COLS)
        p_ctx = p[..., n_lat:]
        return (jnp.einsum("bhqak,bhaqkd->bhqd", p_lat, v_nb)
                + jnp.einsum("bhqc,bhcd->bhqd", p_ctx, v_c))

    o_grid = lax.map(row_block, (jnp.moveaxis(q_grid, 2, 0),
                                 jnp.asarray(row_start, dtype=jnp.int32),
                                 bias_all))
    o_lat = o_grid.transpose(1, 0, 3, 2, 4).reshape(b, l, d) @ wo

    o_ctx = None
    if ctx_out:
        s_c = jnp.einsum("bhqd,bhkd->bhqk", q_c * ATTN_SCALE, k_c).astype(jnp.float32)
        p_c = jax.nn.softmax(s_c, axis=-1).astype(v_c.dtype)
        o_c = jnp.einsum("bhqk,bhkd->bhqd", p_c, v_c)
        o_ctx = o_c.transpose(0, 2, 1, 3).reshape(b, h_ctx.shape[1], d) @ wo
    return o_lat, o_ctx

def conformer_conv(h, w1, b1, dw, dwb, ln_g, ln_b, w2, b2):
    u = h @ w1 + b1
    a, g = jnp.split(u, 2, axis=-1)
    u = a * jax.nn.sigmoid(g)
    u = dwconv(u, dw) + dwb
    u = jax.nn.silu(layernorm(u, ln_g, ln_b))
    return u @ w2 + b2

def short_gated_conv(h, w_in, conv_w, w_out):
    bg, cg, v = jnp.split(h @ w_in, 3, axis=-1)
    return (bg * dwconv(cg * v, conv_w)) @ w_out

def sq_relu_mlp(h, w1, w2):
    return jnp.square(jax.nn.relu(h @ w1)) @ w2

def second_inputs(seed: int = 0) -> dict:
    key = jax.random.key(seed)
    ks = jax.random.split(key, 32)
    nrm = jax.random.normal
    f32 = jnp.float32
    d = D_MODEL
    return {
        "x": nrm(ks[0], (BATCH, SEQ, d), f32),
        "c": nrm(ks[1], (BATCH, d), f32),
        "ctx": nrm(ks[2], (BATCH, CTX_LEN, d), f32),
        "c_ctx": nrm(ks[3], (d,), f32),
        "mod_w": nrm(ks[4], (DEPTH_2, d, N_MOD * d), f32) * (0.5 * d ** -0.5),
        "mod_b": nrm(ks[5], (DEPTH_2, N_MOD * d), f32) * 0.01,
        "norm1_g": 1.0 + 0.01 * nrm(ks[6], (DEPTH_2, d), f32),
        "norm2_g": 1.0 + 0.01 * nrm(ks[7], (DEPTH_2, d), f32),
        "mlp_w1": nrm(ks[8], (DEPTH_2, d, D_FF_2), f32) * d ** -0.5,
        "mlp_w2": nrm(ks[9], (DEPTH_2, D_FF_2, d), f32) * D_FF_2 ** -0.5,
        "na_wqkv": nrm(ks[10], (N_NA, d, 3 * d), f32) * d ** -0.5,
        "na_wo": nrm(ks[11], (N_NA, d, d), f32) * d ** -0.5,
        "na_rpb": nrm(ks[12], (N_NA, N_HEADS, RPB_ROWS, RPB_COLS), f32) * 0.1,
        "cv_w1": nrm(ks[13], (N_CONF, d, 2 * d), f32) * d ** -0.5,
        "cv_b1": nrm(ks[14], (N_CONF, 2 * d), f32) * 0.01,
        "cv_dw": nrm(ks[15], (N_CONF, CONF_KERNEL, d), f32) * CONF_KERNEL ** -0.5,
        "cv_dwb": nrm(ks[16], (N_CONF, d), f32) * 0.01,
        "cv_ln_g": 1.0 + 0.01 * nrm(ks[17], (N_CONF, d), f32),
        "cv_ln_b": nrm(ks[18], (N_CONF, d), f32) * 0.01,
        "cv_w2": nrm(ks[19], (N_CONF, d, d), f32) * d ** -0.5,
        "cv_b2": nrm(ks[20], (N_CONF, d), f32) * 0.01,
        "sc_win": nrm(ks[21], (N_SC, d, 3 * d), f32) * d ** -0.5,
        "sc_conv": nrm(ks[22], (N_SC, SHORT_KERNEL, d), f32) * SHORT_KERNEL ** -0.5,
        "sc_wout": nrm(ks[23], (N_SC, d, d), f32) * d ** -0.5,
        "final_g": 1.0 + 0.01 * nrm(ks[24], (d,), f32),
    }

def second_block(x, c, ctx, c_ctx, mod_w, mod_b, norm1_g, norm2_g, mlp_w1, mlp_w2,
              na_wqkv, na_wo, na_rpb, cv_w1, cv_b1, cv_dw, cv_dwb, cv_ln_g, cv_ln_b,
              cv_w2, cv_b2, sc_win, sc_conv, sc_wout, final_g):
    b = x.shape[0]
    silu_c = jax.nn.silu(c)
    silu_cc = jax.nn.silu(c_ctx)[None]
    last_attn = max(i for i in range(DEPTH_2) if i % N_MIXERS_2 == 0)
    for i in range(DEPTH_2):
        kind = i % N_MIXERS_2
        slot = i // N_MIXERS_2
        ctx_live = i < last_attn
        need_ctx_in = ctx_live or kind == 0
        mod_l = (silu_c @ mod_w[i] + mod_b[i]).reshape(b, N_MOD, 1, D_MODEL)
        a_l = modulate(rmsnorm(x, norm1_g[i]), mod_l[:, 0], mod_l[:, 1])
        a_c = None
        if need_ctx_in:
            mod_c = (silu_cc @ mod_w[i] + mod_b[i]).reshape(1, N_MOD, 1, D_MODEL)
            a_c = modulate(rmsnorm(ctx, norm1_g[i]), mod_c[:, 0], mod_c[:, 1])
        if kind == 0:
            y_l, y_c = neighbourhood_attention(a_l, a_c, na_wqkv[slot], na_wo[slot],
                                               na_rpb[slot], ctx_live)
        elif kind == 1:
            cp = (cv_w1[slot], cv_b1[slot], cv_dw[slot], cv_dwb[slot], cv_ln_g[slot],
                  cv_ln_b[slot], cv_w2[slot], cv_b2[slot])
            y_l = conformer_conv(a_l, *cp)
            y_c = conformer_conv(a_c, *cp) if ctx_live else None
        else:
            sp = (sc_win[slot], sc_conv[slot], sc_wout[slot])
            y_l = short_gated_conv(a_l, *sp)
            y_c = short_gated_conv(a_c, *sp) if ctx_live else None
        x = x + mod_l[:, 2] * y_l
        m_l = modulate(rmsnorm(x, norm2_g[i]), mod_l[:, 3], mod_l[:, 4])
        x = x + mod_l[:, 5] * sq_relu_mlp(m_l, mlp_w1[i], mlp_w2[i])
        if ctx_live:
            ctx = ctx + mod_c[:, 2] * y_c
            m_c = modulate(rmsnorm(ctx, norm2_g[i]), mod_c[:, 3], mod_c[:, 4])
            ctx = ctx + mod_c[:, 5] * sq_relu_mlp(m_c, mlp_w1[i], mlp_w2[i])
    return rmsnorm(x, final_g)


_first_inputs = second_inputs


def second_inputs(seed=0):
    import zlib

    import numpy as np

    out = dict(_first_inputs(seed))
    spreads = {}
    factors = {'norm1_g': 8.0,
     'norm2_g': 6.41,
     'na_rpb': 8.0,
     'cv_b1': 64.0,
     'cv_dwb': 64.0,
     'cv_ln_g': 64.0,
     'cv_ln_b': 64.0,
     'cv_b2': 64.0,
     'final_g': 33.872}
    for name, (base, spread) in spreads.items():
        noise = np.random.default_rng([zlib.crc32(name.encode()), seed]).standard_normal(out[name].shape)
        drawn = base * np.exp(spread * noise) if base else spread * noise
        out[name] = __import__('jax').numpy.asarray(drawn.astype(out[name].dtype))
    for name, factor in factors.items():
        out[name] = (out[name] * factor).astype(out[name].dtype)
    return out


_narrow_inputs = second_inputs


def second_inputs(seed=0):

    out = dict(_narrow_inputs(seed))
    wider = {'cv_ln_g': 5.96, 'cv_ln_b': 5.72, 'cv_b2': 4.32, 'final_g': 6.67}
    for name, times in wider.items():
        mean = out[name].mean()
        out[name] = (mean + times * (out[name] - mean)).astype(out[name].dtype)
    return out


def setup_inputs(seed=0):
    out = dict(first_inputs(seed))
    for name, value in second_inputs(seed + 1).items():
        if name != "x":
            out[name + "_2"] = value
    return out


def reference(
    x, positions, attn_norm, attn_w_in, attn_w_out, mlstm_norm, mlstm_w_in, mlstm_conv_w,
    mlstm_conv_b, mlstm_ig_bias, mlstm_fg_bias, mlstm_head_gain, mlstm_w_out, ffn_norm,
    ffn_w_in, ffn_w_out, final_norm, c_2, ctx_2, c_ctx_2, mod_w_2, mod_b_2, norm1_g_2,
    norm2_g_2, mlp_w1_2, mlp_w2_2, na_wqkv_2, na_wo_2, na_rpb_2, cv_w1_2, cv_b1_2, cv_dw_2,
    cv_dwb_2, cv_ln_g_2, cv_ln_b_2, cv_w2_2, cv_b2_2, sc_win_2, sc_conv_2, sc_wout_2, final_g_2,
):
    x = first_block(
        x, positions, attn_norm, attn_w_in, attn_w_out, mlstm_norm, mlstm_w_in, mlstm_conv_w,
        mlstm_conv_b, mlstm_ig_bias, mlstm_fg_bias, mlstm_head_gain, mlstm_w_out, ffn_norm,
        ffn_w_in, ffn_w_out, final_norm,
    )
    return second_block(
        x, c_2, ctx_2, c_ctx_2, mod_w_2, mod_b_2, norm1_g_2, norm2_g_2, mlp_w1_2, mlp_w2_2,
        na_wqkv_2, na_wo_2, na_rpb_2, cv_w1_2, cv_b1_2, cv_dw_2, cv_dwb_2, cv_ln_g_2, cv_ln_b_2,
        cv_w2_2, cv_b2_2, sc_win_2, sc_conv_2, sc_wout_2, final_g_2,
    )


_drawn_inputs = setup_inputs


def setup_inputs(seed=0):
    import zlib

    import numpy as np

    out = dict(_drawn_inputs(seed))
    spreads = {}
    factors = {'mlstm_ig_bias': 64.0}
    for name, (base, spread) in spreads.items():
        noise = np.random.default_rng([zlib.crc32(name.encode()), seed]).standard_normal(out[name].shape)
        drawn = base * np.exp(spread * noise) if base else spread * noise
        out[name] = jnp.asarray(drawn.astype(out[name].dtype))
    for name, factor in factors.items():
        out[name] = (out[name] * factor).astype(out[name].dtype)
    return out
```

```python
from contextlib import ExitStack

import numpy as np

import concourse.bass as bass
from concourse import mybir

F32 = mybir.dt.float32
F32R = mybir.dt.float32r
I32 = mybir.dt.int32
ALU = mybir.AluOpType
ACT = mybir.ActivationFunctionType
AX = mybir.AxisListType

P = 128
D = 1024
KT = 8
S = 256
DFF = 2816
DFF2 = 4096
NEG = -1.0e30
ROPE_FREQ = [1.0, 0.44036659598350525, 0.1939227432012558, 0.08539710193872452, 0.03760603070259094,
             0.016560440883040428, 0.007292664609849453, 0.0032114461064338684, 0.0014142135623842478,
             0.0006227724370546639, 0.00027424816832155466, 0.00012076973507646471, 5.3182957344688475e-05,
             2.34199997066753e-05, 1.0313385246263351e-05, 4.541670477919979e-06]
TWO_PI_A = 6.28125
TWO_PI_B = 1.9340515136718750e-03
TWO_PI_C = float(2.0 * np.pi - 6.28125 - 1.9340515136718750e-03)
ROUND = 12582912.0

ROWS = [("attn_norm", 1), ("mlstm_norm", 1), ("mlstm_head_gain", 1), ("ffn_norm", 2), ("final_norm", 1),
        ("mlstm_conv_w", 4), ("mlstm_conv_b", 1), ("norm1_g_2", 4), ("norm2_g_2", 4), ("cv_b1_2", 2),
        ("cv_dw_2", 31), ("cv_dwb_2", 1), ("cv_ln_g_2", 1), ("cv_ln_b_2", 1), ("cv_b2_2", 1),
        ("sc_conv_2", 3), ("final_g_2", 1), ("mod_b_2", 24), ("c_2", 1), ("c_ctx_2", 1)]
ROW = {}
NROW = 0
for _n, _k in ROWS:
    ROW[_n] = NROW
    NROW += _k


def const_layout():
    at, out = 0, {}
    for name, width in (("ident", 128), ("flip", 128), ("ones", 128), ("amask", 1152), ("nmask", 64),
                        ("mmask", 384), ("rot", 32), ("freq", 1)):
        out[name] = (at, width)
        at += width
    return out, at


def constants():
    lay, width = const_layout()
    c = np.zeros((P, width), np.float32)

    def put(name, a):
        a = np.asarray(a, np.float32)
        at = lay[name][0]
        c[:a.shape[0], at:at + a.shape[1]] = a

    put("ident", np.eye(P))
    put("flip", np.eye(P)[::-1])
    put("ones", np.ones((P, P)))
    t = np.arange(S)
    masks = []
    for r, window in ((1, 128), (4, 128), (16, 128)):
        dist = t[:, None] - t[None, :]
        ok = (dist >= 0) & (dist % r == 0) & (dist // r <= window)
        masks.append(np.where(ok, 0.0, NEG))
    put("amask", np.concatenate([m[128:, :] for m in masks] + [m[:128, :128] for m in masks], axis=1))
    col = np.arange(64)
    start = np.clip(col - 8, 0, 48)
    ok = (col[None, :] >= start[:, None]) & (col[None, :] < start[:, None] + 16)
    nm = np.where(ok, 0.0, NEG)
    put("nmask", np.concatenate([nm, nm])[::-1])
    keep = t[:, None] <= t[None, :]
    mm = np.where(keep, 0.0, NEG)
    put("mmask", np.concatenate([mm[:128, :], mm[128:, 128:]], axis=1))
    rot = np.zeros((32, 32))
    for i in range(16):
        rot[16 + i, i] = -1.0
        rot[i, 16 + i] = 1.0
    put("rot", rot)
    put("freq", np.array(ROPE_FREQ + ROPE_FREQ, np.float32)[:, None])
    return c


class Step:

    def matmul(self, *a, **k):
        self.op = lambda e: e.matmul(*a, **k)

    def transpose(self, *a, **k):
        self.op = lambda e: e.transpose(*a, **k)

    def activation(self, *a, **k):
        self.op = lambda e: e.activation(*a, **k)

    def tensor_copy(self, *a, **k):
        self.op = lambda e: e.tensor_copy(*a, **k)

    def tensor_tensor(self, *a, **k):
        self.op = lambda e: e.tensor_tensor(*a, **k)

    def tensor_scalar(self, *a, **k):
        self.op = lambda e: e.tensor_scalar(*a, **k)

    def scalar_tensor_tensor(self, *a, **k):
        self.op = lambda e: e.scalar_tensor_tensor(*a, **k)

    def tensor_reduce(self, *a, **k):
        self.op = lambda e: e.tensor_reduce(*a, **k)

    def tensor_tensor_scan(self, *a, **k):
        self.op = lambda e: e.tensor_tensor_scan(*a, **k)

    def reciprocal(self, *a, **k):
        self.op = lambda e: e.reciprocal(*a, **k)

    def memset(self, *a, **k):
        self.op = lambda e: e.memset(*a, **k)


def step(fn):
    s = Step()
    fn(s)
    return s.op


class Queue:

    def __init__(self, sem, step=1):
        self.sem, self.n, self.ops, self.seen = sem, 0, [], {}

    def wait(self, deps):
        for d in flat(deps):
            sem, v = d
            if self.seen.get(sem.name, 0) < v:
                self.seen[sem.name] = v
                self.ops.append(lambda e, sem=sem, v=v: e.wait_ge(sem, v))

    def go(self, fn, *deps):
        self.wait(deps)
        self.ops.append(step(fn))

    def do(self, fn, *deps):
        self.wait(deps)
        self.n += 1
        sem, op = self.sem, step(fn)
        self.ops.append(lambda e: op(e).then_inc(sem, 1))
        return (sem, self.n)

    def dma(self, out, in_, sem, *deps):
        self.wait(deps)
        self.ops.append(lambda e: e.dma_start(out, in_).then_inc(sem, 16))


def flat(deps):
    for d in deps:
        if d is None:
            continue
        if isinstance(d, tuple) and len(d) == 2 and isinstance(d[1], int):
            yield d
        else:
            yield from flat(d)


class Memory:
    pass


RAW = 3
HL = 2
NBANK = 6


def allocate(nc, ctx):
    m = Memory()
    lay, width = const_layout()

    def sb(name, shape, dt=F32, stack=ctx):
        return stack.enter_context(nc.sbuf_tensor(name, shape, dt))

    m.cst = sb("cst", [P, width])
    m.PV = sb("PV", [P, KT, NROW])
    m.eps = sb("eps", [P, 1])
    m.rope = sb("rope", [32, 2, S])
    m.sc = sb("sc", [P, KT, 2])
    m.s4 = sb("s4", [P, KT, 4], F32R)
    m.mod = sb("mod", [P, 4, 48, 2])
    m.gs = sb("gs", [P, 4, 2, KT, 2])
    m.macc = sb("macc", [4, 2, 256])
    m.gb = sb("gb", [8, 2])
    m.stat = sb("stat", [P, 64])
    m.X = sb("X", [P, KT, 512])
    m.raw = [sb(f"raw{i}", [P, 2048]) for i in range(RAW)]
    m.hi = [sb(f"hi{i}", [P, 2048], F32R) for i in range(HL)]
    m.lo = [sb(f"lo{i}", [P, 2048], F32R) for i in range(HL)]
    m.XN = sb("XN", [P, 2, KT, 512], F32R)
    m.SQ = sb("SQ", [P, 2, 512])
    m.RS = sb("RS", [P, 512])
    m.TN = sb("TN", [P, 3, 512])

    def phase(*tensors):
        with ExitStack() as st:
            return [sb(n, s, d, st) for n, s, d in tensors]

    m.rows, m.xin, m.cin, m.pos, m.ang = phase(
        ("rows", [P, D], F32), ("xin", [P, 2, D], F32), ("cin", [P, 2, D], F32),
        ("pos", [32, S], I32), ("ang", [32, 4, S], F32))
    m.QK, m.V1, m.PB, m.PT1, m.RT = phase(
        ("QK", [P, 3, 2, 4, S], F32), ("V1", [P, 2, 3, 512], F32), ("PB", [P, 2, 1152], F32),
        ("PT1", [P, 2, 3, 384], F32), ("RT", [32, 2, 512], F32))
    m.HF, m.SG = phase(("HF", [P, 2, 22, S], F32R), ("SG", [P, 2, 2, S], F32))
    m.CB, m.QKM, m.VM, m.SO, m.HS, m.WT, m.G8, m.AC, m.T3 = phase(
        ("CB", [P, KT, 260], F32), ("QKM", [P, KT, S], F32), ("VM", [P, 2, D], F32), ("SO", [P, KT, S], F32),
        ("HS", [P, KT, S], F32), ("WT", [P, 2, 384 + S], F32), ("G8", [8, 8, S], F32),
        ("AC", [P, 2, 8], F32), ("T3", [P, 2, 3, S], F32))
    m.QB, m.KB, m.VB, m.TB, m.PB2, m.PT2 = phase(
        ("QB", [P, KT, 512], F32), ("KB", [P, KT, 512], F32), ("VB", [P, 4, D], F32),
        ("TB", [P, 2, 2, 2, S], F32), ("PB2", [P, 3, 512], F32), ("PT2", [P, 2, 4, S], F32))
    m.H2, m.RL = phase(("H2", [P, 2, 2, KT, 512], F32R), ("RL", [P, 4, 512], F32))
    m.U, m.CV, m.AB, m.SGM = phase(
        ("U", [P, KT, 2, 286], F32), ("CV", [P, KT, 512], F32), ("AB", [P, 2, 2, 512], F32),
        ("SGM", [P, 2, 512], F32))
    m.YH, m.CG, m.UP, m.CO = phase(
        ("YH", [P, 2, KT, 512], F32R), ("CG", [P, 2, 2, 512], F32), ("UP", [P, 2, 2, 2, 258], F32), ("CO", [P, 2, 2, 512], F32))
    m.FO, = phase(("FO", [P, 2, D], F32))

    m.ps = [ctx.enter_context(nc.psum_tensor(f"ps{i}", [P, 512], F32)) for i in range(8)]
    m.sem = {n: ctx.enter_context(nc.semaphore(f"s_{n}"))
             for n in ["pe", "act", "dve", "pool", "ld", "x", "ci", "pos", "gb", "tb0", "tb1", "out"]
             + [f"raw{i}" for i in range(RAW)]}
    m.lay = lay
    return m


def program(m, T, units):
    pe, act, dve, pool = (Queue(m.sem[n]) for n in ("pe", "act", "dve", "pool"))
    sp = Queue(None)
    ps = m.ps
    bank_free = [None] * 8
    state = {"bank": 0, "unit": 0, "split": 0, "tn": 0}
    order = []
    raw_free = [None] * RAW
    raw_count = [0] * RAW
    hl_free = [None] * HL
    hl_ready = {}
    pend = []

    def cst(name, rows=P):
        at, w = m.lay[name]
        return m.cst[0:rows, at:at + w]

    ident, ones = cst("ident"), cst("ones")

    def pv(name, k, i=0):
        r = ROW[name] + i
        return m.PV[:, k, r:r + 1]

    def bank():
        b = state["bank"]
        state["bank"] = (b + 1) % NBANK
        pe.wait([bank_free[b]])
        return b, ps[b]

    def split(j):
        src, kt, cols = units[j]
        r, h = j % RAW, j % HL
        n = kt * cols
        raw_count[r] += 16
        sp.dma(m.raw[r][:, 0:n].rearrange("p (k n) -> p k n", k=kt), src, m.sem[f"raw{r}"], raw_free[r])
        landed = (m.sem[f"raw{r}"], raw_count[r])
        raw, hi, lo = m.raw[r], m.hi[h], m.lo[h]
        a = act.do(lambda e: e.activation(hi[:, 0:n], raw[:, 0:n], ACT.Copy), landed, hl_free[h])
        d = dve.do(lambda e: e.tensor_tensor(lo[:, 0:n], raw[:, 0:n], hi[:, 0:n].bitcast(F32), ALU.subtract),
                   landed, a, hl_free[h])
        raw_free[r] = [a, d]
        hl_ready[j] = d

    def take(src, kt, cols):
        j = state["unit"]
        state["unit"] += 1
        order.append((src, kt, cols))
        h = j % HL
        if units is None:
            return j, m.hi[h][:, 0:kt * cols].rearrange("p (k n) -> p k n", k=kt), \
                m.lo[h][:, 0:kt * cols].rearrange("p (k n) -> p k n", k=kt)
        assert units[j][1:] == (kt, cols)
        while state["split"] <= min(j + 1, len(units) - 1):
            split(state["split"])
            state["split"] += 1
        pe.wait([hl_ready[j]])
        return j, m.hi[h][:, 0:kt * cols].rearrange("p (k n) -> p k n", k=kt), \
            m.lo[h][:, 0:kt * cols].rearrange("p (k n) -> p k n", k=kt)

    def used(j, tok):
        hl_free[j % HL] = tok

    def flush():
        todo = list(pend)
        pend.clear()
        for f in todo:
            f()

    def weight(w, k0, kt, c0, cols):
        return w[k0:k0 + kt * P, c0:c0 + cols].rearrange("(k p) n -> p k n", p=P)

    def mm3(out, whi, wlo, xhi, xlo, first, last, signal=False):
        pairs = [(whi, xhi), (whi, xlo), (wlo, xhi)]
        tok = None
        for i, (a, b) in enumerate(pairs):
            f = (lambda e, a=a, b=b, i=i: e.matmul(out, a, b, start=first and i == 0, stop=last and i == 2))
            if (last or signal) and i == 2:
                tok = pe.do(f)
            else:
                pe.go(f)
        return tok

    def linear(w, k0, kt, c0, cols, xhi, xlo, xtok, evac):
        j, hi, lo = take(weight(w, k0, kt, c0, cols), kt, cols)
        for t in range(cols // P):
            b, acc = bank()
            n = xhi(0).shape[-1]
            acc = acc[:, 0:n]
            for k in range(kt):
                pe.wait([xtok[k]])
                tok = mm3(acc, hi[:, k, t * P:(t + 1) * P], lo[:, k, t * P:(t + 1) * P], xhi(k), xlo(k),
                          k == 0, k == kt - 1)
            used(j, tok)
            if t == 0:
                flush()
            bank_free[b] = evac(t, acc, tok)

    def linear_tok(w, c0, cols, ntt, xtok, evac):
        j, hi, lo = take(weight(w, 0, KT, c0, cols), KT, cols)
        for t in range(ntt):
            b, acc = bank()
            acc = acc[:, 0:cols]
            for k in range(KT):
                pe.wait([xtok[k]])
                tok = mm3(acc, m.XN[:, 0, k, t * P:(t + 1) * P], m.XN[:, 1, k, t * P:(t + 1) * P],
                          hi[:, k, :], lo[:, k, :], k == 0, k == KT - 1)
            used(j, tok)
            if t == 0:
                flush()
            bank_free[b] = evac(t, acc, tok)

    def xn(lo, hi):
        return (lambda k: m.XN[:, 0, k, lo:hi]), (lambda k: m.XN[:, 1, k, lo:hi])

    sq_free = [None, None]
    stat = {"tok": None}

    def sumsq(src, i, count, n, tok, square=True):
        buf = i % 2
        if square:
            a = act.do(lambda e: e.activation(m.SQ[:, buf, 0:n], src, ACT.Square), tok, sq_free[buf])
            rhs = m.SQ[:, buf, 0:n]
        else:
            a, rhs = tok, src

        def later():
            f = (lambda e: e.matmul(ps[6][:, 0:n], ones, rhs, start=i == 0, stop=i == count - 1))
            t = pe.do(f, a, bank_free[6] if i == 0 else None)
            if square:
                sq_free[buf] = t
            stat["tok"] = t

        pend.append(later)

    def rstd(n, count, out):
        t = act.do(lambda e: e.activation(out, ps[6][:, 0:n], ACT.Ln, bias=m.eps[:, 0:1], scale=1.0 / count),
                   stat["tok"], eps_tok, rs_free[0])
        bank_free[6] = t
        return act.do(lambda e: e.activation(out, out, ACT.Exp, scale=-0.5), t)

    rs_free = [None]
    tn_free = [None] * 3

    def halves(dst_hi, dst_lo, src, tok, free=None):
        a = act.do(lambda e: e.activation(dst_hi, src, ACT.Copy), tok, free)
        d = dve.do(lambda e: e.tensor_tensor(dst_lo, src, dst_hi.bitcast(F32), ALU.subtract), a, tok, free)
        return d

    def norm(n, gain, shift=None):
        flush()
        free = (m.sem["pe"], pe.n)
        r = rstd(n, D, m.RS[:, 0:n])
        toks = []
        streams = [(0, n)] if shift is None else [(s * S, (s + 1) * S) for s in range(n // S)]
        for k in range(KT):
            buf = state["tn"] % 3
            state["tn"] += 1
            got = []
            for s, (a, b) in enumerate(streams):
                t = dve.do(lambda e, a=a, b=b, s=s: e.scalar_tensor_tensor(
                    out=m.TN[:, buf, a:b], in0=m.X[:, k, a:b], scalar=gain(k, s), in1=m.RS[:, a:b],
                    op0=ALU.mult, op1=ALU.mult), r, tn_free[buf])
                hi, lo, tn = m.XN[:, 0, k, a:b], m.XN[:, 1, k, a:b], m.TN[:, buf, a:b]
                if shift is None:
                    got.append(halves(hi, lo, tn, t, free))
                    continue
                h = act.do(lambda e, hi=hi, tn=tn, s=s: e.activation(hi, tn, ACT.Identity, bias=shift(k, s)),
                           t, free)
                got.append(dve.do(lambda e, hi=hi, lo=lo, tn=tn, s=s: e.scalar_tensor_tensor(
                    out=lo, in0=tn, scalar=shift(k, s), in1=hi.bitcast(F32), op0=ALU.add, op1=ALU.subtract),
                    t, h, free))
            tn_free[buf] = got
            toks.append(got)
        rs_free[0] = toks[-1]
        return toks

    def residual(j, n, gate, acc, tok, last):
        if gate is None:
            t = dve.do(lambda e: e.tensor_tensor(m.X[:, j, 0:n], acc, m.X[:, j, 0:n], ALU.add), tok)
        else:
            for s in range(n // S):
                t = dve.do(lambda e, s=s: e.scalar_tensor_tensor(
                    out=m.X[:, j, s * S:(s + 1) * S], in0=acc[:, s * S:(s + 1) * S], scalar=gate(j, s),
                    in1=m.X[:, j, s * S:(s + 1) * S], op0=ALU.mult, op1=ALU.add), tok)
        if last:
            sumsq(m.X[:, j, 0:n], j, KT, n, t)
        return t

    ld = m.sem["ld"]
    nld = [0]

    def load(out, in_, q=sp):
        q.dma(out, in_, ld)
        nld[0] += 16

    load(m.cst[:, :], T["consts"])
    for name, k in ROWS:
        src = T[name]
        r = ROW[name]
        load(m.rows[r:r + k, :], src)
    load(m.gb[:, 0:1], T["mlstm_ig_bias"].rearrange("a h -> h a"))
    load(m.gb[:, 1:2], T["mlstm_fg_bias"].rearrange("a h -> h a"))
    sp.dma(m.xin[:, :, :], T["x"][0].rearrange("(t p) d -> p t d", p=P), m.sem["x"])
    sp.dma(m.cin[:, :, :], T["ctx_2"][0].rearrange("(t p) d -> p t d", p=P), m.sem["ci"])
    sp.dma(m.pos[:, :], T["positions"].broadcast_to([32, S]), m.sem["pos"])
    loaded = (ld, nld[0])
    x_in, c_in = (m.sem["x"], 16), (m.sem["ci"], 16)
    eps_tok = dve.do(lambda e: e.memset(m.eps[:, :], 1e-6))

    pv_tok = None
    for k in range(KT):
        b, acc = bank()
        t = pe.do(lambda e: e.transpose(acc[:, 0:NROW], m.rows[0:NROW, k * P:(k + 1) * P], ident[0:NROW, 0:NROW]),
                  loaded)
        pv_tok = dve.do(lambda e: e.tensor_copy(m.PV[:, k, :], acc[:, 0:NROW]), t)
        bank_free[b] = pv_tok
    for j in range(KT):
        b, acc = bank()
        for s, (src, arrived) in enumerate(((m.xin, x_in), (m.cin, c_in))):
            for t in range(2):
                o = s * S + t * P
                tok = pe.do(lambda e, o=o, src=src, t=t: e.transpose(
                    acc[:, o:o + P], src[:, t, j * P:(j + 1) * P], ident), arrived, loaded)
        t = dve.do(lambda e: e.tensor_copy(m.X[:, j, :], acc[:, :]), tok)
        bank_free[b] = t
        sumsq(m.X[:, j, 0:S], j, KT, S, t)
        if j >= 1:
            pend.pop(0)()
    c0 = ROW["c_2"]
    t = act.do(lambda e: e.activation(m.sc[:, :, :], m.PV[:, :, c0:c0 + 2], ACT.Silu), pv_tok)
    s4_tok = halves(m.s4[:, :, 0:2], m.s4[:, :, 2:4], m.sc[:, :, :], t)
    A = m.ang
    arrived = (m.sem["pos"], 16)
    t = dve.do(lambda e: e.tensor_copy(A[:, 0, :], m.pos[:, :]), arrived)
    t = dve.do(lambda e: e.tensor_scalar(A[:, 1, :], A[:, 0, :], cst("freq", 32), None, ALU.mult), t, loaded)
    t = dve.do(lambda e: e.tensor_scalar(A[:, 2, :], A[:, 1, :], float(1.0 / (2.0 * np.pi)), ROUND,
                                         ALU.mult, ALU.add), t)
    t = dve.do(lambda e: e.tensor_scalar(A[:, 2, :], A[:, 2, :], ROUND, None, ALU.subtract), t)
    for part in (TWO_PI_A, TWO_PI_B, TWO_PI_C):
        t = dve.do(lambda e, part=part: e.scalar_tensor_tensor(
            out=A[:, 1, :], in0=A[:, 2, :], scalar=-part, in1=A[:, 1, :], op0=ALU.mult, op1=ALU.add), t)
    t = dve.do(lambda e: e.tensor_scalar(A[:, 1, :], A[:, 1, :], 3.1415925, -3.1415925, ALU.min, ALU.max), t)
    t = dve.do(lambda e: e.scalar_tensor_tensor(out=A[:, 3, :], in0=A[:, 1, :], scalar=-1.0, in1=A[:, 1, :],
                                                op0=ALU.mult, op1=ALU.max), t)
    t = dve.do(lambda e: e.tensor_scalar(A[:, 3, :], A[:, 3, :], -1.0, float(np.pi / 2), ALU.mult, ALU.add), t)
    act.do(lambda e: e.activation(m.rope[:, 0, :], A[:, 3, :], ACT.Sin), t)
    rope_tok = act.do(lambda e: e.activation(m.rope[:, 1, :], A[:, 1, :], ACT.Sin), t)
    flush()

    mod_next = [0]
    mod_free = [None, None]
    mod_tok = [None] * 4
    gs_tok = [None] * 4

    def mod_unit():
        n = mod_next[0]
        if n >= 96:
            return
        mod_next[0] += 1
        layer, c = n // 24, n % 24
        j, hi, lo = take(weight(T["mod_w_2"][layer], 0, KT, c * 256, 256), KT, 256)
        b, acc = bank()
        pe.wait([s4_tok])
        def both(k, **flags):
            return lambda e: e.matmul(acc[0:4, 0:256], m.s4[:, k, 0:4], hi[:, k, :], skip_group_check=True, **flags)

        pe.go(both(0, start=True, stop=False))
        for k in range(KT):
            pe.go(lambda e, k=k: e.matmul(acc[0:2, 0:256], m.s4[:, k, 0:2], lo[:, k, :], start=False, stop=False,
                                          skip_group_check=True))
        for k in range(1, KT - 1):
            pe.go(both(k, start=False, stop=False))
        tok = pe.do(both(KT - 1, start=False, stop=True))
        used(j, tok)
        buf = n % 2
        t = act.do(lambda e: e.activation(m.macc[:, buf, :], acc[0:4, 0:256], ACT.Copy), tok, mod_free[buf])
        bank_free[b] = t

        def later():
            for i in range(2):
                o = (2 * c + i) * 4
                q = pe.do(lambda e, i=i, o=o: e.transpose(ps[7][:, o:o + 4], m.macc[:, buf, i * P:(i + 1) * P],
                                                          ident[0:4, 0:4]),
                          t, loaded, bank_free[7] if c == 0 else None)
            mod_free[buf] = q
            if c == 23:
                finish(layer, q)

        pend.append(later)

    def finish(layer, tok):
        mod = m.mod[:, layer, :, :]
        t = dve.do(lambda e: e.tensor_reduce(mod, ps[7][:, 0:192].rearrange("p (i h s) -> p i s h", h=2, s=2),
                                             AX.X, ALU.add), tok)
        bank_free[7] = t
        r = ROW["mod_b_2"] + 6 * layer
        biased = []
        for i in range(6):
            bias = m.PV[:, :, r + i:r + i + 1].broadcast_to([P, KT, 2])
            biased.append(dve.do(lambda e, i=i, bias=bias: e.tensor_tensor(
                m.mod[:, layer, i * KT:(i + 1) * KT, :], m.mod[:, layer, i * KT:(i + 1) * KT, :], bias, ALU.add),
                t, pv_tok))
        for w, name in ((0, "norm1_g_2"), (1, "norm2_g_2")):
            i = 1 + 3 * w
            r = ROW[name] + layer
            gain = m.PV[:, :, r:r + 1].broadcast_to([P, KT, 2])
            t = dve.do(lambda e, w=w, i=i, gain=gain: e.scalar_tensor_tensor(
                out=m.gs[:, layer, w, :, :], in0=m.mod[:, layer, i * KT:(i + 1) * KT, :], scalar=1.0, in1=gain,
                op0=ALU.add, op1=ALU.mult), biased)
        mod_tok[layer] = t

    def modcol(layer, i):
        return lambda k, s: m.mod[:, layer, i * KT + k, s:s + 1]

    xt = norm(S, lambda k, s: pv("attn_norm", k))
    xhi, xlo = xn(0, S)
    w = T["attn_w_in"][0]
    scale = float(P) ** -0.5
    pb_free = [None, None]
    pt_free = [None, None]
    rt_free = [None, None]
    qk_free = None
    amask = cst("amask")
    nrt = [0]
    otoks = [None] * KT
    for half in range(2):
        qk_tok, v_tok = [], []
        for g in range(3):
            for which in range(2):
                for pair in range(2):
                    h0 = half * 4 + pair * 2
                    col = ((g * 3 + which) * 8 + h0) * P
                    dst = m.QK[:, g, which, pair * 2:pair * 2 + 2, :]
                    got = []

                    def evac(t, acc, tok):
                        r = act.do(lambda e: e.activation(dst[:, t, :], acc, ACT.Copy), tok, qk_free)
                        got.append(r)
                        return r

                    linear(w, 0, KT, col, 256, xhi, xlo, xt, evac)

                    def rotate(dst=dst, got=got):
                        b, acc = bank()
                        buf = nrt[0] % 2
                        nrt[0] += 1
                        tok = pe.do(lambda e: e.matmul(acc[0:32, :], cst("rot", 32), dst[0:32, :, :],
                                                       start=True, stop=True), got, loaded)
                        cos = m.rope[:, 0, :].unsqueeze(1).broadcast_to([32, 2, S])
                        sin = m.rope[:, 1, :].unsqueeze(1).broadcast_to([32, 2, S])
                        rt = m.RT[:, buf, :].rearrange("p (h t) -> p h t", h=2)
                        t1 = dve.do(lambda e: e.tensor_tensor(
                            rt, acc[0:32, :].rearrange("p (h t) -> p h t", h=2), sin, ALU.mult), tok, rope_tok)
                        bank_free[b] = t1
                        t2 = dve.do(lambda e: e.tensor_tensor(dst[0:32, :, :], dst[0:32, :, :], cos, ALU.mult),
                                    tok, got)
                        qk_tok.append(dve.do(lambda e: e.tensor_tensor(dst[0:32, :, :], dst[0:32, :, :], rt,
                                                                       ALU.add), t1, t2))

                    pend.append(rotate)
                mod_unit()
            for pair in range(2):
                col = ((g * 3 + 2) * 8 + half * 4 + pair * 2) * P

                def evac(t, acc, tok):
                    r = act.do(lambda e: e.activation(m.V1[:, t, g, pair * 256:pair * 256 + 256], acc, ACT.Copy),
                               tok, qk_free)
                    v_tok.append(r)
                    return r

                linear_tok(w, col, 256, 2, xt, evac)
        flush()
        ready = {}

        def scores(h):
            hh = h % 4
            buf = h % 2
            q = [m.QK[:, g, 0, hh, :] for g in range(3)]
            k = [m.QK[:, g, 1, hh, :] for g in range(3)]
            parts = [[(q[0][:, P:S], k[0], 0, 256), (q[1][:, P:S], k[1], 256, 256)],
                     [(q[2][:, P:S], k[2], 0, 256)],
                     [(q[g][:, 0:P], k[g][:, 0:P], g * P, P) for g in range(3)]]
            at = 0
            toks = []
            for part in parts:
                b, acc = bank()
                for i, (a, c, o, n) in enumerate(part):
                    tok = pe.do(lambda e, a=a, c=c, o=o, n=n, i=i: e.matmul(
                        acc[:, o:o + n], a, c, start=True, stop=True),
                        qk_tok)
                width = o + n
                t = dve.do(lambda e, at=at, width=width: e.tensor_tensor(
                    m.PB[:, buf, at:at + width], acc[:, 0:width], amask[:, at:at + width], ALU.add),
                    tok, pb_free[buf])
                bank_free[b] = t
                toks.append(t)
                at += width
            st = m.stat[:, buf * 8:buf * 8 + 8]
            rngs = ((0, 768), (768, 1152))
            t = [dve.do(lambda e, i=i, r=r: e.tensor_reduce(st[:, i:i + 1], m.PB[:, buf, r[0]:r[1]], AX.X, ALU.max),
                        toks, pb_free[buf]) for i, r in enumerate(rngs)]
            t = dve.do(lambda e: e.tensor_scalar(st[:, 2:4], st[:, 0:2], -scale, None, ALU.mult), t)
            ex = [act.do(lambda e, i=i, r=r: e.activation(
                m.PB[:, buf, r[0]:r[1]], m.PB[:, buf, r[0]:r[1]], ACT.Exp, bias=st[:, 2 + i:3 + i], scale=scale,
                accum_out=st[:, 4 + i:5 + i]), t) for i, r in enumerate(rngs)]
            t = dve.do(lambda e: e.reciprocal(st[:, 6:8], st[:, 4:6]), ex)
            ready[h] = [dve.do(lambda e, i=i, r=r: e.tensor_scalar(
                m.PB[:, buf, r[0]:r[1]], m.PB[:, buf, r[0]:r[1]], st[:, 6 + i:7 + i], None, ALU.mult), t)
                for i, r in enumerate(rngs)]

        def values(h):
            hh = h % 4
            buf = h % 2
            got = []
            for g in range(3):
                b, acc = bank()
                for o, at in ((0, 768 + g * P), (P, g * 256), (2 * P, g * 256 + P)):
                    tok = pe.do(lambda e, o=o, at=at: e.transpose(acc[:, o:o + P], m.PB[:, buf, at:at + P], ident),
                                ready[h])
                q = act if g == 0 else dve
                if q is act:
                    t = act.do(lambda e: e.activation(m.PT1[:, buf, g, :], acc[:, 0:384], ACT.Copy), tok, pt_free[buf])
                else:
                    t = dve.do(lambda e: e.tensor_copy(m.PT1[:, buf, g, :], acc[:, 0:384]), tok, pt_free[buf])
                bank_free[b] = t
                got.append(t)
            pb_free[buf] = tok

            def finish_head():
                b, acc = bank()
                plan = [(0, 0), (0, 1), (1, 1), (2, 1), (1, 0), (2, 0)]
                for i, (g, kt) in enumerate(plan):
                    out = acc[:, 0:S] if kt == 0 else acc[:, P:S]
                    prob = m.PT1[:, buf, g, 0:256] if kt == 0 else m.PT1[:, buf, g, 256:384]
                    tok = pe.do(lambda e: e.matmul(out, m.V1[:, kt, g, hh * P:(hh + 1) * P], prob, start=i == 0,
                                                   stop=i == len(plan) - 1, skip_group_check=True), got, v_tok)
                pt_free[buf] = tok
                otoks[h] = halves(m.XN[:, 0, h, S:512], m.XN[:, 1, h, S:512], acc[:, 0:S], tok)
                bank_free[b] = otoks[h]
                return tok

            return finish_head

        heads = [half * 4 + i for i in range(4)]
        scores(heads[0])
        for i, h in enumerate(heads):
            if i + 1 < 4:
                scores(heads[i + 1])
            f = values(h)
            mod_unit()
            flush()
            qk_free = f()

    def grow(width, xh, xl, xtok, n, gate, wsrc, kts=KT):
        for c in range(4):
            def evac(t, acc, tok):
                return residual(c * 2 + t, n, gate, acc, tok, True)
            linear(wsrc, 0, KT, c * 256, 256, xh, xl, xtok, evac)

    mh, ml = xn(S, 512)
    grow(S, mh, ml, otoks, S, None, T["attn_w_out"][0])

    def swiglu(layer):
        xt = norm(S, lambda k, s: pv("ffn_norm", k, layer))
        xhi, xlo = xn(0, S)
        w = T["ffn_w_in"][layer]
        wo = T["ffn_w_out"][layer]
        htok = [None] * 22
        sg_free = [None] * 2
        sg_tok = {}
        for j in range(11):
            def evac_g(t, acc, tok):
                r = act.do(lambda e: e.activation(m.SG[:, j % 2, t, :], acc, ACT.Silu), tok, sg_free[j % 2])
                sg_tok[t] = r
                return r

            def evac_u(t, acc, tok):
                buf = j % 2
                r = dve.do(lambda e: e.tensor_tensor(m.SG[:, buf, t, :], acc, m.SG[:, buf, t, :], ALU.mult),
                           tok, sg_tok[t])
                i = 2 * j + t
                htok[i] = halves(m.HF[:, 0, i, :], m.HF[:, 1, i, :], m.SG[:, buf, t, :], r)
                if t == 1:
                    sg_free[buf] = [htok[i - 1], htok[i]]
                return r

            linear(w, 0, KT, j * 256, 256, xhi, xlo, xt, evac_g)
            linear(w, 0, KT, DFF + j * 256, 256, xhi, xlo, xt, evac_u)
            mod_unit()
        for c in range(4):
            banks = [bank(), bank()]
            for part, (k0, kt) in enumerate(((0, 8), (8, 8), (16, 6))):
                j, hi, lo = take(weight(wo, k0 * P, kt, c * 256, 256), kt, 256)
                for t in range(2):
                    acc = banks[t][1][:, 0:S]
                    for k in range(kt):
                        kk = k0 + k
                        pe.wait([htok[kk]])
                        tok = mm3(acc, hi[:, k, t * P:(t + 1) * P], lo[:, k, t * P:(t + 1) * P],
                                  m.HF[:, 0, kk, :], m.HF[:, 1, kk, :], kk == 0, kk == 21, k == kt - 1)
                    if kk == 21:
                        if t == 0:
                            flush()
                        bank_free[banks[t][0]] = residual(c * 2 + t, S, None, acc, tok, True)
                used(j, tok)
            mod_unit()

    swiglu(0)

    xt = norm(S, lambda k, s: pv("mlstm_norm", k))
    xhi, xlo = xn(0, S)
    w = T["mlstm_w_in"][0]
    pads = pool.do(lambda e: e.memset(m.CB[:, :, 0:3], 0.0), xt[0])
    one8 = pool.do(lambda e: e.memset(m.G8[:, 7, :], 1.0), xt[0])
    j, hi, lo = take(weight(w, 0, KT, 3072, 16), KT, 16)
    gbanks = []
    for i in range(2):
        b, acc = bank()
        for k in range(KT):
            pe.wait([xt[k]])
            tok = mm3(acc[0:8, 0:S], hi[:, k, i * 8:i * 8 + 8], lo[:, k, i * 8:i * 8 + 8], xhi(k), xlo(k),
                      k == 0, k == KT - 1)
        gbanks.append((b, acc, tok))
    used(j, tok)
    G = m.G8
    z = dve.do(lambda e: e.tensor_scalar(G[:, 0, :], gbanks[1][1][0:8, 0:S], m.gb[:, 1:2], None, ALU.add),
               gbanks[1][2], loaded, xt[KT - 1])
    bank_free[gbanks[1][0]] = z
    az = dve.do(lambda e: e.scalar_tensor_tensor(out=G[:, 1, :], in0=G[:, 0, :], scalar=-1.0,
                                                 in1=G[:, 0, :], op0=ALU.mult, op1=ALU.max), z)
    t = act.do(lambda e: e.activation(G[:, 1, :], G[:, 1, :], ACT.Exp, scale=-1.0), az)
    t = act.do(lambda e: e.activation(G[:, 1, :], G[:, 1, :], ACT.Ln, bias=ones[0:8, 0:1]), t)
    t = dve.do(lambda e: e.scalar_tensor_tensor(out=G[:, 0, :], in0=G[:, 0, :], scalar=0.0,
                                                in1=G[:, 1, :], op0=ALU.min, op1=ALU.subtract), t)
    Bt = dve.do(lambda e: e.tensor_tensor_scan(G[:, 2, :], G[:, 7, :], G[:, 0, :], 0.0,
                                               ALU.mult, ALU.add), t, one8)
    At = dve.do(lambda e: e.scalar_tensor_tensor(out=G[:, 3, :], in0=gbanks[0][1][0:8, 0:S],
                                                 scalar=m.gb[:, 0:1], in1=G[:, 2, :],
                                                 op0=ALU.add, op1=ALU.subtract), Bt, gbanks[0][2])
    bank_free[gbanks[0][0]] = At
    Mt = dve.do(lambda e: e.tensor_tensor_scan(G[:, 4, :], G[:, 3, :], G[:, 3, :], 0.0,
                                               ALU.max, ALU.max), At)
    NMt = dve.do(lambda e: e.tensor_scalar(G[:, 5, :], G[:, 4, :], -1.0, None, ALU.mult), Mt)
    EMt = dve.do(lambda e: e.scalar_tensor_tensor(out=G[:, 6, :], in0=G[:, 2, :], scalar=-1.0,
                                                  in1=G[:, 4, :], op0=ALU.mult, op1=ALU.subtract), Mt)

    qk_done = [None] * KT
    v_tok = []
    so_tok = [None] * KT
    for c in range(4):
        got = {}

        def evac(t, acc, tok):
            r = act.do(lambda e: e.activation(m.CB[:, 2 * c + t, 3:3 + S], acc, ACT.Copy), tok)
            got[t] = r
            return r

        linear(w, 0, KT, c * 256, 256, xhi, xlo, xt, evac)
        mod_unit()
        for t in range(2):
            k = 2 * c + t
            r = dve.do(lambda e: e.tensor_scalar(m.QKM[:, k, :], m.CB[:, k, 0:S], pv("mlstm_conv_w", k, 0),
                                                 pv("mlstm_conv_b", k), ALU.mult, ALU.add), got[t], pads)
            for i in range(1, 4):
                r = dve.do(lambda e, i=i: e.scalar_tensor_tensor(
                    out=m.QKM[:, k, :], in0=m.CB[:, k, i:i + S], scalar=pv("mlstm_conv_w", k, i),
                    in1=m.QKM[:, k, :], op0=ALU.mult, op1=ALU.add), r)
            qk_done[k] = act.do(lambda e: e.activation(m.QKM[:, k, :], m.QKM[:, k, :], ACT.Silu), r)
    for c in range(4):
        def evac(t, acc, tok):
            r = act.do(lambda e: e.activation(m.VM[:, t, c * 256:(c + 1) * 256], acc, ACT.Copy), tok)
            v_tok.append(r)
            return r

        linear_tok(w, 1024 + c * 256, 256, 2, xt, evac)
        mod_unit()
    for c in range(4):
        def evac(t, acc, tok):
            r = act.do(lambda e: e.activation(m.SO[:, 2 * c + t, :], acc, ACT.Sigmoid), tok)
            so_tok[2 * c + t] = r
            return r

        linear(w, 0, KT, 2048 + c * 256, 256, xhi, xlo, xt, evac)
        mod_unit()
    flush()
    b, acc = bank()
    for i in range(2):
        tok = pe.do(lambda e, i=i: e.transpose(acc[:, i * 8:i * 8 + 8], G[:, 3, i * P:(i + 1) * P],
                                               ident[0:8, 0:8]), At)
    ac_tok = dve.do(lambda e: e.tensor_copy(m.AC[:, :, :], acc[:, 0:16].rearrange("p (i h) -> p i h", i=2)), tok)
    bank_free[b] = ac_tok
    mmask = cst("mmask")
    wt_free = [None, None]
    t3_free = [None, None]
    mready = {}

    def weights(h):
        buf = h % 2
        WT = m.WT[:, buf, 0:384]
        EM = m.WT[:, buf, 384:384 + S]
        b, acc = bank()
        tok = pe.do(lambda e: e.matmul(acc[:, :], m.cst[0:8, h:h + 1].broadcast_to([8, P]),
                                       G[:, 5:7, :], start=True, stop=True), NMt, EMt, loaded)
        t1 = dve.do(lambda e: e.tensor_tensor(WT[:, 0:S], acc[:, 0:S], mmask[:, 0:S], ALU.add), tok, wt_free[buf])
        t2 = dve.do(lambda e: e.tensor_tensor(WT[:, S:384], acc[:, P:S], mmask[:, S:384], ALU.add), tok, wt_free[buf])
        e1 = act.do(lambda e: e.activation(EM, acc[:, S:512], ACT.Exp), tok, t1, t2, wt_free[buf])
        bank_free[b] = [t1, t2, e1]
        e2 = act.do(lambda e: e.activation(WT[:, 0:S], WT[:, 0:S], ACT.Exp, bias=m.AC[:, 0, h:h + 1]), t1, ac_tok)
        e3 = act.do(lambda e: e.activation(WT[:, S:384], WT[:, S:384], ACT.Exp, bias=m.AC[:, 1, h:h + 1]), t2)
        o = 64 * (h % 2)
        Q = m.QKM[o:o + 64, h // 2, :]
        K = m.QKM[o:o + 64, 4 + h // 2, :]
        b, acc = bank()
        pe.go(lambda e: e.matmul(acc[:, 0:S], K[:, 0:P], Q, start=True, stop=True),
              qk_done[h // 2], qk_done[4 + h // 2])
        tok = pe.do(lambda e: e.matmul(acc[:, S:384], K[:, P:S], Q[:, P:S], start=True, stop=True))
        t = dve.do(lambda e: e.scalar_tensor_tensor(out=WT, in0=acc[:, 0:384], scalar=0.125, in1=WT,
                                                    op0=ALU.mult, op1=ALU.mult), tok, e2, e3)
        bank_free[b] = t
        mready[h] = (t, e1)

    def cell(h):
        buf = h % 2
        WT = m.WT[:, buf, 0:384]
        EM = m.WT[:, buf, 384:384 + S]
        T3 = m.T3[:, buf, :, :]
        t, e1 = mready[h]
        bn, num = bank()
        bd, den = bank()
        V = m.VM[:, :, h * P:(h + 1) * P]
        for dst, l0, l1 in ((num, V[:, 0, :], V[:, 1, :]), (den, ones, ones)):
            pe.go(lambda e: e.matmul(dst[:, 0:P], l0, WT[:, 0:P], start=True, stop=True), t, v_tok)
            pe.go(lambda e: e.matmul(dst[:, P:S], l0, WT[:, P:S], start=True, stop=False))
            tok = pe.do(lambda e: e.matmul(dst[:, P:S], l1, WT[:, S:384], start=False, stop=True))
        a = act.do(lambda e: e.activation(T3[:, 0, :], den[:, 0:S], ACT.Abs), tok, t3_free[buf])
        bank_free[bd] = a
        d = dve.do(lambda e: e.tensor_tensor(T3[:, 0, :], T3[:, 0, :], EM, ALU.max), a, e1)
        wt_free[buf] = [tok, d]
        d = dve.do(lambda e: e.reciprocal(T3[:, 0, :], T3[:, 0, :]), d)
        d = dve.do(lambda e: e.tensor_tensor(m.HS[:, h, :], num[:, 0:S], T3[:, 0, :], ALU.mult), d, tok)
        bank_free[bn] = d
        a = act.do(lambda e: e.activation(T3[:, 1, :], m.HS[:, h, :], ACT.Square), d, t3_free[buf])

        def close():
            b, acc = bank()
            tok = pe.do(lambda e: e.matmul(acc[:, 0:S], ones, T3[:, 1, :], start=True, stop=True), a)
            r = act.do(lambda e: e.activation(T3[:, 2, :], acc[:, 0:S], ACT.Ln, bias=m.eps[:, 0:1],
                                              scale=1.0 / P), tok, eps_tok)
            bank_free[b] = r
            r = act.do(lambda e: e.activation(T3[:, 2, :], T3[:, 2, :], ACT.Exp, scale=-0.5), r)
            r = dve.do(lambda e: e.scalar_tensor_tensor(out=m.HS[:, h, :], in0=m.HS[:, h, :],
                                                        scalar=pv("mlstm_head_gain", h), in1=T3[:, 2, :],
                                                        op0=ALU.mult, op1=ALU.mult), r, d, a)
            t3_free[buf] = [r, tok]
            r = dve.do(lambda e: e.tensor_tensor(m.HS[:, h, :], m.HS[:, h, :], m.SO[:, h, :], ALU.mult),
                       r, so_tok[h])
            otoks[h] = halves(m.XN[:, 0, h, S:512], m.XN[:, 1, h, S:512], m.HS[:, h, :], r)

        return close

    weights(0)
    close = None
    for h in range(8):
        if h + 1 < 8:
            weights(h + 1)
        nxt = cell(h)
        mod_unit()
        flush()
        if close:
            close()
        close = nxt
    close()
    grow(S, mh, ml, otoks, S, None, T["mlstm_w_out"][0])
    swiglu(1)
    while mod_next[0] < 96:
        mod_unit()
        flush()

    flush()
    r = rstd(S, D, m.RS[:, 0:S])
    for k in range(KT):
        t = dve.do(lambda e: e.scalar_tensor_tensor(out=m.X[:, k, 0:S], in0=m.X[:, k, 0:S],
                                                    scalar=pv("final_norm", k), in1=m.RS[:, 0:S],
                                                    op0=ALU.mult, op1=ALU.mult), r)
        sumsq(m.X[:, k, :], k, KT, 512, t)
        if k >= 1:
            pend.pop(0)()
    rs_free[0] = t

    def neighbourhood(layer, slot, ctx_out):
        n = 512 if ctx_out else S
        xt = norm(512, lambda k, s: m.gs[:, layer, 0, k, s:s + 1], modcol(layer, 0))
        w = T["na_wqkv_2"][slot]
        start = xt[KT - 1]
        tbs = [m.sem["tb0"], m.sem["tb1"]]
        tb_tok = [None] * 8
        tb_free = [None, None]
        nmask = cst("nmask").unsqueeze(1).broadcast_to([P, 16, 64])

        def table(q):
            buf = q % 2
            rpb = T["na_rpb_2"]
            count = 0
            for hh in range(2):
                h = q * 2 + hh
                for qb in range(2):
                    for rr in range(2):
                        base = slot * 7440 + h * 465 + (rr + 6 - 2 * qb) * 31 - 48
                        src = bass.AP(tensor=rpb.tensor, offset=base, ap=[[1, 64], [31, 4], [1, 64]])
                        dst = m.TB[rr * 64:rr * 64 + 64, buf, hh, qb, :].rearrange("p (a c) -> p a c", a=4)
                        pool.dma(dst, src, tbs[buf], start, tb_free[buf])
                        count += 16
            tb_count[buf] += count
            v = m.TB[:, buf, :, :, :].rearrange("p h q (a c) -> p (h q a) c", c=64)
            tb_tok[q] = pool.do(lambda e: e.tensor_tensor(v, v, nmask, ALU.add), (tbs[buf], tb_count[buf]), loaded)

        table(0)
        table(1)
        qt, kt_, vt = [], [], []
        xh, xl = xn(0, n)
        for c in range(4):
            def evac(t, acc, tok):
                r = act.do(lambda e: e.activation(m.QB[:, 2 * c + t, 0:n], acc, ACT.Copy, scale=0.125), tok)
                qt.append(r)
                return r
            linear(w, 0, KT, c * 256, 256, xh, xl, xt, evac)
        xh, xl = xn(0, 512)
        for c in range(4):
            def evac(t, acc, tok):
                r = act.do(lambda e: e.activation(m.KB[:, 2 * c + t, :], acc, ACT.Copy), tok)
                kt_.append(r)
                return r
            linear(w, 0, KT, 1024 + c * 256, 256, xh, xl, xt, evac)
        for c in range(4):
            def evac(t, acc, tok):
                r = act.do(lambda e: e.activation(m.VB[:, t, c * 256:(c + 1) * 256], acc, ACT.Copy), tok)
                vt.append(r)
                return r
            linear_tok(w, 2048 + c * 256, 256, 4, xt, evac)
        flush()
        flip = cst("flip")
        pb_free = [None] * 3
        pt_free = [None] * 2
        otok = [[] for _ in range(KT)]
        jobs = []
        for h in range(16):
            jobs.append((h, 0))
            if ctx_out:
                jobs.append((h, 1))
        npb = [0]
        obank = {}

        def attend(i):
            h, cx = jobs[i]
            o = 64 * (h % 2)
            out = []
            for qb in range(2):
                pbuf = npb[0] % 3
                npb[0] += 1
                b, acc = bank()
                q = m.QB[o:o + 64, h // 2, cx * S + qb * P:cx * S + (qb + 1) * P]
                width = 256 if cx else 512
                k = m.KB[o:o + 64, h // 2, 512 - width:512]
                if cx:
                    tok = pe.do(lambda e: e.matmul(acc[:, 0:256], q, k, start=True, stop=True), qt, kt_)
                else:
                    pe.go(lambda e: e.matmul(acc[:, S:512], q, k[:, S:512], start=True, stop=True), qt, kt_)
                    pe.go(lambda e: e.matmul(acc[:, 0:S], q, k[:, 0:S], start=True, stop=False))
                    tok = pe.do(lambda e: e.matmul(acc[:, 0:S], flip, m.TB[:, (h // 2) % 2, h % 2, qb, :],
                                                   start=False, stop=True), tb_tok[h // 2])
                    if h % 2 == 1 and qb == 1:
                        tb_free[(h // 2) % 2] = tok
                        if h // 2 + 2 < 8:
                            table(h // 2 + 2)
                st = m.stat[:, 16 + pbuf * 4:20 + pbuf * 4]
                PBx = m.PB2[:, pbuf, 0:width]
                t = dve.do(lambda e: e.tensor_reduce(st[:, 0:1], acc[:, 0:width], AX.X, ALU.max, negate=True),
                           tok, pb_free[pbuf])
                ex = act.do(lambda e: e.activation(PBx, acc[:, 0:width], ACT.Exp, bias=st[:, 0:1],
                                                   accum_out=st[:, 1:2]), t, pb_free[pbuf])
                bank_free[b] = ex
                t = dve.do(lambda e: e.reciprocal(st[:, 2:3], st[:, 1:2]), ex)
                t = dve.do(lambda e: e.tensor_scalar(PBx, PBx, st[:, 2:3], None, ALU.mult), t)
                out.append((pbuf, t))
            return out

        def finish_job(i, probs):
            h, cx = jobs[i]
            o = 64 * (h % 2)
            buf = i % 2
            nk = 2 if cx else 4
            got = []
            for qb in range(2):
                pbuf, t = probs[qb]
                b, acc = bank()
                for kt in range(nk):
                    tok = pe.do(lambda e, kt=kt: e.transpose(acc[:, kt * P:(kt + 1) * P],
                                                             m.PB2[:, pbuf, kt * P:(kt + 1) * P], ident), t)
                pb_free[pbuf] = tok
                dst = m.PT2[:, buf, 0:nk, qb * P:(qb + 1) * P]
                src = acc[:, 0:nk * P].rearrange("p (k q) -> p k q", k=nk)
                if qb == 0:
                    c = act.do(lambda e: e.activation(dst, src, ACT.Copy), tok, pt_free[buf])
                else:
                    c = dve.do(lambda e: e.tensor_copy(dst, src), tok, pt_free[buf])
                bank_free[b] = c
                got.append(c)

            def pv_product():
                b, acc = bank()
                k0 = 2 if cx else 0
                for kt in range(nk):
                    f = (lambda e, kt=kt: e.matmul(acc[o:o + 64, 0:S], m.VB[:, k0 + kt, h * 64:(h + 1) * 64],
                                                   m.PT2[:, buf, kt, :], start=kt == 0, stop=kt == nk - 1))
                    if kt < nk - 1:
                        pe.go(f, got, vt)
                    else:
                        tok = pe.do(f)
                pt_free[buf] = tok
                hi = m.XN[o:o + 64, 0, h // 2, cx * S:(cx + 1) * S]
                lo = m.XN[o:o + 64, 1, h // 2, cx * S:(cx + 1) * S]
                r = halves(hi, lo, acc[o:o + 64, 0:S], tok)
                bank_free[b] = r
                otok[h // 2].append(r)

            return pv_product

        probs = attend(0)
        last = None
        for i in range(len(jobs)):
            f = finish_job(i, probs)
            if i + 1 < len(jobs):
                probs = attend(i + 1)
            f()
        xh, xl = xn(0, n)
        grow(n, xh, xl, otok, n, modcol(layer, 2), T["na_wo_2"][slot])

    tb_count = [0, 0]

    def conformer(layer):
        xt = norm(512, lambda k, s: m.gs[:, layer, 0, k, s:s + 1], modcol(layer, 0))
        xh, xl = xn(0, 512)
        w = T["cv_w1_2"][0]
        pads = [pool.do(lambda e, a=a: e.memset(m.U[:, :, :, a:a + 15], 0.0), xt[KT - 1]) for a in (0, 271)]
        ab_free = [None, None]
        cv_tok = [None] * KT
        for c in range(4):
            at = {}

            def evac_a(t, acc, tok):
                at[t] = act.do(lambda e: e.activation(m.AB[:, c % 2, t, :], acc, ACT.Identity,
                                                      bias=pv("cv_b1_2", 2 * c + t, 0)), tok, ab_free[c % 2])
                return at[t]

            def evac_g(t, acc, tok):
                k = 2 * c + t
                r = act.do(lambda e: e.activation(m.SGM[:, t, :], acc, ACT.Sigmoid,
                                                  bias=pv("cv_b1_2", k, 1)), tok, sg_free[t])
                u = dve.do(lambda e: e.tensor_tensor(
                    m.U[:, k, :, 15:271], m.AB[:, c % 2, t, :].rearrange("p (s t) -> p s t", s=2),
                    m.SGM[:, t, :].rearrange("p (s t) -> p s t", s=2), ALU.mult), r, at[t], pads)
                sg_free[t] = u
                if t == 1:
                    ab_free[c % 2] = u
                ut[k] = u
                return r

            ut = {}
            if c == 0:
                sg_free = [None, None]
            linear(w, 0, KT, c * 256, 256, xh, xl, xt, evac_a)
            linear(w, 0, KT, 1024 + c * 256, 256, xh, xl, xt, evac_g)
            for t in range(2):
                k = 2 * c + t
                out = m.CV[:, k, :].rearrange("p (s t) -> p s t", s=2)
                r = dve.do(lambda e: e.tensor_scalar(out, m.U[:, k, :, 0:S], pv("cv_dw_2", k, 0),
                                                     pv("cv_dwb_2", k), ALU.mult, ALU.add), ut[k], pads)
                for i in range(1, 31):
                    r = dve.do(lambda e, i=i: e.scalar_tensor_tensor(
                        out=out, in0=m.U[:, k, :, i:i + S], scalar=pv("cv_dw_2", k, i), in1=out,
                        op0=ALU.mult, op1=ALU.add), r)
                cv_tok[k] = r
                sumsq(m.CV[:, k, :], k, KT, 512, r, square=False)
        flush()
        r = act.do(lambda e: e.activation(m.RS[:, :], ps[6][:, :], ACT.Copy, scale=-1.0 / D), stat["tok"], rs_free[0])
        bank_free[6] = r
        for k in range(KT):
            cv_tok[k] = dve.do(lambda e: e.tensor_tensor(m.CV[:, k, :], m.CV[:, k, :], m.RS[:, :], ALU.add), r, cv_tok[k])
            sumsq(m.CV[:, k, :], k, KT, 512, cv_tok[k])
            if k >= 1:
                pend.pop(0)()
        flush()
        rs_free[0] = cv_tok[KT - 1]
        r = rstd(512, D, m.RS[:, :])
        free = (m.sem["pe"], pe.n)
        toks = []
        for k in range(KT):
            t = dve.do(lambda e: e.scalar_tensor_tensor(out=m.CV[:, k, :], in0=m.CV[:, k, :], scalar=pv("cv_ln_g_2", k),
                                                        in1=m.RS[:, :], op0=ALU.mult, op1=ALU.mult), r, cv_tok[k])
            t = act.do(lambda e: e.activation(m.CV[:, k, :], m.CV[:, k, :], ACT.Silu, bias=pv("cv_ln_b_2", k)), t)
            toks.append(halves(m.XN[:, 0, k, :], m.XN[:, 1, k, :], m.CV[:, k, :], t, free))
        rs_free[0] = toks[-1]
        gate = modcol(layer, 2)
        w2 = T["cv_w2_2"][0]
        for c in range(4):
            def evac(t, acc, tok):
                j = 2 * c + t
                buf = t
                y = act.do(lambda e: e.activation(m.AB[:, 0, buf, :], acc, ACT.Identity, bias=pv("cv_b2_2", j)),
                           tok, ab2_free[buf])
                ab2_free[buf] = residual(j, 512, gate, m.AB[:, 0, buf, :], y, True)
                return y
            if c == 0:
                ab2_free = [None, None]
            linear(w2, 0, KT, c * 256, 256, xh, xl, toks, evac)

    def shortconv(layer):
        xt = norm(512, lambda k, s: m.gs[:, layer, 0, k, s:s + 1], modcol(layer, 0))
        xh, xl = xn(0, 512)
        w = T["sc_win_2"][0]
        pads = [pool.do(lambda e, a=a: e.memset(m.UP[:, :, :, :, a:a + 1], 0.0), xt[KT - 1]) for a in (0, 257)]
        y = [None] * KT
        cgt, uft, cot = {}, {}, {}
        cg_free = [None, None]
        up_free = [None, None]
        co_free = [None, None]
        for c in range(4):
            buf = c % 2

            def evac_c(t, acc, tok):
                cgt[t] = act.do(lambda e: e.activation(m.CG[:, buf, t, :], acc, ACT.Copy), tok, cg_free[buf])
                return cgt[t]

            def evac_v(t, acc, tok):
                uft[t] = dve.do(lambda e: e.tensor_tensor(
                    m.UP[:, buf, t, :, 1:257], acc.rearrange("p (s t) -> p s t", s=2),
                    m.CG[:, buf, t, :].rearrange("p (s t) -> p s t", s=2), ALU.mult), tok, cgt[t], up_free[buf])
                if t == 1:
                    cg_free[buf] = uft[1]
                return uft[t]

            def evac_b(t, acc, tok):
                k = 2 * c + t
                r = dve.do(lambda e: e.tensor_tensor(m.CO[:, buf, t, :], acc, m.CO[:, buf, t, :], ALU.mult),
                           tok, cot[t])
                y[k] = (r, buf, t)
                return r

            linear(w, 0, KT, 1024 + c * 256, 256, xh, xl, xt, evac_c)
            linear(w, 0, KT, 2048 + c * 256, 256, xh, xl, xt, evac_v)
            for t in range(2):
                k = 2 * c + t
                out = m.CO[:, buf, t, :].rearrange("p (s t) -> p s t", s=2)
                r = dve.do(lambda e: e.tensor_scalar(out, m.UP[:, buf, t, :, 0:S], pv("sc_conv_2", k, 0), None,
                                                     ALU.mult), uft[t], pads, co_free[buf])
                for i in (1, 2):
                    r = dve.do(lambda e, i=i: e.scalar_tensor_tensor(
                        out=out, in0=m.UP[:, buf, t, :, i:i + S], scalar=pv("sc_conv_2", k, i), in1=out,
                        op0=ALU.mult, op1=ALU.add), r)
                cot[t] = r
            up_free[buf] = r
            linear(w, 0, KT, c * 256, 256, xh, xl, xt, evac_b)
            done = []
            for t in range(2):
                k = 2 * c + t
                r = y[k][0]
                y[k] = halves(m.YH[:, 0, k, :], m.YH[:, 1, k, :], m.CO[:, buf, t, :], r)
                done.append(y[k])
            co_free[buf] = done
        yh, yl = (lambda k: m.YH[:, 0, k, :]), (lambda k: m.YH[:, 1, k, :])
        grow(512, yh, yl, y, 512, modcol(layer, 2), T["sc_wout_2"][0])

    def mlp(layer, n):
        xt = norm(n, lambda k, s: m.gs[:, layer, 1, k, s:s + 1], modcol(layer, 3))
        xh, xl = xn(0, n)
        w1, w2 = T["mlp_w1_2"][layer], T["mlp_w2_2"][layer]
        gate = modcol(layer, 5)
        h_free = [None, None]
        htok = {}
        rl_free = [None] * 4
        nrl = [0]

        def up(q):
            buf = q % 2
            toks = [None] * KT
            for c in range(4):
                def evac(t, acc, tok):
                    r = nrl[0] % 4
                    nrl[0] += 1
                    a = act.do(lambda e: e.activation(m.RL[:, r, 0:n], acc, ACT.Relu), tok, rl_free[r])
                    d = dve.do(lambda e: e.tensor_tensor(m.RL[:, r, 0:n], acc, m.RL[:, r, 0:n], ALU.mult), a, tok)
                    k = 2 * c + t
                    toks[k] = halves(m.H2[:, buf, 0, k, 0:n], m.H2[:, buf, 1, k, 0:n], m.RL[:, r, 0:n], d, h_free[buf])
                    rl_free[r] = toks[k]
                    return d
                linear(w1, 0, KT, q * D + c * 256, 256, xh, xl, xt, evac)
            htok[q] = toks

        def down(q):
            buf = q % 2
            hh, hl = (lambda k: m.H2[:, buf, 0, k, 0:n]), (lambda k: m.H2[:, buf, 1, k, 0:n])
            for c in range(4):
                def evac(t, acc, tok):
                    h_free[buf] = tok
                    return residual(2 * c + t, n, gate, acc, tok, q == 3)
                linear(w2, q * D, KT, c * 256, 256, hh, hl, htok[q], evac)

        up(0)
        for q in range(4):
            if q + 1 < 4:
                up(q + 1)
            down(q)

    neighbourhood(0, 0, True)
    mlp(0, 512)
    conformer(1)
    mlp(1, 512)
    shortconv(2)
    mlp(2, 512)
    neighbourhood(3, 1, False)
    mlp(3, S)

    flush()
    r = rstd(S, D, m.RS[:, 0:S])
    fo = []
    for k in range(KT):
        buf = k % 2
        t = dve.do(lambda e: e.scalar_tensor_tensor(out=m.X[:, k, 0:S], in0=m.X[:, k, 0:S], scalar=pv("final_g_2", k),
                                                    in1=m.RS[:, 0:S], op0=ALU.mult, op1=ALU.mult), r)
        b, acc = bank()
        for i in range(2):
            tok = pe.do(lambda e, i=i: e.transpose(acc[:, i * P:(i + 1) * P], m.X[:, k, i * P:(i + 1) * P], ident), t)
        t = act.do(lambda e: e.activation(m.FO[:, :, k * P:(k + 1) * P],
                                          acc[:, 0:S].rearrange("p (i d) -> p i d", i=2), ACT.Copy), tok)
        bank_free[b] = t
    sp.dma(T["out"][0].rearrange("(t p) d -> p t d", p=P), m.FO[:, :, :], m.sem["out"], t)
    sp.wait([(m.sem["out"], 16)])
    return order, {"pe": pe, "act": act, "dve": dve, "pool": pool, "sp": sp}


def build(nc, T):
    with ExitStack() as ctx:
        m = allocate(nc, ctx)
        units, _ = program(m, T, None)
        _, q = program(m, T, units)
        block = ctx.enter_context(nc.Block())

        @block.sync
        def _(e):
            for f in q["sp"].ops:
                f(e)

        @block.tensor
        def _(e):
            for f in q["pe"].ops:
                f(e)

        @block.scalar
        def _(e):
            for f in q["act"].ops:
                f(e)

        @block.vector
        def _(e):
            for f in q["dve"].ops:
                f(e)

        @block.gpsimd
        def _(e):
            for f in q["pool"].ops:
                f(e)


_INS = ["x", "positions", "attn_norm", "attn_w_in", "attn_w_out", "mlstm_norm", "mlstm_w_in", "mlstm_conv_w",
        "mlstm_conv_b", "mlstm_ig_bias", "mlstm_fg_bias", "mlstm_head_gain", "mlstm_w_out", "ffn_norm", "ffn_w_in",
        "ffn_w_out", "final_norm", "c_2", "ctx_2", "c_ctx_2", "mod_w_2", "mod_b_2", "norm1_g_2", "norm2_g_2",
        "mlp_w1_2", "mlp_w2_2", "na_wqkv_2", "na_wo_2", "na_rpb_2", "cv_w1_2", "cv_b1_2", "cv_dw_2", "cv_dwb_2",
        "cv_ln_g_2", "cv_ln_b_2", "cv_w2_2", "cv_b2_2", "sc_win_2", "sc_conv_2", "sc_wout_2", "final_g_2"]
_AS_ROWS = {name: k for name, k in ROWS}


def kernel(**inputs):
    import concourse.bacc as _bacc
    from concourse.bass_utils import run_bass_kernel_spmd as _run

    nc = _bacc.Bacc("TRN2", target_bir_lowering=False, num_devices=1)
    arrays, T = {}, {}
    for name in _INS:
        a = np.ascontiguousarray(inputs[name])
        if name in _AS_ROWS:
            a = a.reshape(_AS_ROWS[name], D)
        arrays[f"in_{name}"] = a
        T[name] = nc.dram_tensor(f"in_{name}", a.shape, mybir.dt.from_np(a.dtype), kind="ExternalInput").ap()
    arrays["in_consts"] = constants()
    T["consts"] = nc.dram_tensor("in_consts", arrays["in_consts"].shape, F32, kind="ExternalInput").ap()
    T["out"] = nc.dram_tensor("out_0", (1, S, D), F32, kind="ExternalOutput").ap()
    build(nc, T)
    r = _run(nc, [arrays], core_ids=[0])
    return r.results[0]["out_0"]
```

```python
from contextlib import ExitStack

import numpy as np

import concourse.bass as bass
from concourse import mybir

F32 = mybir.dt.float32
F32R = mybir.dt.float32r
I32 = mybir.dt.int32
ALU = mybir.AluOpType
ACT = mybir.ActivationFunctionType
AX = mybir.AxisListType

P = 128
D = 1024
KT = 8
S = 256
DFF = 2816
DFF2 = 4096
NEG = -1.0e30
ROPE_FREQ = [1.0, 0.44036659598350525, 0.1939227432012558, 0.08539710193872452, 0.03760603070259094,
             0.016560440883040428, 0.007292664609849453, 0.0032114461064338684, 0.0014142135623842478,
             0.0006227724370546639, 0.00027424816832155466, 0.00012076973507646471, 5.3182957344688475e-05,
             2.34199997066753e-05, 1.0313385246263351e-05, 4.541670477919979e-06]
TWO_PI_A = 6.28125
TWO_PI_B = 1.9340515136718750e-03
TWO_PI_C = float(2.0 * np.pi - 6.28125 - 1.9340515136718750e-03)
ROUND = 12582912.0

ROWS = [("attn_norm", 1), ("mlstm_norm", 1), ("mlstm_head_gain", 1), ("ffn_norm", 2), ("final_norm", 1),
        ("mlstm_conv_w", 4), ("mlstm_conv_b", 1), ("norm1_g_2", 4), ("norm2_g_2", 4), ("cv_b1_2", 2),
        ("cv_dw_2", 31), ("cv_dwb_2", 1), ("cv_ln_g_2", 1), ("cv_ln_b_2", 1), ("cv_b2_2", 1),
        ("sc_conv_2", 3), ("final_g_2", 1), ("mod_b_2", 24), ("c_2", 1), ("c_ctx_2", 1)]
ROW = {}
NROW = 0
for _n, _k in ROWS:
    ROW[_n] = NROW
    NROW += _k


def const_layout():
    at, out = 0, {}
    for name, width in (("ident", 128), ("ones", 128), ("nmask", 64), ("fold", 2),
                        ("mmask", 384), ("rot", 32), ("freq", 1), ("amask", 1152)):
        out[name] = (at, width)
        at += width
    return out, at


def constants():
    lay, width = const_layout()
    c = np.zeros((P, width), np.float32)

    def put(name, a):
        a = np.asarray(a, np.float32)
        at = lay[name][0]
        c[:a.shape[0], at:at + a.shape[1]] = a

    fold = np.zeros((P, 2))
    for g in range(4):
        fold[32 * g, 0] = fold[32 * g + 1, 1] = 1.0
    put("fold", fold)
    put("ident", np.eye(P))
    put("ones", np.ones((P, P)))
    t = np.arange(S)
    masks = []
    for r, window in ((1, 128), (4, 128), (16, 128)):
        dist = t[:, None] - t[None, :]
        ok = (dist >= 0) & (dist % r == 0) & (dist // r <= window)
        masks.append(np.where(ok, 0.0, NEG))
    put("amask", np.concatenate([m[128:, :] for m in masks] + [m[:128, :128] for m in masks], axis=1))
    col = np.arange(64)
    start = np.clip(col - 8, 0, 48)
    ok = (col[None, :] >= start[:, None]) & (col[None, :] < start[:, None] + 16)
    nm = np.where(ok, 0.0, NEG)
    put("nmask", np.concatenate([nm, nm])[::-1])
    keep = t[:, None] <= t[None, :]
    mm = np.where(keep, 0.0, NEG)
    put("mmask", np.concatenate([mm[:128, :], mm[128:, 128:]], axis=1))
    rot = np.zeros((32, 32))
    for i in range(16):
        rot[16 + i, i] = -1.0
        rot[i, 16 + i] = 1.0
    put("rot", rot)
    put("freq", np.array(ROPE_FREQ + ROPE_FREQ, np.float32)[:, None])
    return c


class Step:

    def matmul(self, *a, **k):
        self.op = lambda e: e.matmul(*a, **k)

    def transpose(self, *a, **k):
        self.op = lambda e: e.transpose(*a, **k)

    def activation(self, *a, **k):
        self.op = lambda e: e.activation(*a, **k)

    def tensor_copy(self, *a, **k):
        self.op = lambda e: e.tensor_copy(*a, **k)

    def tensor_tensor(self, *a, **k):
        self.op = lambda e: e.tensor_tensor(*a, **k)

    def tensor_scalar(self, *a, **k):
        self.op = lambda e: e.tensor_scalar(*a, **k)

    def scalar_tensor_tensor(self, *a, **k):
        self.op = lambda e: e.scalar_tensor_tensor(*a, **k)

    def tensor_reduce(self, *a, **k):
        self.op = lambda e: e.tensor_reduce(*a, **k)

    def tensor_tensor_reduce(self, *a, **k):
        self.op = lambda e: e.tensor_tensor_reduce(*a, **k)

    def tensor_tensor_scan(self, *a, **k):
        self.op = lambda e: e.tensor_tensor_scan(*a, **k)

    def reciprocal(self, *a, **k):
        self.op = lambda e: e.reciprocal(*a, **k)

    def memset(self, *a, **k):
        self.op = lambda e: e.memset(*a, **k)


def step(fn):
    s = Step()
    fn(s)
    return s.op


class Queue:

    def __init__(self, sem, step=1):
        self.sem, self.n, self.ops, self.seen = sem, 0, [], {}
        self.total = 0

    def wait(self, deps):
        for d in flat(deps):
            sem, v = d
            if self.seen.get(sem.name, 0) < v:
                self.seen[sem.name] = v
                self.ops.append(lambda e, sem=sem, v=v: e.wait_ge(sem, v))

    def go(self, fn, *deps):
        self.wait(deps)
        self.ops.append(step(fn))
        self.total += 1

    def do(self, fn, *deps):
        self.wait(deps)
        self.n += 1
        sem, op = self.sem, step(fn)
        self.total += 1
        self.ops.append(lambda e: op(e).then_inc(sem, 1))
        return (sem, self.n)

    def dma(self, out, in_, sem, *deps):
        self.wait(deps)
        self.ops.append(lambda e: e.dma_start(out, in_).then_inc(sem, 16))


def flat(deps):
    for d in deps:
        if d is None:
            continue
        if isinstance(d, tuple) and len(d) == 2 and isinstance(d[1], int):
            yield d
        else:
            yield from flat(d)


class Memory:
    pass


RAW = 3
HL = 2
NBANK = 6


def allocate(nc, ctx):
    m = Memory()
    lay, width = const_layout()

    def sb(name, shape, dt=F32, stack=ctx):
        return stack.enter_context(nc.sbuf_tensor(name, shape, dt))

    m.width = lay["amask"][0]
    m.cst = sb("cst", [P, m.width])
    m.PV = sb("PV", [P, KT, NROW])
    m.eps = sb("eps", [P, 1])
    m.sc = sb("sc", [P, KT, 32])
    m.mod = sb("mod", [P, 4, 48, 2])
    m.gs = sb("gs", [P, 4, 2, KT, 2])
    m.macc = sb("macc", [P, 2, 256])
    m.gb = sb("gb", [8, 2])
    m.stat = sb("stat", [P, 64])
    m.X = sb("X", [P, KT, 512])
    m.raw = [sb(f"raw{i}", [P, 2048]) for i in range(RAW)]
    m.hi = [sb(f"hi{i}", [P, 2048], F32R) for i in range(HL)]
    m.lo = [sb(f"lo{i}", [P, 2048], F32R) for i in range(HL)]
    m.XN = sb("XN", [P, 2, KT, 512], F32R)
    m.SQ = sb("SQ", [P, 2, 512])
    m.SA = sb("SA", [P, 512])
    m.RS = sb("RS", [P, 512])
    m.TN = sb("TN", [P, 2, 512])

    def phase(*tensors):
        with ExitStack() as st:
            return [sb(n, s, d, st) for n, s, d in tensors]

    m.amask, m.rope, m.rows, m.xin, m.pos, m.ang = phase(
        ("amask", [P, 1152], F32), ("rope", [32, 2, S], F32), ("rows", [P, D], F32), ("xin", [P, 2, D], F32),
        ("pos", [32, S], I32), ("ang", [32, 4, S], F32))
    _, _, m.QK, m.V1, m.PB, m.PT1, m.RT = phase(
        ("amask_", [P, 1152], F32), ("rope_", [32, 2, S], F32),
        ("QK", [P, 2, 3, 2, 2, S], F32), ("V1", [P, 2, 2, 3, 256], F32), ("PB", [P, 2, 1152], F32),
        ("PT1", [P, 2, 3, 384], F32), ("RT", [32, 2, 512], F32))
    m.HF, m.SG = phase(("HF", [P, 2, 22, S], F32R), ("SG", [P, 2, 2, S], F32))
    m.CB, m.QKM, m.VM, m.SO, m.HS, m.WT, m.G8, m.AC, m.HT = phase(
        ("CB", [P, KT, 260], F32), ("QKM", [P, KT, S], F32), ("VM", [P, 2, 8, P + 1], F32), ("SO", [P, KT, S], F32),
        ("HS", [P, 2, S], F32), ("WT", [P, 2, 384], F32), ("G8", [8, 8, S], F32),
        ("AC", [P, 2, 2, 8], F32), ("HT", [P, 2, 2, P], F32))
    _, _, m.cin = phase(("HF_", [P, 2, 22, S], F32), ("SG_", [P, 2, 2, S], F32), ("cin", [P, 2, D], F32))
    m.QB, m.KB, m.VB, m.OB, m.TB, m.PB2, m.PT2 = phase(
        ("QB", [P, 2, 2, 512], F32), ("KB", [P, 2, 2, 512], F32), ("VB", [P, 2, 4, 256], F32),
        ("OB", [P, 2, KT, 512], F32R), ("TB", [P, 2, 2, 512], F32), ("PB2", [P, 2, 2, 512], F32),
        ("PT2", [P, 2, 4, S], F32))
    m.H2, m.RL = phase(("H2", [P, 2, 2, KT, 512], F32R), ("RL", [P, 4, 512], F32))
    m.U, m.CV, m.AB, m.SGM = phase(
        ("U", [P, KT, 2, 286], F32), ("CV", [P, KT, 512], F32), ("AB", [P, 2, 2, 512], F32),
        ("SGM", [P, 2, 512], F32))
    m.YH, m.CG, m.UP, m.CO = phase(
        ("YH", [P, 2, KT, 512], F32R), ("CG", [P, 2, 2, 512], F32), ("UP", [P, 2, 2, 2, 258], F32), ("CO", [P, 2, 2, 512], F32))
    m.FO, = phase(("FO", [P, 2, D], F32),)

    m.ps = [ctx.enter_context(nc.psum_tensor(f"ps{i}", [P, 512], F32)) for i in range(8)]
    m.sem = {n: ctx.enter_context(nc.semaphore(f"s_{n}"))
             for n in ["pe", "act", "dve", "pool", "ld", "x", "ci", "pos", "cst", "tb0", "tb1", "out"]
             + [f"raw{i}" for i in range(RAW)]}
    m.lay = lay
    return m


def program(m, T, units):
    pe, act, dve, pool = (Queue(m.sem[n]) for n in ("pe", "act", "dve", "pool"))
    sp = Queue(None)
    ps = m.ps
    bank_free = [None] * 8
    state = {"bank": 0, "unit": 0, "next": 0, "halved": 0, "tn": 0}
    order = []
    raw_free = [None] * RAW
    raw_count = [0] * RAW
    raw_known = set()
    hl_free = [None] * HL
    hl_slot = {}
    ready_at = {}
    background = []
    pend = []

    def cst(name, rows=P):
        at, w = m.lay[name]
        assert at < m.width
        return m.cst[0:rows, at:at + w]

    ident, ones = cst("ident"), cst("ones")

    def pv(name, k, i=0):
        r = ROW[name] + i
        return m.PV[:, k, r:r + 1]

    def bank():
        b = state["bank"]
        state["bank"] = (b + 1) % NBANK
        pe.wait([bank_free[b]])
        return b, ps[b]

    def bring(j):
        src, kt, cols, whole = units[j]
        r = j % RAW
        n = kt * cols
        raw_count[r] += 16
        sp.dma(m.raw[r][:, 0:n].rearrange("p (k n) -> p k n", k=kt), src, m.sem[f"raw{r}"], raw_free[r])
        landed = (m.sem[f"raw{r}"], raw_count[r])
        if whole:
            ready_at[j] = [landed]
            return
        h = state["halved"] % HL
        state["halved"] += 1
        hl_slot[j] = h
        raw, hi, lo = m.raw[r], m.hi[h], m.lo[h]
        cuts = [0, (kt + 1) // 2 * cols, n]
        ready_at[j] = []
        free = []
        for a, b in zip(cuts, cuts[1:]):
            t = act.do(lambda e: e.activation(hi[:, a:b], raw[:, a:b], ACT.Copy), landed, hl_free[h])
            d = dve.do(lambda e: e.tensor_tensor(lo[:, a:b], raw[:, a:b], hi[:, a:b].bitcast(F32), ALU.subtract),
                       landed, t, hl_free[h])
            ready_at[j].append(d)
            free += [t, d]
        raw_free[r] = free
        raw_known.add(j)

    def take(src, kt, cols, whole=False):
        j = state["unit"]
        state["unit"] += 1
        order.append((src, kt, cols, whole))
        n = kt * cols
        if units is not None:
            assert units[j][1:] == (kt, cols, whole)
            held = sum(not units[i][3] for i in range(j, state["next"]))
            while state["next"] < len(units):
                i = state["next"]
                if i > j and (held + (not units[i][3]) > HL or (i >= RAW and i - RAW not in raw_known)):
                    break
                bring(i)
                held += not units[i][3]
                state["next"] += 1
        if whole:
            return j, m.raw[j % RAW][:, 0:n].rearrange("p (k n) -> p k n", k=kt)
        h = hl_slot.get(j, 0)
        return j, m.hi[h][:, 0:n].rearrange("p (k n) -> p k n", k=kt), \
            m.lo[h][:, 0:n].rearrange("p (k n) -> p k n", k=kt)

    def ready(j, k, kt):
        if units is not None:
            pe.wait([ready_at[j][0 if k < (kt + 1) // 2 else -1]])

    def used(j, tok, whole=False):
        if whole:
            raw_free[j % RAW] = tok
            raw_known.add(j)
        else:
            hl_free[hl_slot.get(j, 0)] = tok

    def advance(n=1):
        for _ in range(n):
            if background and next(background[0], None) is None:
                background.pop(0)

    def flush():
        todo = list(pend)
        pend.clear()
        for f in todo:
            f()

    def weight(w, k0, kt, c0, cols):
        return w[k0:k0 + kt * P, c0:c0 + cols].rearrange("(k p) n -> p k n", p=P)

    def mm3(out, whi, wlo, xhi, xlo, first, last, signal=False):
        pairs = [(whi, xhi), (whi, xlo), (wlo, xhi)]
        tok = None
        for i, (a, b) in enumerate(pairs):
            f = (lambda e, a=a, b=b, i=i: e.matmul(out, a, b, start=first and i == 0, stop=last and i == 2))
            if (last or signal) and i == 2:
                tok = pe.do(f)
            else:
                pe.go(f)
        return tok

    def linear(w, k0, kt, c0, cols, xhi, xlo, xtok, evac, adv=1, outer=False):
        j, hi, lo = take(weight(w, k0, kt, c0, cols), kt, cols)
        n = xhi(0).shape[-1]
        tiles = list(range(cols // P))
        for group in ([tiles] if outer else [[t] for t in tiles]):
            banks = [bank() for _ in group]
            toks = [None] * len(group)
            for k in range(kt):
                pe.wait([xtok[k]])
                ready(j, k, kt)
                for i, t in enumerate(group):
                    toks[i] = mm3(banks[i][1][:, 0:n], hi[:, k, t * P:(t + 1) * P], lo[:, k, t * P:(t + 1) * P],
                                  xhi(k), xlo(k), k == 0, k == kt - 1)
            used(j, toks[-1])
            if group[0] == 0:
                flush()
            for i, t in enumerate(group):
                bank_free[banks[i][0]] = evac(t, banks[i][1][:, 0:n], toks[i])
            advance(adv * len(group))

    def linear_tok(w, c0, cols, ntt, xtok, evac, adv=1):
        j, hi, lo = take(weight(w, 0, KT, c0, cols), KT, cols)
        for t in range(ntt):
            b, acc = bank()
            acc = acc[:, 0:cols]
            for k in range(KT):
                pe.wait([xtok[k]])
                ready(j, k, KT)
                tok = mm3(acc, m.XN[:, 0, k, t * P:(t + 1) * P], m.XN[:, 1, k, t * P:(t + 1) * P],
                          hi[:, k, :], lo[:, k, :], k == 0, k == KT - 1)
            used(j, tok)
            if t == 0:
                flush()
            bank_free[b] = evac(t, acc, tok)
            advance(adv)

    def xn(lo, hi):
        return (lambda k: m.XN[:, 0, k, lo:hi]), (lambda k: m.XN[:, 1, k, lo:hi])

    sq_free = [None, None]
    sa_free = [None]
    stat = {"tok": None}

    NP = 6

    def sumsq(src, i, n, tok):
        buf = i % 2
        dst = m.SA[:, 0:n] if i == 0 else m.SQ[:, buf, 0:n]
        a = act.do(lambda e: e.activation(dst, src, ACT.Square), tok, sa_free[0] if i == 0 else sq_free[buf])
        if i == 0:
            stat["sa"] = a
            return
        if i < NP:
            stat["sa"] = pool.do(lambda e: e.tensor_tensor(m.SA[:, 0:n], m.SA[:, 0:n], dst, ALU.add), a, stat["sa"])
            sq_free[buf] = stat["sa"]
            return
        sa = stat["sa"]

        def later():
            if i == NP:
                sa_free[0] = pe.do(lambda e: e.matmul(ps[6][:, 0:n], ones, m.SA[:, 0:n], start=True, stop=False),
                                   sa, bank_free[6])
            stat["tok"] = pe.do(lambda e: e.matmul(ps[6][:, 0:n], ones, dst, start=False, stop=i == KT - 1), a)
            sq_free[buf] = stat["tok"]

        pend.append(later)

    def total(src, i, n, tok):
        def later():
            stat["tok"] = pe.do(lambda e: e.matmul(ps[6][:, 0:n], ones, src, start=i == 0, stop=i == KT - 1),
                                tok, bank_free[6] if i == 0 else None)

        pend.append(later)

    def rstd(n, count, out):
        t = act.do(lambda e: e.activation(out, ps[6][:, 0:n], ACT.Ln, bias=m.eps[:, 0:1], scale=1.0 / count),
                   stat["tok"], eps_tok, rs_free[0])
        bank_free[6] = t
        return act.do(lambda e: e.activation(out, out, ACT.Exp, scale=-0.5), t)

    rs_free = [None]
    tn_free = [None] * 2

    def halves(dst_hi, dst_lo, src, tok, free=None):
        a = act.do(lambda e: e.activation(dst_hi, src, ACT.Copy), tok, free)
        d = dve.do(lambda e: e.tensor_tensor(dst_lo, src, dst_hi.bitcast(F32), ALU.subtract), a, tok, free)
        return d

    def norm(n, gain, shift=None, fillers=0):
        flush()
        free = (m.sem["pe"], pe.n)
        r = rstd(n, D, m.RS[:, 0:n])
        toks = []
        streams = [(0, n)] if shift is None else [(s * S, (s + 1) * S) for s in range(n // S)]
        for k in range(KT):
            buf = state["tn"] % 2
            state["tn"] += 1
            got = []
            for s, (a, b) in enumerate(streams):
                t = dve.do(lambda e, a=a, b=b, s=s: e.scalar_tensor_tensor(
                    out=m.TN[:, buf, a:b], in0=m.X[:, k, a:b], scalar=gain(k, s), in1=m.RS[:, a:b],
                    op0=ALU.mult, op1=ALU.mult), r, tn_free[buf])
                hi, lo, tn = m.XN[:, 0, k, a:b], m.XN[:, 1, k, a:b], m.TN[:, buf, a:b]
                if shift is None:
                    got.append(halves(hi, lo, tn, t, free))
                    continue
                h = act.do(lambda e, hi=hi, tn=tn, s=s: e.activation(hi, tn, ACT.Identity, bias=shift(k, s)),
                           t, free)
                got.append(dve.do(lambda e, hi=hi, lo=lo, tn=tn, s=s: e.scalar_tensor_tensor(
                    out=lo, in0=tn, scalar=shift(k, s), in1=hi.bitcast(F32), op0=ALU.add, op1=ALU.subtract),
                    t, h, free))
            tn_free[buf] = got
            toks.append(got)
        rs_free[0] = toks[-1]
        fill(fillers)
        return toks

    def residual(j, n, gate, acc, tok, last):
        if gate is None:
            t = dve.do(lambda e: e.tensor_tensor(m.X[:, j, 0:n], acc, m.X[:, j, 0:n], ALU.add), tok)
        else:
            for s in range(n // S):
                t = dve.do(lambda e, s=s: e.scalar_tensor_tensor(
                    out=m.X[:, j, s * S:(s + 1) * S], in0=acc[:, s * S:(s + 1) * S], scalar=gate(j, s),
                    in1=m.X[:, j, s * S:(s + 1) * S], op0=ALU.mult, op1=ALU.add), tok)
        if last:
            sumsq(m.X[:, j, 0:n], j, n, t)
        return t

    marks = []

    def note(name):
        marks.append((name, pe.total))

    note("setup")
    ld = m.sem["ld"]
    nld = [0]

    def load(out, in_, q=sp):
        q.dma(out, in_, ld)
        nld[0] += 16

    sp.dma(m.xin[:, :, :], T["x"][0].rearrange("(t p) d -> p t d", p=P), m.sem["x"])
    sp.dma(m.cst[:, :], T["consts"][:, 0:m.width], m.sem["cst"])
    for name, k in ROWS:
        src = T[name]
        r = ROW[name]
        load(m.rows[r:r + k, :], src)
    load(m.gb[:, 0:1], T["mlstm_ig_bias"].rearrange("a h -> h a"))
    load(m.gb[:, 1:2], T["mlstm_fg_bias"].rearrange("a h -> h a"))
    load(m.amask[:, :], T["consts"][:, m.width:m.width + 1152])
    sp.dma(m.pos[:, :], T["positions"].broadcast_to([32, S]), m.sem["pos"])
    consts = (m.sem["cst"], 16)
    loaded = [(ld, nld[0]), consts]
    x_in, c_in = (m.sem["x"], 16), (m.sem["ci"], 16)
    eps_tok = dve.do(lambda e: e.memset(m.eps[:, :], 1e-6))

    for j in range(KT):
        b, acc = bank()
        for t in range(2):
            tok = pe.do(lambda e: e.transpose(acc[:, t * P:(t + 1) * P], m.xin[:, t, j * P:(j + 1) * P], ident),
                        x_in, consts)
        t = dve.do(lambda e: e.tensor_copy(m.X[:, j, 0:S], acc[:, 0:S]), tok)
        bank_free[b] = t
        sumsq(m.X[:, j, 0:S], j, S, t)
    pv_tok = None
    for k in range(KT):
        b, acc = bank()
        t = pe.do(lambda e: e.transpose(acc[:, 0:NROW], m.rows[0:NROW, k * P:(k + 1) * P], ident[0:NROW, 0:NROW]),
                  loaded)
        pv_tok = dve.do(lambda e: e.tensor_copy(m.PV[:, k, :], acc[:, 0:NROW]), t)
        bank_free[b] = pv_tok
    c0 = ROW["c_2"]
    t = dve.do(lambda e: e.memset(m.sc[:, :, :], 0.0))
    sc_tok = act.do(lambda e: e.activation(m.sc[:, :, 0:2], m.PV[:, :, c0:c0 + 2], ACT.Silu), pv_tok, t)
    A = m.ang
    arrived = (m.sem["pos"], 16)
    t = dve.do(lambda e: e.tensor_copy(A[:, 0, :], m.pos[:, :]), arrived)
    t = dve.do(lambda e: e.tensor_scalar(A[:, 1, :], A[:, 0, :], cst("freq", 32), None, ALU.mult), t, loaded)
    t = dve.do(lambda e: e.tensor_scalar(A[:, 2, :], A[:, 1, :], float(1.0 / (2.0 * np.pi)), ROUND,
                                         ALU.mult, ALU.add), t)
    t = dve.do(lambda e: e.tensor_scalar(A[:, 2, :], A[:, 2, :], ROUND, None, ALU.subtract), t)
    for part in (TWO_PI_A, TWO_PI_B, TWO_PI_C):
        t = dve.do(lambda e, part=part: e.scalar_tensor_tensor(
            out=A[:, 1, :], in0=A[:, 2, :], scalar=-part, in1=A[:, 1, :], op0=ALU.mult, op1=ALU.add), t)
    t = dve.do(lambda e: e.tensor_scalar(A[:, 1, :], A[:, 1, :], 3.1415925, -3.1415925, ALU.min, ALU.max), t)
    t = dve.do(lambda e: e.scalar_tensor_tensor(out=A[:, 3, :], in0=A[:, 1, :], scalar=-1.0, in1=A[:, 1, :],
                                                op0=ALU.mult, op1=ALU.max), t)
    t = dve.do(lambda e: e.tensor_scalar(A[:, 3, :], A[:, 3, :], -1.0, float(np.pi / 2), ALU.mult, ALU.add), t)
    act.do(lambda e: e.activation(m.rope[:, 0, :], A[:, 3, :], ACT.Sin), t)
    rope_tok = act.do(lambda e: e.activation(m.rope[:, 1, :], A[:, 1, :], ACT.Sin), t)
    flush()

    mod_next = [0]
    mod_free = [None, None]
    mod_tok = [None] * 4
    gs_tok = [None] * 4

    def mod_unit():
        n = mod_next[0]
        if n >= 96:
            return
        mod_next[0] += 1
        layer, c = n // 24, n % 24
        j, raw = take(weight(T["mod_w_2"][layer], 0, KT, c * 256, 256), KT, 256, True)
        b, acc = bank()
        if units is not None:
            pe.wait(ready_at[j])
        pe.wait([sc_tok])
        for k in range(KT):
            g = 32 * (k % 4)
            f = (lambda e: e.matmul(acc[g:g + 32, 0:256], m.sc[:, k, :], raw[:, k, :], start=k < 4, stop=k >= 4))
            if k < KT - 1:
                pe.go(f)
            else:
                tok = pe.do(f)
        used(j, tok, True)
        buf = n % 2
        t = act.do(lambda e: e.activation(m.macc[:, buf, :], acc[:, 0:256], ACT.Copy), tok, mod_free[buf])
        bank_free[b] = t

        def later():
            for i in range(2):
                o = (2 * c + i) * 2
                q = pe.do(lambda e: e.matmul(ps[7][:, o:o + 2], m.macc[:, buf, i * P:(i + 1) * P], cst("fold"),
                                             start=True, stop=True),
                          t, consts, bank_free[7] if c == 0 else None)
            mod_free[buf] = q
            if c == 23:
                finish(layer, q)

        pend.append(later)

    def finish(layer, tok):
        r = ROW["mod_b_2"] + 6 * layer
        biased = []
        for i in range(6):
            bias = m.PV[:, :, r + i:r + i + 1].broadcast_to([P, KT, 2])
            biased.append(dve.do(lambda e: e.tensor_tensor(
                m.mod[:, layer, i * KT:(i + 1) * KT, :],
                ps[7][:, i * 16:(i + 1) * 16].rearrange("p (k s) -> p k s", s=2), bias, ALU.add), tok, pv_tok))
        bank_free[7] = biased
        for w, name in ((0, "norm1_g_2"), (1, "norm2_g_2")):
            i = 1 + 3 * w
            r = ROW[name] + layer
            gain = m.PV[:, :, r:r + 1].broadcast_to([P, KT, 2])
            t = dve.do(lambda e, w=w, i=i, gain=gain: e.scalar_tensor_tensor(
                out=m.gs[:, layer, w, :, :], in0=m.mod[:, layer, i * KT:(i + 1) * KT, :], scalar=1.0, in1=gain,
                op0=ALU.add, op1=ALU.mult), biased)
        mod_tok[layer] = t

    def modcol(layer, i):
        return lambda k, s: m.mod[:, layer, i * KT + k, s:s + 1]

    def fill(n):
        for _ in range(n):
            mod_unit()
            flush()

    def drain(n=0):
        while background:
            advance()
            if n:
                mod_unit()
                n -= 1
            flush()

    note("attn norm")
    xt = norm(S, lambda k, s: pv("attn_norm", k), fillers=3)
    xhi, xlo = xn(0, S)
    w = T["attn_w_in"][0]
    scale = float(P) ** -0.5
    pb_free = [None, None]
    pt_free = [None, None]
    qk_free = [None, None]
    nrt = [0]
    otoks = [None] * KT

    def attend1(pair, qk_tok, v_tok):
        pbuf = pair % 2
        probs = {}

        def scores(h):
            hh = h % 2
            buf = h % 2
            q = [m.QK[:, pbuf, g, 0, hh, :] for g in range(3)]
            k = [m.QK[:, pbuf, g, 1, hh, :] for g in range(3)]
            parts = [[(q[0][:, P:S], k[0], 0, 256), (q[1][:, P:S], k[1], 256, 256)],
                     [(q[2][:, P:S], k[2], 0, 256)],
                     [(q[g][:, 0:P], k[g][:, 0:P], g * P, P) for g in range(3)]]
            st = m.stat[:, buf * 16:buf * 16 + 16]
            at = 0
            toks = []
            for n, part in enumerate(parts):
                b, acc = bank()
                for a, c, o, width in part:
                    tok = pe.do(lambda e: e.matmul(acc[:, o:o + width], a, c, start=True, stop=True), qk_tok)
                end = o + width
                t = dve.do(lambda e: e.tensor_tensor_reduce(
                    out=m.PB[:, buf, at:at + end], in0=acc[:, 0:end], in1=m.amask[:, at:at + end], scale=1.0,
                    scalar=-3.0e38, op0=ALU.add, op1=ALU.max, accum_out=st[:, n:n + 1]),
                    tok, pb_free[buf], loaded)
                bank_free[b] = t
                toks.append(t)
                at += end
            t = dve.do(lambda e: e.tensor_tensor(st[:, 3:4], st[:, 0:1], st[:, 1:2], ALU.max), toks)
            t = dve.do(lambda e: e.tensor_scalar(st[:, 4:6], st[:, 2:4], -scale, None, ALU.mult), t)
            rngs = ((768, 1152), (0, 768))
            ex = [act.do(lambda e: e.activation(
                m.PB[:, buf, r[0]:r[1]], m.PB[:, buf, r[0]:r[1]], ACT.Exp, bias=st[:, 4 + i:5 + i], scale=scale,
                accum_out=st[:, 6 + i:7 + i]), t) for i, r in enumerate(rngs)]
            t = dve.do(lambda e: e.reciprocal(st[:, 8:10], st[:, 6:8]), ex)
            probs[h] = [dve.do(lambda e: e.tensor_scalar(
                m.PB[:, buf, r[0]:r[1]], m.PB[:, buf, r[0]:r[1]], st[:, 8 + i:9 + i], None, ALU.mult), t)
                for i, r in enumerate(rngs)]

        got = {}

        def turn(h):
            buf = h % 2
            got[h] = []
            for g in range(3):
                b, acc = bank()
                for o, at in ((0, 768 + g * P), (P, g * 256), (2 * P, g * 256 + P)):
                    tok = pe.do(lambda e: e.transpose(acc[:, o:o + P], m.PB[:, buf, at:at + P], ident), probs[h])
                if g == 0:
                    t = dve.do(lambda e: e.tensor_copy(m.PT1[:, buf, g, :], acc[:, 0:384]), tok, pt_free[buf])
                else:
                    t = act.do(lambda e: e.activation(m.PT1[:, buf, g, :], acc[:, 0:384], ACT.Copy), tok,
                               pt_free[buf])
                bank_free[b] = t
                got[h].append(t)
            pb_free[buf] = tok

        def mix(h):
            hh = h % 2
            buf = h % 2
            b, acc = bank()
            plan = [(0, 0), (0, 1), (1, 1), (2, 1), (1, 0), (2, 0)]
            for i, (g, kt) in enumerate(plan):
                out = acc[:, 0:S] if kt == 0 else acc[:, P:S]
                prob = m.PT1[:, buf, g, 0:256] if kt == 0 else m.PT1[:, buf, g, 256:384]
                tok = pe.do(lambda e: e.matmul(out, m.V1[:, pbuf, kt, g, hh * P:(hh + 1) * P], prob, start=i == 0,
                                               stop=i == len(plan) - 1, skip_group_check=True), got[h], v_tok)
            pt_free[buf] = tok
            otoks[h] = halves(m.XN[:, 0, h, S:512], m.XN[:, 1, h, S:512], acc[:, 0:S], tok)
            bank_free[b] = otoks[h]
            qk_free[pbuf] = tok

        h0, h1 = 2 * pair, 2 * pair + 1
        for f, h, idle in ((scores, h0, 1), (scores, h1, 1), (turn, h0, 0), (mix, h0, 0), (turn, h1, 1),
                           (mix, h1, 0)):
            f(h)
            for _ in range(1 + idle):
                yield True

    for pair in range(4):
        pbuf = pair % 2
        note("pair%d" % pair)
        qk_tok, v_tok = [], []
        for g in range(3):
            for which in range(2):
                col = ((g * 3 + which) * 8 + pair * 2) * P
                dst = m.QK[:, pbuf, g, which, :, :]
                got = []

                def evac(t, acc, tok):
                    r = act.do(lambda e: e.activation(dst[:, t, :], acc, ACT.Copy), tok, qk_free[pbuf])
                    got.append(r)
                    return r

                linear(w, 0, KT, col, 256, xhi, xlo, xt, evac, outer=pair + g + which == 0)

                def rotate(dst=dst, got=got, qk_tok=qk_tok):
                    b, acc = bank()
                    buf = nrt[0] % 2
                    nrt[0] += 1
                    tok = pe.do(lambda e: e.matmul(acc[0:32, :], cst("rot", 32), dst[0:32, :, :],
                                                   start=True, stop=True), got, consts)
                    cos = m.rope[:, 0, :].unsqueeze(1).broadcast_to([32, 2, S])
                    sin = m.rope[:, 1, :].unsqueeze(1).broadcast_to([32, 2, S])
                    rt = m.RT[:, buf, :].rearrange("p (h t) -> p h t", h=2)
                    t1 = dve.do(lambda e: e.tensor_tensor(
                        rt, acc[0:32, :].rearrange("p (h t) -> p h t", h=2), sin, ALU.mult), tok, rope_tok)
                    bank_free[b] = t1
                    t2 = dve.do(lambda e: e.tensor_tensor(dst[0:32, :, :], dst[0:32, :, :], cos, ALU.mult),
                                tok, got)
                    qk_tok.append(dve.do(lambda e: e.tensor_tensor(dst[0:32, :, :], dst[0:32, :, :], rt,
                                                                   ALU.add), t1, t2))

                pend.append(rotate)
            col = ((g * 3 + 2) * 8 + pair * 2) * P

            def evac(t, acc, tok):
                r = act.do(lambda e: e.activation(m.V1[:, pbuf, t, g, :], acc, ACT.Copy), tok, qk_free[pbuf])
                v_tok.append(r)
                return r

            linear_tok(w, col, 256, 2, xt, evac)
        flush()
        assert not background
        background.append(attend1(pair, qk_tok, v_tok))
    note("attn last")
    drain(5)

    def grow(xh, xl, xtok, n, gate, wsrc, outer=False):
        for c in range(4):
            def evac(t, acc, tok):
                return residual(c * 2 + t, n, gate, acc, tok, True)
            linear(wsrc, 0, KT, c * 256, 256, xh, xl, xtok, evac, outer=outer and c == 0)

    note("attn out")
    mh, ml = xn(S, 512)
    grow(mh, ml, otoks, S, None, T["attn_w_out"][0])

    def swiglu(layer):
        note("ffn")
        xt = norm(S, lambda k, s: pv("ffn_norm", k, layer), fillers=3)
        if layer == 1:
            pool.dma(m.cin[:, :, :], T["ctx_2"][0].rearrange("(t p) d -> p t d", p=P), m.sem["ci"], xt)
        xhi, xlo = xn(0, S)
        w = T["ffn_w_in"][layer]
        wo = T["ffn_w_out"][layer]
        htok = [None] * 22
        note("ffn in")
        sg_free = [None] * 2
        sg_tok = {}
        for j in range(11):
            def evac_g(t, acc, tok):
                r = act.do(lambda e: e.activation(m.SG[:, j % 2, t, :], acc, ACT.Silu), tok, sg_free[j % 2])
                sg_tok[t] = r
                return r

            def evac_u(t, acc, tok):
                buf = j % 2
                r = dve.do(lambda e: e.tensor_tensor(m.SG[:, buf, t, :], acc, m.SG[:, buf, t, :], ALU.mult),
                           tok, sg_tok[t])
                i = 2 * j + t
                htok[i] = halves(m.HF[:, 0, i, :], m.HF[:, 1, i, :], m.SG[:, buf, t, :], r)
                if t == 1:
                    sg_free[buf] = [htok[i - 1], htok[i]]
                return r

            linear(w, 0, KT, j * 256, 256, xhi, xlo, xt, evac_g, outer=j == 0)
            linear(w, 0, KT, DFF + j * 256, 256, xhi, xlo, xt, evac_u)
            if j % 2:
                mod_unit()
            if layer == 1 and j == 4:
                background.append(enter_ctx())
        note("ffn out")
        for c in range(4):
            banks = [bank(), bank()]
            for part, (k0, kt) in enumerate(((0, 8), (8, 8), (16, 6))):
                j, hi, lo = take(weight(wo, k0 * P, kt, c * 256, 256), kt, 256)
                for t in range(2):
                    acc = banks[t][1][:, 0:S]
                    for k in range(kt):
                        kk = k0 + k
                        pe.wait([htok[kk]])
                        ready(j, k, kt)
                        tok = mm3(acc, hi[:, k, t * P:(t + 1) * P], lo[:, k, t * P:(t + 1) * P],
                                  m.HF[:, 0, kk, :], m.HF[:, 1, kk, :], kk == 0, kk == 21, k == kt - 1)
                    if kk == 21:
                        if t == 0:
                            flush()
                        bank_free[banks[t][0]] = residual(c * 2 + t, S, None, acc, tok, True)
                used(j, tok)

    def enter_ctx():
        for j in range(KT):
            b, acc = bank()
            for t in range(2):
                tok = pe.do(lambda e: e.transpose(acc[:, t * P:(t + 1) * P], m.cin[:, t, j * P:(j + 1) * P], ident),
                            c_in, consts)
            bank_free[b] = dve.do(lambda e: e.tensor_copy(m.X[:, j, S:512], acc[:, 0:S]), tok)
            yield True

    swiglu(0)

    note("mlstm")
    xt = norm(S, lambda k, s: pv("mlstm_norm", k), fillers=3)
    xhi, xlo = xn(0, S)
    w = T["mlstm_w_in"][0]
    pads = pool.do(lambda e: e.memset(m.CB[:, :, 0:3], 0.0), xt)
    one8 = pool.do(lambda e: e.memset(m.G8[:, 7, :], 1.0), xt)
    vone = pool.do(lambda e: e.memset(m.VM[:, :, :, P:P + 1], 1.0), xt)
    j, hi, lo = take(weight(w, 0, KT, 3072, 16), KT, 16)
    gbanks = []
    for i in range(2):
        b, acc = bank()
        for k in range(KT):
            pe.wait([xt[k]])
            ready(j, k, KT)
            tok = mm3(acc[0:8, 0:S], hi[:, k, i * 8:i * 8 + 8], lo[:, k, i * 8:i * 8 + 8], xhi(k), xlo(k),
                      k == 0, k == KT - 1)
        gbanks.append((b, acc, tok))
    used(j, tok)
    G = m.G8
    z = dve.do(lambda e: e.tensor_scalar(G[:, 0, :], gbanks[1][1][0:8, 0:S], m.gb[:, 1:2], None, ALU.add),
               gbanks[1][2], loaded, xt[KT - 1])
    bank_free[gbanks[1][0]] = z
    az = dve.do(lambda e: e.scalar_tensor_tensor(out=G[:, 1, :], in0=G[:, 0, :], scalar=-1.0,
                                                 in1=G[:, 0, :], op0=ALU.mult, op1=ALU.max), z)
    t = act.do(lambda e: e.activation(G[:, 1, :], G[:, 1, :], ACT.Exp, scale=-1.0), az)
    t = act.do(lambda e: e.activation(G[:, 1, :], G[:, 1, :], ACT.Ln, bias=ones[0:8, 0:1]), t)
    t = dve.do(lambda e: e.scalar_tensor_tensor(out=G[:, 0, :], in0=G[:, 0, :], scalar=0.0,
                                                in1=G[:, 1, :], op0=ALU.min, op1=ALU.subtract), t)
    Bt = dve.do(lambda e: e.tensor_tensor_scan(G[:, 2, :], G[:, 7, :], G[:, 0, :], 0.0,
                                               ALU.mult, ALU.add), t, one8)
    At = dve.do(lambda e: e.scalar_tensor_tensor(out=G[:, 3, :], in0=gbanks[0][1][0:8, 0:S],
                                                 scalar=m.gb[:, 0:1], in1=G[:, 2, :],
                                                 op0=ALU.add, op1=ALU.subtract), Bt, gbanks[0][2])
    bank_free[gbanks[0][0]] = At
    Mt = dve.do(lambda e: e.tensor_tensor_scan(G[:, 4, :], G[:, 3, :], G[:, 3, :], 0.0,
                                               ALU.max, ALU.max), At)
    NMt = dve.do(lambda e: e.tensor_scalar(G[:, 5, :], G[:, 4, :], -1.0, None, ALU.mult), Mt)
    EMt = dve.do(lambda e: e.scalar_tensor_tensor(out=G[:, 6, :], in0=G[:, 2, :], scalar=-1.0,
                                                  in1=G[:, 4, :], op0=ALU.mult, op1=ALU.subtract), Mt)

    ac_tok = []

    def columns():
        b, acc = bank()
        for w8, row in enumerate((3, 6)):
            for i in range(2):
                o = w8 * 16 + i * 8
                tok = pe.do(lambda e: e.transpose(acc[:, o:o + 8], G[:, row, i * P:(i + 1) * P], ident[0:8, 0:8]),
                            At, EMt, consts)
        t = dve.do(lambda e: e.tensor_copy(m.AC[:, 0, :, :], acc[:, 0:16].rearrange("p (i h) -> p i h", i=2)), tok)
        t2 = act.do(lambda e: e.activation(m.AC[:, 1, :, :], acc[:, 16:32].rearrange("p (i h) -> p i h", i=2),
                                           ACT.Exp), tok, t)
        bank_free[b] = [t, t2]
        ac_tok.extend([t, t2])

    qk_done = [None] * KT
    v_tok = []
    so_tok = [None] * KT
    mmask = cst("mmask")
    wt_free = [None, None]
    ht_free = [None, None]

    def cells():
        hot = {}

        def weights(h):
            buf = h % 2
            WT = m.WT[:, buf, :]
            b, acc = bank()
            tok = pe.do(lambda e: e.matmul(acc[:, 0:S], m.cst[0:8, h:h + 1].broadcast_to([8, P]), G[:, 5, :],
                                           start=True, stop=True), NMt, consts)
            t1 = dve.do(lambda e: e.tensor_tensor(WT[:, 0:S], acc[:, 0:S], mmask[:, 0:S], ALU.add), tok, wt_free[buf])
            t2 = dve.do(lambda e: e.tensor_tensor(WT[:, S:384], acc[:, P:S], mmask[:, S:384], ALU.add),
                        tok, wt_free[buf])
            bank_free[b] = [t1, t2]
            e2 = act.do(lambda e: e.activation(WT[:, 0:S], WT[:, 0:S], ACT.Exp, bias=m.AC[:, 0, 0, h:h + 1]),
                        t1, ac_tok)
            e3 = act.do(lambda e: e.activation(WT[:, S:384], WT[:, S:384], ACT.Exp, bias=m.AC[:, 0, 1, h:h + 1]), t2)
            o = 64 * (h % 2)
            Q = m.QKM[o:o + 64, h // 2, :]
            K = m.QKM[o:o + 64, 4 + h // 2, :]
            b, acc = bank()
            pe.go(lambda e: e.matmul(acc[:, 0:S], K[:, 0:P], Q, start=True, stop=True),
                  qk_done[h // 2], qk_done[4 + h // 2])
            tok = pe.do(lambda e: e.matmul(acc[:, S:384], K[:, P:S], Q[:, P:S], start=True, stop=True))
            t = dve.do(lambda e: e.scalar_tensor_tensor(out=WT, in0=acc[:, 0:384], scalar=0.125, in1=WT,
                                                        op0=ALU.mult, op1=ALU.mult), tok, e2, e3)
            bank_free[b] = t
            hot[h] = t

        def cell(h):
            buf = h % 2
            WT = m.WT[:, buf, :]
            b, acc = bank()
            V = m.VM[:, :, h, :]
            pe.go(lambda e: e.matmul(acc[:, 0:129], WT[:, 0:P], V[:, 0, :], start=True, stop=True),
                  hot[h], v_tok, vone)
            pe.go(lambda e: e.matmul(acc[:, 256:385], WT[:, P:S], V[:, 0, :], start=True, stop=False))
            tok = pe.do(lambda e: e.matmul(acc[:, 256:385], WT[:, S:384], V[:, 1, :], start=False, stop=True))
            wt_free[buf] = tok
            num = acc.rearrange("p (i v) -> p i v", i=2)
            st = m.stat[:, 32 + buf * 16:48 + buf * 16]
            t = act.do(lambda e: e.activation(st[:, 0:2], num[:, :, P:P + 1].rearrange("p i v -> p (i v)"), ACT.Abs),
                       tok)
            t = dve.do(lambda e: e.tensor_tensor(st[:, 2:4], st[:, 0:2], m.AC[:, 1, :, h], ALU.max), t, ac_tok)
            t = dve.do(lambda e: e.reciprocal(st[:, 4:6], st[:, 2:4]), t)
            sq = [act.do(lambda e: e.activation(m.HT[:, buf, i, :], num[:, i, 0:P], ACT.Square,
                                                scale=st[:, 4 + i:5 + i], accum_out=st[:, 6 + i:7 + i]),
                         t, ht_free[buf]) for i in range(2)]
            t2 = act.do(lambda e: e.activation(st[:, 8:10], st[:, 6:8], ACT.Ln, bias=m.eps[:, 0:1], scale=1.0 / P),
                        sq, eps_tok)
            t2 = act.do(lambda e: e.activation(st[:, 8:10], st[:, 8:10], ACT.Exp, scale=-0.5), t2)
            t = dve.do(lambda e: e.tensor_tensor(st[:, 10:12], st[:, 8:10], st[:, 4:6], ALU.mult), t2)
            last = [act.do(lambda e: e.activation(m.HT[:, buf, i, :], num[:, i, 0:P], ACT.Copy,
                                                  scale=st[:, 10 + i:11 + i]), t, sq) for i in range(2)]
            bank_free[b] = last
            hot[h] = last

        def close(h):
            buf = h % 2
            b, acc = bank()
            for i in range(2):
                tok = pe.do(lambda e: e.transpose(acc[:, i * P:(i + 1) * P], m.HT[:, buf, i, :], ident), hot[h])
            ht_free[buf] = tok
            r = dve.do(lambda e: e.scalar_tensor_tensor(out=m.HS[:, buf, :], in0=acc[:, 0:S],
                                                        scalar=pv("mlstm_head_gain", h), in1=m.SO[:, h, :],
                                                        op0=ALU.mult, op1=ALU.mult), tok, so_tok[h], hs_free[buf])
            bank_free[b] = r
            otoks[h] = hs_free[buf] = halves(m.XN[:, 0, h, S:512], m.XN[:, 1, h, S:512], m.HS[:, buf, :], r)

        def has(h):
            return qk_done[h // 2] is not None and qk_done[4 + h // 2] is not None

        weights(0)
        yield True
        for h in range(8):
            while h + 1 < 8 and not has(h + 1):
                yield True
            if h + 1 < 8:
                weights(h + 1)
            yield True
            cell(h)
            yield True
            while h and so_tok[h - 1] is None:
                yield True
            if h:
                close(h - 1)
                yield True
        while so_tok[7] is None:
            yield True
        close(7)

    hs_free = [None, None]

    def convolved(c):
        got = {}

        def evac(t, acc, tok):
            r = act.do(lambda e: e.activation(m.CB[:, 2 * c + t, 3:3 + S], acc, ACT.Copy), tok)
            got[t] = r
            return r

        linear(w, 0, KT, c * 256, 256, xhi, xlo, xt, evac, adv=2)
        for t in range(2):
            k = 2 * c + t
            r = dve.do(lambda e: e.tensor_scalar(m.QKM[:, k, :], m.CB[:, k, 0:S], pv("mlstm_conv_w", k, 0),
                                                 pv("mlstm_conv_b", k), ALU.mult, ALU.add), got[t], pads)
            for i in range(1, 4):
                r = dve.do(lambda e: e.scalar_tensor_tensor(
                    out=m.QKM[:, k, :], in0=m.CB[:, k, i:i + S], scalar=pv("mlstm_conv_w", k, i),
                    in1=m.QKM[:, k, :], op0=ALU.mult, op1=ALU.add), r)
            qk_done[k] = act.do(lambda e: e.activation(m.QKM[:, k, :], m.QKM[:, k, :], ACT.Silu), r)

    for c in range(4):
        def evac(t, acc, tok):
            r = act.do(lambda e: e.activation(m.VM[:, t, 2 * c:2 * c + 2, 0:P],
                                              acc.rearrange("p (h v) -> p h v", h=2), ACT.Copy), tok)
            v_tok.append(r)
            return r

        linear_tok(w, 1024 + c * 256, 256, 2, xt, evac)
        if c == 0:
            columns()
    convolved(0)
    convolved(2)
    convolved(1)
    background.append(cells())
    convolved(3)
    for c in range(4):
        def evac(t, acc, tok):
            r = act.do(lambda e: e.activation(m.SO[:, 2 * c + t, :], acc, ACT.Sigmoid), tok)
            so_tok[2 * c + t] = r
            return r

        linear(w, 0, KT, 2048 + c * 256, 256, xhi, xlo, xt, evac, adv=2)
    flush()
    note("mlstm cell")
    drain(8)
    note("mlstm out")
    grow(mh, ml, otoks, S, None, T["mlstm_w_out"][0])
    swiglu(1)
    fill(48 - mod_next[0])

    note("between")
    flush()
    r = rstd(S, D, m.RS[:, 0:S])
    for k in range(KT):
        t = dve.do(lambda e: e.scalar_tensor_tensor(out=m.X[:, k, 0:S], in0=m.X[:, k, 0:S],
                                                    scalar=pv("final_norm", k), in1=m.RS[:, 0:S],
                                                    op0=ALU.mult, op1=ALU.mult), r)
        sumsq(m.X[:, k, :], k, 512, t)
    rs_free[0] = t

    def neighbourhood(layer, slot, ctx_out):
        n = 512 if ctx_out else S
        note("na norm")
        xt = norm(512, lambda k, s: m.gs[:, layer, 0, k, s:s + 1], modcol(layer, 0))
        w = T["na_wqkv_2"][slot]
        start = xt[KT - 1]
        tbs = [m.sem["tb0"], m.sem["tb1"]]
        tb_tok = [None] * 16
        tb_free = [None, None]
        nmask = cst("nmask").unsqueeze(1).broadcast_to([P, 4, 64])
        zero = pool.do(lambda e: e.memset(m.TB[:, :, :, S:512], 0.0), xt)

        def table(i):
            pair, qb = i // 2, i % 2
            buf = i % 2
            rpb = T["na_rpb_2"]
            for hh in range(2):
                h = pair * 2 + hh
                for rr in range(2):
                    base = slot * 7440 + h * 465 + (rr + 6 - 2 * qb) * 31 - 48
                    src = bass.AP(tensor=rpb.tensor, offset=base, ap=[[1, 64], [31, 4], [1, 64]])
                    dst = m.TB[rr * 64:rr * 64 + 64, buf, hh, 0:S].rearrange("p (a c) -> p a c", a=4)
                    pool.dma(dst, src, tbs[buf], start, tb_free[buf])
                    tb_count[buf] += 16
            got = []
            for hh in range(2):
                v = m.TB[:, buf, hh, 0:S].rearrange("p (a c) -> p a c", c=64)
                got.append(pool.do(lambda e: e.tensor_tensor(v, v, nmask, ALU.add),
                                   (tbs[buf], tb_count[buf]), consts))
            tb_tok[i] = got

        table(0)
        table(1)
        pb_free = [None, None]
        pt_free = [None]
        npb = [0]
        in_free = [None, None]
        otok = [[] for _ in range(KT)]

        def attend(group, qt, kt_, vt):
            gb = group % 2

            def softmax(buf, width, toks, st, pieces):
                ex = []
                for hh in range(2):
                    for i in range(pieces):
                        c = hh * pieces + i
                        v = m.PB2[:, buf, hh, i * width:(i + 1) * width]
                        ex.append((v, act.do(lambda e: e.activation(
                            v, toks[hh][1][:, i * width:(i + 1) * width], ACT.Exp, bias=st[:, c:c + 1],
                            accum_out=st[:, 4 + c:5 + c]), toks[hh][0], pb_free[buf]), c))
                n = 2 * pieces
                t = dve.do(lambda e: e.reciprocal(st[:, 8:8 + n], st[:, 4:4 + n]), [x[1] for x in ex])
                return [dve.do(lambda e: e.tensor_scalar(v, v, st[:, 8 + c:9 + c], None, ALU.mult), t)
                        for v, _, c in ex], [x[1] for x in ex]

            def lat_scores(p, qb):
                buf = npb[0] % 2
                npb[0] += 1
                i = (group * 2 + p) * 2 + qb
                st = m.stat[:, buf * 16:buf * 16 + 16]
                banks = [bank(), bank()]
                maxed = []
                for hh in range(2):
                    o = 64 * hh
                    acc = banks[hh][1]
                    tok = pe.do(lambda e: e.matmul(acc[:, :], m.QB[o:o + 64, gb, p, qb * P:(qb + 1) * P],
                                                   m.KB[o:o + 64, gb, p, :], start=True, stop=True), qt, kt_)
                    t = dve.do(lambda e: e.tensor_tensor_reduce(
                        out=m.PB2[:, buf, hh, :], in0=acc[:, :], in1=m.TB[:, qb, hh, :], scale=1.0, scalar=-3.0e38,
                        op0=ALU.add, op1=ALU.max, accum_out=st[:, 12 + hh:13 + hh]),
                        tok, tb_tok[i], zero, pb_free[buf])
                    bank_free[banks[hh][0]] = t
                    maxed.append(t)
                tb_free[qb] = maxed
                if i + 2 < 16:
                    table(i + 2)
                t = dve.do(lambda e: e.tensor_scalar(st[:, 0:2], st[:, 12:14], -1.0, None, ALU.mult), maxed)
                return buf, softmax(buf, 512, [(t, m.PB2[:, buf, hh, :]) for hh in range(2)], st, 1)[0]

            def ctx_scores(p):
                buf = npb[0] % 2
                npb[0] += 1
                st = m.stat[:, buf * 16:buf * 16 + 16]
                banks = [bank(), bank()]
                for qb in range(2):
                    for hh in range(2):
                        o = 64 * hh
                        acc = banks[hh][1]
                        tok = pe.do(lambda e: e.matmul(
                            acc[:, qb * S:(qb + 1) * S], m.QB[o:o + 64, gb, p, S + qb * P:S + (qb + 1) * P],
                            m.KB[o:o + 64, gb, p, S:512], start=True, stop=True), qt, kt_)
                ts = []
                for hh in range(2):
                    v = banks[hh][1].rearrange("p (i k) -> p i k", i=2)
                    ts.append(dve.do(lambda e: e.tensor_reduce(st[:, 2 * hh:2 * hh + 2], v, AX.X, ALU.max,
                                                               negate=True), tok, pb_free[buf]))
                done, ex = softmax(buf, S, [(ts[hh], banks[hh][1]) for hh in range(2)], st, 2)
                for hh in range(2):
                    bank_free[banks[hh][0]] = ex
                return buf, done

            def turn(buf, ready_, blocks, where):
                got = []
                for hh in range(2):
                    b, acc = bank()
                    for i, (col, kt, q) in enumerate(blocks):
                        tok = pe.do(lambda e: e.transpose(acc[:, i * P:(i + 1) * P],
                                                          m.PB2[:, buf, hh, col:col + P], ident), ready_)
                    dst = where(hh)
                    src = acc[:, :].rearrange("p (k q) -> p k q", q=P)[:, :, ::-1]
                    dst = dst.rearrange("p k (b q) -> p (k b) q", q=P) if dst.shape[2] > P else dst
                    if hh == 0:
                        c = act.do(lambda e: e.activation(dst, src, ACT.Copy), tok, pt_free[0])
                    else:
                        c = dve.do(lambda e: e.tensor_copy(dst, src), tok, pt_free[0])
                    bank_free[b] = c
                    got.append(c)
                pb_free[buf] = tok
                return got

            def mix(p, got, k0, nk, at):
                tile = group * 2 + p
                b, acc = bank()
                for kt in range(nk):
                    for hh in range(2):
                        o = 64 * hh
                        c = (2 * p + hh) * 64
                        tok = pe.do(lambda e: e.matmul(acc[o:o + 64, 0:S], m.VB[:, gb, k0 + kt, c:c + 64],
                                                       m.PT2[:, hh, kt, :], start=kt == 0, stop=kt == nk - 1),
                                    got, vt)
                pt_free[0] = tok
                r = halves(m.OB[:, 0, tile, at:at + S], m.OB[:, 1, tile, at:at + S], acc[:, 0:S], tok)
                bank_free[b] = r
                otok[tile].append(r)
                in_free[gb] = tok

            def lat_turn(s, qb):
                return turn(s[0], s[1], [(kt * P, kt, qb) for kt in range(4)],
                            lambda hh: m.PT2[:, hh, :, qb * P:(qb + 1) * P])

            def ctx_turn(s):
                return turn(s[0], s[1], [(qb * S + kt * P, kt, qb) for kt in range(2) for qb in range(2)],
                            lambda hh: m.PT2[:, hh, 0:2, :])

            s0 = lat_scores(0, 0)
            yield True
            for p in range(2):
                s1 = lat_scores(p, 1)
                yield True
                got = lat_turn(s0, 0)
                yield True
                if ctx_out:
                    sc = ctx_scores(p)
                    yield True
                got = got + lat_turn(s1, 1)
                yield True
                if p == 0:
                    s0 = lat_scores(1, 0)
                    yield True
                mix(p, got, 0, 4, 0)
                yield True
                if ctx_out:
                    got = ctx_turn(sc)
                    yield True
                    mix(p, got, 2, 2, S)
                    yield True

        note("na qkv")
        for group in range(4):
            gb = group % 2
            qt, kt_, vt = [], [], []

            def evac_q(t, acc, tok):
                r = act.do(lambda e: e.activation(m.QB[:, gb, t, 0:n].rearrange("p (b q) -> p b q", q=P),
                                                  acc.rearrange("p (b q) -> p b q", q=P)[:, :, ::-1], ACT.Copy,
                                                  scale=0.125), tok, in_free[gb])
                qt.append(r)
                return r

            def evac_k(t, acc, tok):
                r = act.do(lambda e: e.activation(m.KB[:, gb, t, :], acc, ACT.Copy), tok, in_free[gb])
                kt_.append(r)
                return r

            def evac_v(t, acc, tok):
                r = act.do(lambda e: e.activation(m.VB[:, gb, t, :], acc, ACT.Copy), tok, in_free[gb])
                vt.append(r)
                return r

            xh, xl = xn(0, n)
            linear(w, 0, KT, group * 256, 256, xh, xl, xt, evac_q, adv=2, outer=group == 0)
            xh, xl = xn(0, 512)
            linear(w, 0, KT, 1024 + group * 256, 256, xh, xl, xt, evac_k, adv=2)
            linear_tok(w, 2048 + group * 256, 256, 4, xt, evac_v, adv=2)
            flush()
            drain()
            background.append(attend(group, qt, kt_, vt))
        note("na attn")
        drain(8 if layer == 0 else 0)
        note("na out")
        grow(lambda k: m.OB[:, 0, k, 0:n], lambda k: m.OB[:, 1, k, 0:n], otok, n, modcol(layer, 2),
             T["na_wo_2"][slot])

    tb_count = [0, 0]

    def conformer(layer):
        note("cv norm")
        xt = norm(512, lambda k, s: m.gs[:, layer, 0, k, s:s + 1], modcol(layer, 0))
        xh, xl = xn(0, 512)
        w = T["cv_w1_2"][0]
        note("cv w1")
        pads = [pool.do(lambda e, a=a: e.memset(m.U[:, :, :, a:a + 15], 0.0), xt[KT - 1]) for a in (0, 271)]
        ab_free = [None, None]
        cv_tok = [None] * KT
        ut = {}

        def convolve(c):
            for t in range(2):
                k = 2 * c + t
                out = m.CV[:, k, :].rearrange("p (s t) -> p s t", s=2)
                r = dve.do(lambda e: e.tensor_scalar(out, m.U[:, k, :, 0:S], pv("cv_dw_2", k, 0),
                                                     pv("cv_dwb_2", k), ALU.mult, ALU.add), ut[k], pads)
                for i in range(1, 31):
                    r = dve.do(lambda e, i=i: e.scalar_tensor_tensor(
                        out=out, in0=m.U[:, k, :, i:i + S], scalar=pv("cv_dw_2", k, i), in1=out,
                        op0=ALU.mult, op1=ALU.add), r)
                cv_tok[k] = r
                total(m.CV[:, k, :], k, 512, r)

        for c in range(4):
            at = {}

            def evac_a(t, acc, tok):
                at[t] = act.do(lambda e: e.activation(m.AB[:, c % 2, t, :], acc, ACT.Identity,
                                                      bias=pv("cv_b1_2", 2 * c + t, 0)), tok, ab_free[c % 2])
                return at[t]

            def evac_g(t, acc, tok):
                k = 2 * c + t
                r = act.do(lambda e: e.activation(m.SGM[:, t, :], acc, ACT.Sigmoid,
                                                  bias=pv("cv_b1_2", k, 1)), tok, sg_free[t])
                u = dve.do(lambda e: e.tensor_tensor(
                    m.U[:, k, :, 15:271], m.AB[:, c % 2, t, :].rearrange("p (s t) -> p s t", s=2),
                    m.SGM[:, t, :].rearrange("p (s t) -> p s t", s=2), ALU.mult), r, at[t], pads)
                sg_free[t] = u
                if t == 1:
                    ab_free[c % 2] = u
                ut[k] = u
                return r

            if c == 0:
                sg_free = [None, None]
            linear(w, 0, KT, c * 256, 256, xh, xl, xt, evac_a, outer=c == 0)
            linear(w, 0, KT, 1024 + c * 256, 256, xh, xl, xt, evac_g)
            if c:
                convolve(c - 1)
            fill(12)
        convolve(3)
        fill(96 - mod_next[0])
        flush()
        note("cv ln")
        r = act.do(lambda e: e.activation(m.RS[:, :], ps[6][:, :], ACT.Copy, scale=-1.0 / D), stat["tok"], rs_free[0])
        bank_free[6] = r
        for k in range(KT):
            cv_tok[k] = dve.do(lambda e: e.tensor_tensor(m.CV[:, k, :], m.CV[:, k, :], m.RS[:, :], ALU.add), r, cv_tok[k])
            sumsq(m.CV[:, k, :], k, 512, cv_tok[k])
        flush()
        rs_free[0] = cv_tok[KT - 1]
        r = rstd(512, D, m.RS[:, :])
        free = (m.sem["pe"], pe.n)
        toks = []
        for k in range(KT):
            t = dve.do(lambda e: e.scalar_tensor_tensor(out=m.CV[:, k, :], in0=m.CV[:, k, :], scalar=pv("cv_ln_g_2", k),
                                                        in1=m.RS[:, :], op0=ALU.mult, op1=ALU.mult), r, cv_tok[k])
            t = act.do(lambda e: e.activation(m.CV[:, k, :], m.CV[:, k, :], ACT.Silu, bias=pv("cv_ln_b_2", k)), t)
            toks.append(halves(m.XN[:, 0, k, :], m.XN[:, 1, k, :], m.CV[:, k, :], t, free))
        rs_free[0] = toks[-1]
        gate = modcol(layer, 2)
        w2 = T["cv_w2_2"][0]
        note("cv w2")
        for c in range(4):
            def evac(t, acc, tok):
                j = 2 * c + t
                buf = t
                y = act.do(lambda e: e.activation(m.AB[:, 0, buf, :], acc, ACT.Identity, bias=pv("cv_b2_2", j)),
                           tok, ab2_free[buf])
                ab2_free[buf] = residual(j, 512, gate, m.AB[:, 0, buf, :], y, True)
                return y
            if c == 0:
                ab2_free = [None, None]
            linear(w2, 0, KT, c * 256, 256, xh, xl, toks, evac, outer=c == 0)

    def shortconv(layer):
        note("sc norm")
        xt = norm(512, lambda k, s: m.gs[:, layer, 0, k, s:s + 1], modcol(layer, 0))
        xh, xl = xn(0, 512)
        w = T["sc_win_2"][0]
        note("sc in")
        pads = [pool.do(lambda e, a=a: e.memset(m.UP[:, :, :, :, a:a + 1], 0.0), xt[KT - 1]) for a in (0, 257)]
        y = [None] * KT
        cgt, uft, cot = {}, {}, {}
        cg_free = [None, None]
        up_free = [None, None]
        co_free = [None, None]
        for c in range(4):
            buf = c % 2

            def evac_c(t, acc, tok):
                cgt[t] = act.do(lambda e: e.activation(m.CG[:, buf, t, :], acc, ACT.Copy), tok, cg_free[buf])
                return cgt[t]

            def evac_v(t, acc, tok):
                uft[t] = dve.do(lambda e: e.tensor_tensor(
                    m.UP[:, buf, t, :, 1:257], acc.rearrange("p (s t) -> p s t", s=2),
                    m.CG[:, buf, t, :].rearrange("p (s t) -> p s t", s=2), ALU.mult), tok, cgt[t], up_free[buf])
                if t == 1:
                    cg_free[buf] = uft[1]
                return uft[t]

            def evac_b(t, acc, tok):
                k = 2 * c + t
                r = dve.do(lambda e: e.tensor_tensor(m.CO[:, buf, t, :], acc, m.CO[:, buf, t, :], ALU.mult),
                           tok, cot[t])
                y[k] = (r, buf, t)
                return r

            linear(w, 0, KT, 1024 + c * 256, 256, xh, xl, xt, evac_c, outer=c == 0)
            linear(w, 0, KT, 2048 + c * 256, 256, xh, xl, xt, evac_v)
            for t in range(2):
                k = 2 * c + t
                out = m.CO[:, buf, t, :].rearrange("p (s t) -> p s t", s=2)
                r = dve.do(lambda e: e.tensor_scalar(out, m.UP[:, buf, t, :, 0:S], pv("sc_conv_2", k, 0), None,
                                                     ALU.mult), uft[t], pads, co_free[buf])
                for i in (1, 2):
                    r = dve.do(lambda e, i=i: e.scalar_tensor_tensor(
                        out=out, in0=m.UP[:, buf, t, :, i:i + S], scalar=pv("sc_conv_2", k, i), in1=out,
                        op0=ALU.mult, op1=ALU.add), r)
                cot[t] = r
            up_free[buf] = r
            linear(w, 0, KT, c * 256, 256, xh, xl, xt, evac_b)
            done = []
            for t in range(2):
                k = 2 * c + t
                r = y[k][0]
                y[k] = halves(m.YH[:, 0, k, :], m.YH[:, 1, k, :], m.CO[:, buf, t, :], r)
                done.append(y[k])
            co_free[buf] = done
        note("sc out")
        yh, yl = (lambda k: m.YH[:, 0, k, :]), (lambda k: m.YH[:, 1, k, :])
        grow(yh, yl, y, 512, modcol(layer, 2), T["sc_wout_2"][0])

    def mlp(layer, n):
        note("mlp norm")
        xt = norm(n, lambda k, s: m.gs[:, layer, 1, k, s:s + 1], modcol(layer, 3))
        xh, xl = xn(0, n)
        note("mlp")
        w1, w2 = T["mlp_w1_2"][layer], T["mlp_w2_2"][layer]
        gate = modcol(layer, 5)
        h_free = [None, None]
        htok = {}
        rl_free = [None] * 4
        nrl = [0]

        def up(q):
            buf = q % 2
            toks = [None] * KT
            for c in range(4):
                def evac(t, acc, tok):
                    r = nrl[0] % 4
                    nrl[0] += 1
                    a = act.do(lambda e: e.activation(m.RL[:, r, 0:n], acc, ACT.Relu), tok, rl_free[r])
                    d = dve.do(lambda e: e.tensor_tensor(m.RL[:, r, 0:n], acc, m.RL[:, r, 0:n], ALU.mult), a, tok)
                    k = 2 * c + t
                    toks[k] = halves(m.H2[:, buf, 0, k, 0:n], m.H2[:, buf, 1, k, 0:n], m.RL[:, r, 0:n], d, h_free[buf])
                    rl_free[r] = toks[k]
                    return d
                linear(w1, 0, KT, q * D + c * 256, 256, xh, xl, xt, evac, outer=q + c == 0)
            htok[q] = toks

        def down(q):
            buf = q % 2
            hh, hl = (lambda k: m.H2[:, buf, 0, k, 0:n]), (lambda k: m.H2[:, buf, 1, k, 0:n])
            for c in range(4):
                def evac(t, acc, tok):
                    h_free[buf] = tok
                    return residual(2 * c + t, n, gate, acc, tok, q == 3)
                linear(w2, q * D, KT, c * 256, 256, hh, hl, htok[q], evac)

        up(0)
        for q in range(4):
            if q + 1 < 4:
                up(q + 1)
            down(q)

    neighbourhood(0, 0, True)
    mlp(0, 512)
    conformer(1)
    mlp(1, 512)
    shortconv(2)
    mlp(2, 512)
    neighbourhood(3, 1, False)
    mlp(3, S)

    note("final")
    flush()
    r = rstd(S, D, m.RS[:, 0:S])
    fo = []
    for k in range(KT):
        buf = k % 2
        t = dve.do(lambda e: e.scalar_tensor_tensor(out=m.X[:, k, 0:S], in0=m.X[:, k, 0:S], scalar=pv("final_g_2", k),
                                                    in1=m.RS[:, 0:S], op0=ALU.mult, op1=ALU.mult), r)
        b, acc = bank()
        for i in range(2):
            tok = pe.do(lambda e, i=i: e.transpose(acc[:, i * P:(i + 1) * P], m.X[:, k, i * P:(i + 1) * P], ident), t)
        t = act.do(lambda e: e.activation(m.FO[:, :, k * P:(k + 1) * P],
                                          acc[:, 0:S].rearrange("p (i d) -> p i d", i=2), ACT.Copy), tok)
        bank_free[b] = t
    sp.dma(T["out"][0].rearrange("(t p) d -> p t d", p=P), m.FO[:, :, :], m.sem["out"], t)
    sp.wait([(m.sem["out"], 16)])
    note("end")
    return order, {"marks": marks, "pe": pe, "act": act, "dve": dve, "pool": pool, "sp": sp}


def build(nc, T):
    with ExitStack() as ctx:
        m = allocate(nc, ctx)
        units, _ = program(m, T, None)
        _, q = program(m, T, units)
        block = ctx.enter_context(nc.Block())

        @block.sync
        def _(e):
            for f in q["sp"].ops:
                f(e)

        @block.tensor
        def _(e):
            for f in q["pe"].ops:
                f(e)

        @block.scalar
        def _(e):
            for f in q["act"].ops:
                f(e)

        @block.vector
        def _(e):
            for f in q["dve"].ops:
                f(e)

        @block.gpsimd
        def _(e):
            for f in q["pool"].ops:
                f(e)


_INS = ["x", "positions", "attn_norm", "attn_w_in", "attn_w_out", "mlstm_norm", "mlstm_w_in", "mlstm_conv_w",
        "mlstm_conv_b", "mlstm_ig_bias", "mlstm_fg_bias", "mlstm_head_gain", "mlstm_w_out", "ffn_norm", "ffn_w_in",
        "ffn_w_out", "final_norm", "c_2", "ctx_2", "c_ctx_2", "mod_w_2", "mod_b_2", "norm1_g_2", "norm2_g_2",
        "mlp_w1_2", "mlp_w2_2", "na_wqkv_2", "na_wo_2", "na_rpb_2", "cv_w1_2", "cv_b1_2", "cv_dw_2", "cv_dwb_2",
        "cv_ln_g_2", "cv_ln_b_2", "cv_w2_2", "cv_b2_2", "sc_win_2", "sc_conv_2", "sc_wout_2", "final_g_2"]
_AS_ROWS = {name: k for name, k in ROWS}


def kernel(**inputs):
    import concourse.bacc as _bacc
    from concourse.bass_utils import run_bass_kernel_spmd as _run

    nc = _bacc.Bacc("TRN2", target_bir_lowering=False, num_devices=1)
    arrays, T = {}, {}
    for name in _INS:
        a = np.ascontiguousarray(inputs[name])
        if name in _AS_ROWS:
            a = a.reshape(_AS_ROWS[name], D)
        arrays[f"in_{name}"] = a
        T[name] = nc.dram_tensor(f"in_{name}", a.shape, mybir.dt.from_np(a.dtype), kind="ExternalInput").ap()
    arrays["in_consts"] = constants()
    T["consts"] = nc.dram_tensor("in_consts", arrays["in_consts"].shape, F32, kind="ExternalInput").ap()
    T["out"] = nc.dram_tensor("out_0", (1, S, D), F32, kind="ExternalOutput").ap()
    build(nc, T)
    r = _run(nc, [arrays], core_ids=[0])
    return r.results[0]["out_0"]
```

```python
from contextlib import ExitStack

import numpy as np

import concourse.bass as bass
from concourse import mybir

F32 = mybir.dt.float32
F32R = mybir.dt.float32r
I32 = mybir.dt.int32
ALU = mybir.AluOpType
ACT = mybir.ActivationFunctionType
AX = mybir.AxisListType

P = 128
D = 1024
KT = 8
S = 256
DFF = 2816
DFF2 = 4096
NEG = -1.0e30
ROPE_FREQ = [1.0, 0.44036659598350525, 0.1939227432012558, 0.08539710193872452, 0.03760603070259094,
             0.016560440883040428, 0.007292664609849453, 0.0032114461064338684, 0.0014142135623842478,
             0.0006227724370546639, 0.00027424816832155466, 0.00012076973507646471, 5.3182957344688475e-05,
             2.34199997066753e-05, 1.0313385246263351e-05, 4.541670477919979e-06]
TWO_PI_A = 6.28125
TWO_PI_B = 1.9340515136718750e-03
TWO_PI_C = float(2.0 * np.pi - 6.28125 - 1.9340515136718750e-03)
ROUND = 12582912.0

ROWS = [("attn_norm", 1), ("mlstm_norm", 1), ("mlstm_head_gain", 1), ("ffn_norm", 2), ("final_norm", 1),
        ("mlstm_conv_w", 4), ("mlstm_conv_b", 1), ("norm1_g_2", 4), ("norm2_g_2", 4), ("cv_b1_2", 2),
        ("cv_dw_2", 31), ("cv_dwb_2", 1), ("cv_ln_g_2", 1), ("cv_ln_b_2", 1), ("cv_b2_2", 1),
        ("sc_conv_2", 3), ("final_g_2", 1), ("mod_b_2", 24), ("c_2", 1), ("c_ctx_2", 1)]
ROW = {}
NROW = 0
for _n, _k in ROWS:
    ROW[_n] = NROW
    NROW += _k


def const_layout():
    at, out = 0, {}
    for name, width in (("ident", 128), ("ones", 128), ("nmask", 64), ("fold", 2),
                        ("mmask", 384), ("rot", 32), ("freq", 1), ("amask", 1152)):
        out[name] = (at, width)
        at += width
    return out, at


def constants():
    lay, width = const_layout()
    c = np.zeros((P, width), np.float32)

    def put(name, a):
        a = np.asarray(a, np.float32)
        at = lay[name][0]
        c[:a.shape[0], at:at + a.shape[1]] = a

    fold = np.zeros((P, 2))
    for g in range(4):
        fold[32 * g, 0] = fold[32 * g + 1, 1] = 1.0
    put("fold", fold)
    put("ident", np.eye(P))
    put("ones", np.ones((P, P)))
    t = np.arange(S)
    masks = []
    for r, window in ((1, 128), (4, 128), (16, 128)):
        dist = t[:, None] - t[None, :]
        ok = (dist >= 0) & (dist % r == 0) & (dist // r <= window)
        masks.append(np.where(ok, 0.0, NEG))
    put("amask", np.concatenate([m[128:, :] for m in masks] + [m[:128, :128] for m in masks], axis=1))
    col = np.arange(64)
    start = np.clip(col - 8, 0, 48)
    ok = (col[None, :] >= start[:, None]) & (col[None, :] < start[:, None] + 16)
    nm = np.where(ok, 0.0, NEG)
    put("nmask", np.concatenate([nm, nm])[::-1])
    keep = t[:, None] <= t[None, :]
    mm = np.where(keep, 0.0, NEG)
    put("mmask", np.concatenate([mm[:128, :], mm[128:, 128:]], axis=1))
    rot = np.zeros((32, 32))
    for i in range(16):
        rot[16 + i, i] = -1.0
        rot[i, 16 + i] = 1.0
    put("rot", rot)
    put("freq", np.array(ROPE_FREQ + ROPE_FREQ, np.float32)[:, None])
    return c


class Step:

    def matmul(self, *a, **k):
        self.op = lambda e: e.matmul(*a, **k)

    def transpose(self, *a, **k):
        self.op = lambda e: e.transpose(*a, **k)

    def activation(self, *a, **k):
        self.op = lambda e: e.activation(*a, **k)

    def tensor_copy(self, *a, **k):
        self.op = lambda e: e.tensor_copy(*a, **k)

    def tensor_tensor(self, *a, **k):
        self.op = lambda e: e.tensor_tensor(*a, **k)

    def tensor_scalar(self, *a, **k):
        self.op = lambda e: e.tensor_scalar(*a, **k)

    def scalar_tensor_tensor(self, *a, **k):
        self.op = lambda e: e.scalar_tensor_tensor(*a, **k)

    def tensor_reduce(self, *a, **k):
        self.op = lambda e: e.tensor_reduce(*a, **k)

    def tensor_tensor_reduce(self, *a, **k):
        self.op = lambda e: e.tensor_tensor_reduce(*a, **k)

    def tensor_tensor_scan(self, *a, **k):
        self.op = lambda e: e.tensor_tensor_scan(*a, **k)

    def reciprocal(self, *a, **k):
        self.op = lambda e: e.reciprocal(*a, **k)

    def memset(self, *a, **k):
        self.op = lambda e: e.memset(*a, **k)

    def preload_act_table_set(self, *a, **k):
        self.op = lambda e: e.preload_act_table_set(*a, **k)


def step(fn):
    s = Step()
    fn(s)
    return s.op


class Queue:

    def __init__(self, sem, step=1):
        self.sem, self.n, self.ops, self.seen = sem, 0, [], {}

    def wait(self, deps):
        for d in flat(deps):
            sem, v = d
            if self.seen.get(sem.name, 0) < v:
                self.seen[sem.name] = v
                self.ops.append(lambda e, sem=sem, v=v: e.wait_ge(sem, v))

    def go(self, fn, *deps):
        self.wait(deps)
        self.ops.append(step(fn))

    def do(self, fn, *deps):
        self.wait(deps)
        self.n += 1
        sem, op = self.sem, step(fn)
        self.ops.append(lambda e: op(e).then_inc(sem, 1))
        return (sem, self.n)

    def dma(self, out, in_, sem, *deps):
        self.wait(deps)
        self.ops.append(lambda e: e.dma_start(out, in_).then_inc(sem, 16))


def flat(deps):
    for d in deps:
        if d is None:
            continue
        if isinstance(d, tuple) and len(d) == 2 and isinstance(d[1], int):
            yield d
        else:
            yield from flat(d)


class Memory:
    pass


RAW = 3
HL = 2
NBANK = 6


def allocate(nc, ctx):
    m = Memory()
    lay, width = const_layout()

    def sb(name, shape, dt=F32, stack=ctx):
        return stack.enter_context(nc.sbuf_tensor(name, shape, dt))

    m.width = lay["amask"][0]
    m.cst = sb("cst", [P, m.width])
    m.PV = sb("PV", [P, KT, NROW])
    m.eps = sb("eps", [P, 1])
    m.sc = sb("sc", [P, KT, 32])
    m.mod = sb("mod", [P, 4, 48, 2])
    m.gs = sb("gs", [P, 4, 2, KT, 2])
    m.macc = sb("macc", [P, 512])
    m.gb = sb("gb", [8, 2])
    m.stat = sb("stat", [P, 64])
    m.X = sb("X", [P, KT, 512])
    m.raw = [sb(f"raw{i}", [P, 2048]) for i in range(RAW)]
    m.hi = [sb(f"hi{i}", [P, 2048], F32R) for i in range(HL)]
    m.lo = [sb(f"lo{i}", [P, 2048], F32R) for i in range(HL)]
    m.XN = sb("XN", [P, 2, KT, 512], F32R)
    m.SQ = sb("SQ", [P, 2, 512])
    m.SA = sb("SA", [P, 512])
    m.RS = sb("RS", [P, 512])
    m.TN = sb("TN", [P, 2, 512])

    def phase(*tensors):
        with ExitStack() as st:
            return [sb(n, s, d, st) for n, s, d in tensors]

    m.amask, m.rope, m.QK, m.V1, m.PB, m.PT1, m.RT, m.pos, m.ang = phase(
        ("amask", [P, 1152], F32), ("rope", [32, 2, S], F32),
        ("QK", [P, 2, 3, 2, 2, S], F32), ("V1", [P, 2, 2, 3, 256], F32), ("PB", [P, 2, 1152], F32),
        ("PT1", [P, 2, 3, 384], F32), ("RT", [32, 2, 512], F32),
        ("pos", [32, S], I32), ("ang", [32, 4, S], F32))
    m.HF, m.SG = phase(("HF", [P, 2, 22, S], F32R), ("SG", [P, 2, 2, S], F32))
    m.CB, m.QKM, m.VM, m.SO, m.HS, m.WT, m.G8, m.AC, m.HT, m.SG1 = phase(
        ("CB", [P, KT, 260], F32), ("QKM", [P, KT, S], F32), ("VM", [P, 2, 8, P + 1], F32), ("SO", [P, KT, S], F32),
        ("HS", [P, 2, S], F32), ("WT", [P, 2, 384], F32), ("G8", [8, 8, S], F32),
        ("AC", [P, 2, 2, 8], F32), ("HT", [P, 2, 2, P], F32), ("SG1", [P, 2, S], F32))
    m.QB, m.KB, m.VB, m.OB, m.TB, m.PB2, m.PT2 = phase(
        ("QB", [P, 2, 2, 512], F32), ("KB", [P, 2, 2, 512], F32), ("VB", [P, 2, 4, 256], F32),
        ("OB", [P, 2, KT, 512], F32R), ("TB", [P, 2, 2, 512], F32), ("PB2", [P, 2, 2, 512], F32),
        ("PT2", [P, 2, 4, S], F32))
    m.H2, m.RL = phase(("H2", [P, 2, 2, KT, 512], F32R), ("RL", [P, 4, 512], F32))
    m.U, m.CV, m.AB, m.SGM, m.TAP = phase(
        ("U", [P, KT, 2, 286], F32), ("CV", [P, KT, 512], F32), ("AB", [P, 2, 2, 512], F32),
        ("SGM", [P, 2, 512], F32), ("TAP", [P, 4, 512], F32))
    m.YH, m.CG, m.UP, m.CO = phase(
        ("YH", [P, 2, KT, 512], F32R), ("CG", [P, 2, 2, 512], F32), ("UP", [P, 2, 2, 2, 258], F32),
        ("CO", [P, 2, 2, 512], F32))

    m.ps = [ctx.enter_context(nc.psum_tensor(f"ps{i}", [P, 512], F32)) for i in range(8)]
    m.sem = {n: ctx.enter_context(nc.semaphore(f"s_{n}"))
             for n in ["pe", "act", "dve", "pool", "ld", "x0", "x1", "pv", "ci", "pos", "cst", "tb0", "tb1", "out"]
             + [f"raw{i}" for i in range(RAW)]}
    m.lay = lay
    return m


def program(m, T, units):
    pe, act, dve, pool = (Queue(m.sem[n]) for n in ("pe", "act", "dve", "pool"))
    sp = Queue(None)
    ps = m.ps
    bank_free = [None] * 8
    state = {"bank": 0, "unit": 0, "next": 0, "halved": 0, "last": 0, "pre": 0, "turn": 0,
             "totals": 0, "pace": 0.0, "credit": 0.0}
    order = []
    raw_free = [None] * RAW
    raw_count = [0] * RAW
    raw_known = set()
    hl_free = [None] * HL
    hl_slot = {}
    ready_at = {}
    background = []
    apart = []
    pend = []

    def cst(name, rows=P):
        at, w = m.lay[name]
        assert at < m.width
        return m.cst[0:rows, at:at + w]

    ident, ones = cst("ident"), cst("ones")

    def pv(name, k, i=0):
        r = ROW[name] + i
        return m.PV[:, k, r:r + 1]

    open_banks = set()

    def bank():
        b = state["bank"]
        while b in open_banks:
            b = (b + 1) % NBANK
        state["bank"] = (b + 1) % NBANK
        pe.wait([bank_free[b]])
        return b, ps[b]

    def bring(j, late):
        src, kt, cols, whole = units[j]
        r = j % RAW
        n = kt * cols
        raw_count[r] += 16
        sp.dma(m.raw[r][:, 0:n].rearrange("p (k n) -> p k n", k=kt), src, m.sem[f"raw{r}"], raw_free[r])
        landed = (m.sem[f"raw{r}"], raw_count[r])
        if whole:
            ready_at[j] = [landed]
            return
        h = state["halved"] % HL
        state["halved"] += 1
        hl_slot[j] = h
        raw, hi, lo = m.raw[r], m.hi[h], m.lo[h]
        cuts = [0, (kt + 1) // 2 * cols, n]
        ready_at[j] = []

        def split():
            free = []
            for a, b in zip(cuts, cuts[1:]):
                t = act.do(lambda e: e.activation(hi[:, a:b], raw[:, a:b], ACT.Copy), landed, hl_free[h])
                d = dve.do(lambda e: e.tensor_tensor(lo[:, a:b], raw[:, a:b], hi[:, a:b].bitcast(F32), ALU.subtract),
                           landed, t, hl_free[h])
                ready_at[j].append(d)
                free += [t, d]
            raw_free[r] = free
            raw_known.add(j)

        late.append(split)

    late = []

    def splits():
        while late:
            late.pop(0)()

    def take(src, kt, cols, whole=False):
        if not whole:
            splits()
        j = state["unit"]
        state["unit"] += 1
        order.append((src, kt, cols, whole))
        n = kt * cols
        if units is not None:
            assert units[j][1:] == (kt, cols, whole)
            if not whole:
                state["last"] = j
            held = sum(not units[i][3] for i in range(state["last"], state["next"]))
            while state["next"] < len(units):
                i = state["next"]
                if i > j and (held + (not units[i][3]) > HL or (i >= RAW and i - RAW not in raw_known)):
                    break
                assert i < RAW or i - RAW in raw_known
                bring(i, late)
                if not any(units[x][3] for x in range(j, i)):
                    splits()
                held += not units[i][3]
                state["next"] += 1
        if whole:
            return j, m.raw[j % RAW][:, 0:n].rearrange("p (k n) -> p k n", k=kt)
        h = hl_slot.get(j, 0)
        return j, m.hi[h][:, 0:n].rearrange("p (k n) -> p k n", k=kt), \
            m.lo[h][:, 0:n].rearrange("p (k n) -> p k n", k=kt)

    def ahead_of_all():
        if units is not None:
            bring(0, late)
            splits()
            state["next"] = 1

    def ready(j, k, kt):
        if units is not None:
            pe.wait([ready_at[j][0 if k < (kt + 1) // 2 else -1]])

    def used(j, tok, whole=False):
        if whole:
            raw_free[j % RAW] = tok
            raw_known.add(j)
        else:
            hl_free[hl_slot.get(j, 0)] = tok

    def advance(n=1):
        for _ in range(n):
            state["turn"] += 1
            if apart and state["turn"] % 3 and next(apart[0], None) is None:
                apart.pop(0)
            if background and next(background[0], None) is None:
                background.pop(0)

    def share(k, kt, n):
        return n * (k + 1) // kt - n * k // kt

    def flush(fold=False):
        todo = list(pend)
        pend.clear()
        for f in todo:
            f()
        if fold and not apart:
            folds()

    def weight(w, k0, kt, c0, cols):
        return w[k0:k0 + kt * P, c0:c0 + cols].rearrange("(k p) n -> p k n", p=P)

    def mm3(out, whi, wlo, xhi, xlo, first, last, signal=False):
        pairs = [(whi, xhi), (whi, xlo), (wlo, xhi)]
        tok = None
        for i, (a, b) in enumerate(pairs):
            f = (lambda e, a=a, b=b, i=i: e.matmul(out, a, b, start=first and i == 0, stop=last and i == 2))
            if (last or signal) and i == 2:
                tok = pe.do(f)
            else:
                pe.go(f)
        return tok

    def beside():
        state["credit"] += state["pace"]
        n, state["pre"] = state["pre"], 0
        if n == 0 and state["credit"] >= 1:
            state["credit"] -= 1
            n = 1
        for _ in range(min(n, state["until"] - mod_next[0])):
            mod_unit()

    def linear(w, k0, kt, c0, cols, xhi, xlo, xtok, evac, adv=1, outer=False, until=None):
        j, hi, lo = take(weight(w, k0, kt, c0, cols), kt, cols)
        beside()
        n = xhi(0).shape[-1]
        tiles = list(range(cols // P))
        for group in ([tiles] if outer else [[t] for t in tiles]):
            banks = [bank() for _ in group]
            open_banks.update(b for b, _ in banks)
            toks = [None] * len(group)
            for k in range(kt):
                if until:
                    until(k)
                pe.wait([xtok[k]])
                ready(j, k, kt)
                for i, t in enumerate(group):
                    toks[i] = mm3(banks[i][1][:, 0:n], hi[:, k, t * P:(t + 1) * P], lo[:, k, t * P:(t + 1) * P],
                                  xhi(k), xlo(k), k == 0, k == kt - 1)
                if k < kt - 1:
                    advance(share(k, kt, adv * len(group)))
            used(j, toks[-1])
            if group[0] == 0:
                flush(True)
            open_banks.difference_update(b for b, _ in banks)
            for i, t in enumerate(group):
                bank_free[banks[i][0]] = evac(t, banks[i][1][:, 0:n], toks[i])
            advance(share(kt - 1, kt, adv * len(group)))

    def linear_tok(w, c0, cols, ntt, xtok, evac, adv=1):
        j, hi, lo = take(weight(w, 0, KT, c0, cols), KT, cols)
        beside()
        for t in range(ntt):
            b, acc = bank()
            acc = acc[:, 0:cols]
            for k in range(KT):
                pe.wait([xtok[k]])
                ready(j, k, KT)
                tok = mm3(acc, m.XN[:, 0, k, t * P:(t + 1) * P], m.XN[:, 1, k, t * P:(t + 1) * P],
                          hi[:, k, :], lo[:, k, :], k == 0, k == KT - 1)
                if k < KT - 1:
                    advance(share(k, KT, adv))
            used(j, tok)
            if t == 0:
                flush(True)
            bank_free[b] = evac(t, acc, tok)
            advance(share(KT - 1, KT, adv))

    def xn(lo, hi):
        return (lambda k: m.XN[:, 0, k, lo:hi]), (lambda k: m.XN[:, 1, k, lo:hi])

    sq_free = [None, None]
    sa_free = [None]
    stat = {"tok": None}

    def sumsq(src, i, n, tok, by_pool=7):
        buf = i % 2
        dst = m.SA[:, 0:n] if i == 0 else m.SQ[:, buf, 0:n]
        a = act.do(lambda e: e.activation(dst, src, ACT.Square), tok, sa_free[0] if i == 0 else sq_free[buf])
        if i == 0:
            stat["sa"] = a
        elif i < by_pool:
            stat["sa"] = pool.do(lambda e: e.tensor_tensor(m.SA[:, 0:n], m.SA[:, 0:n], dst, ALU.add), a, stat["sa"])
            sq_free[buf] = stat["sa"]
        if i < by_pool - 1:
            return
        sa = stat["sa"]

        def later():
            if i == by_pool - 1:
                stat["tok"] = pe.do(lambda e: e.matmul(ps[6][:, 0:n], ones, m.SA[:, 0:n], start=True, stop=False),
                                    sa, bank_free[6])
                sa_free[0] = stat["tok"]
            else:
                stat["tok"] = pe.do(lambda e: e.matmul(ps[6][:, 0:n], ones, dst, start=False, stop=i == KT - 1), a)
                sq_free[buf] = stat["tok"]

        pend.append(later)

    def total(src, i, n, tok):
        def later():
            at = state["totals"]
            state["totals"] += 1
            stat["tok"] = pe.do(lambda e: e.matmul(ps[6][:, 0:n], ones, src, start=at == 0, stop=at == KT - 1),
                                tok, bank_free[6] if at == 0 else None)

        due.append(later)

    due = []

    def totals(n):
        for _ in range(min(n, len(due))):
            due.pop(0)()

    def rstd(n, count, out):
        t = act.do(lambda e: e.activation(out, ps[6][:, 0:n], ACT.Ln, bias=m.eps[:, 0:1], scale=1.0 / count),
                   stat["tok"], eps_tok, rs_free[0])
        bank_free[6] = t
        return act.do(lambda e: e.activation(out, out, ACT.Exp, scale=-0.5), t)

    rs_free = [None]
    tn_free = [None] * 4

    def halves(dst_hi, dst_lo, src, tok, free=None):
        a = act.do(lambda e: e.activation(dst_hi, src, ACT.Copy), tok, free)
        d = dve.do(lambda e: e.tensor_tensor(dst_lo, src, dst_hi.bitcast(F32), ALU.subtract), a, tok, free)
        return d

    def norm(n, gain, shift=None, fillers=1):
        flush()
        free = (m.sem["pe"], pe.n)
        r = rstd(n, D, m.RS[:, 0:n])
        streams = [(0, n)] if shift is None else [(s * S, (s + 1) * S) for s in range(n // S)]
        split = [None] * KT
        toks = [None] * KT
        tmp = [m.TN[:, 0, :], m.TN[:, 1, :], m.SQ[:, 0, :], m.SQ[:, 1, :]]
        ahead = 3 - len(streams)
        for k in range(KT + ahead):
            if k < KT:
                buf = k % 4
                hs = []
                for s, (a, b) in enumerate(streams):
                    t = dve.do(lambda e, a=a, b=b, s=s: e.scalar_tensor_tensor(
                        out=tmp[buf][:, a:b], in0=m.X[:, k, a:b], scalar=gain(k, s), in1=m.RS[:, a:b],
                        op0=ALU.mult, op1=ALU.mult), r, tn_free[buf])
                    hi, tn = m.XN[:, 0, k, a:b], tmp[buf][:, a:b]
                    if shift is None:
                        h = act.do(lambda e, hi=hi, tn=tn: e.activation(hi, tn, ACT.Copy), t, free)
                    else:
                        h = act.do(lambda e, hi=hi, tn=tn, s=s: e.activation(hi, tn, ACT.Identity, bias=shift(k, s)),
                                   t, free)
                    hs.append((t, h))
                split[k] = hs
            if k >= ahead:
                i = k - ahead
                buf = i % 4
                got = []
                for s, (a, b) in enumerate(streams):
                    hi, lo, tn = m.XN[:, 0, i, a:b], m.XN[:, 1, i, a:b], tmp[buf][:, a:b]
                    if shift is None:
                        f = (lambda e, hi=hi, lo=lo, tn=tn: e.tensor_tensor(lo, tn, hi.bitcast(F32), ALU.subtract))
                    else:
                        f = (lambda e, hi=hi, lo=lo, tn=tn, s=s: e.scalar_tensor_tensor(
                            out=lo, in0=tn, scalar=shift(i, s), in1=hi.bitcast(F32), op0=ALU.add, op1=ALU.subtract))
                    got.append(dve.do(f, split[i][s], free))
                tn_free[buf] = got
                toks[i] = got
        sq_free[0], sq_free[1] = tn_free[2], tn_free[3]
        rs_free[0] = toks[-1]
        state["pre"] += fillers
        return toks

    def residual(j, n, gate, acc, tok, last):
        if gate is None:
            t = dve.do(lambda e: e.tensor_tensor(m.X[:, j, 0:n], acc, m.X[:, j, 0:n], ALU.add), tok)
        else:
            for s in range(n // S):
                t = dve.do(lambda e, s=s: e.scalar_tensor_tensor(
                    out=m.X[:, j, s * S:(s + 1) * S], in0=acc[:, s * S:(s + 1) * S], scalar=gate(j, s),
                    in1=m.X[:, j, s * S:(s + 1) * S], op0=ALU.mult, op1=ALU.add), tok)
        if last:
            sumsq(m.X[:, j, 0:n], j, n, t)
        return t

    def tables(name):
        act.go(lambda e: e.preload_act_table_set(name))

    LNEXP, SILU, SIGMOID = "natural_log_exp_and_others", "silu_and_others", "sigmoid_and_others"
    mod_next = [0]
    cond = [None]
    state["until"] = 24
    state["pace"] = 0.16
    ld = m.sem["ld"]
    nld = [0]

    def load(out, in_, q=act):
        q.dma(out, in_, ld)
        nld[0] += 16

    for i in range(2):
        sp.dma(m.X[:, 4 * i:4 * i + 4, 0:S], T["x"][:, 4 * i:4 * i + 4, :], m.sem[f"x{i}"])
    sp.dma(m.cst[:, :], T["consts"][:, 0:m.width], m.sem["cst"])
    sp.dma(m.PV[:, :, :], T["params"], m.sem["pv"])
    sp.dma(m.pos[:, :], T["positions"].broadcast_to([32, S]), m.sem["pos"])
    consts = (m.sem["cst"], 16)
    x_in, c_in = [(m.sem["x0"], 16), (m.sem["x1"], 16)], (m.sem["ci"], 16)
    pe.wait([consts])
    eps_tok = dve.do(lambda e: e.memset(m.eps[:, :], 1e-6))

    for j in range(KT):
        sumsq(m.X[:, j, 0:S], j, S, x_in[j // 4], 4)
        flush()
    pv_tok = (m.sem["pv"], 16)
    c0 = ROW["c_2"]
    sc_zero = dve.do(lambda e: e.memset(m.sc[:, :, :], 0.0))
    flush()

    mod_free = [None]
    mod_tok = [None] * 4

    def mod_unit():
        n = mod_next[0]
        if n >= 48:
            return
        mod_next[0] += 1
        layer, c = n // 12, n % 12
        b, acc = bank()
        for half in range(2):
            j, raw = take(weight(T["mod_w_2"][layer], half * 512, 4, c * 512, 512), 4, 512, True)
            if units is not None:
                pe.wait(ready_at[j])
            pe.wait([cond[0]])
            for k in range(4):
                g = 32 * k
                tok = pe.do(lambda e: e.matmul(acc[g:g + 32, :], m.sc[:, half * 4 + k, :], raw[:, k, :],
                                               start=half == 0, stop=half == 1))
            used(j, tok, True)
        folds()
        t = act.do(lambda e: e.activation(m.macc[:, :], acc[:, :], ACT.Copy), tok, mod_free[0])
        bank_free[b] = t
        splits()

        def fold():
            for i in range(4):
                o = (4 * c + i) * 2
                q = pe.do(lambda e: e.matmul(ps[7][:, o:o + 2], m.macc[:, i * P:(i + 1) * P], cst("fold"),
                                             start=True, stop=True),
                          t, consts, bank_free[7] if c == 0 else None)
            mod_free[0] = q
            if c == 11:
                finish(layer, q)

        foldable.append(fold)

    foldable = []

    def folds():
        while foldable:
            foldable.pop(0)()

    def finish(layer, tok):
        r = ROW["mod_b_2"] + 6 * layer
        biased = []
        for i in range(6):
            bias = m.PV[:, :, r + i:r + i + 1].broadcast_to([P, KT, 2])
            biased.append(dve.do(lambda e: e.tensor_tensor(
                m.mod[:, layer, i * KT:(i + 1) * KT, :],
                ps[7][:, i * 16:(i + 1) * 16].rearrange("p (k s) -> p k s", s=2), bias, ALU.add), tok, pv_tok))
        bank_free[7] = biased
        for w, name in ((0, "norm1_g_2"), (1, "norm2_g_2")):
            i = 1 + 3 * w
            r = ROW[name] + layer
            gain = m.PV[:, :, r:r + 1].broadcast_to([P, KT, 2])
            t = dve.do(lambda e, w=w, i=i, gain=gain: e.scalar_tensor_tensor(
                out=m.gs[:, layer, w, :, :], in0=m.mod[:, layer, i * KT:(i + 1) * KT, :], scalar=1.0, in1=gain,
                op0=ALU.add, op1=ALU.mult), biased)
        mod_tok[layer] = t

    def modcol(layer, i):
        for q in (dve, act):
            q.wait([mod_tok[layer]])
        return lambda k, s: m.mod[:, layer, i * KT + k, s:s + 1]

    def fill(n):
        for _ in range(n):
            mod_unit()
            flush()

    def drain(n=0):
        while background:
            advance()
            if n:
                mod_unit()
                n -= 1
            flush()

    ahead_of_all()
    dve.wait([pv_tok, x_in])
    tables(LNEXP)
    xt = norm(S, lambda k, s: pv("attn_norm", k), fillers=0)
    rope_tok, loaded = [], []

    def conditions():
        tables(SILU)
        sc_tok = act.do(lambda e: e.activation(m.sc[:, :, 0:2], m.PV[:, :, c0:c0 + 2], ACT.Silu), pv_tok, sc_zero)
        cond[0] = sc_tok
        load(m.gb[:, :], T["gate_bias"])
        load(m.amask[:, :], T["consts"][:, m.width:m.width + 1152])
        loaded.extend([(ld, nld[0]), consts])
        A = m.ang
        arrived = (m.sem["pos"], 16)
        t = dve.do(lambda e: e.tensor_copy(A[:, 0, :], m.pos[:, :]), arrived)
        t = dve.do(lambda e: e.tensor_scalar(A[:, 1, :], A[:, 0, :], cst("freq", 32), None, ALU.mult), t, consts)
        t = dve.do(lambda e: e.tensor_scalar(A[:, 2, :], A[:, 1, :], float(1.0 / (2.0 * np.pi)), ROUND,
                                             ALU.mult, ALU.add), t)
        t = dve.do(lambda e: e.tensor_scalar(A[:, 2, :], A[:, 2, :], ROUND, None, ALU.subtract), t)
        for part in (TWO_PI_A, TWO_PI_B, TWO_PI_C):
            t = dve.do(lambda e, part=part: e.scalar_tensor_tensor(
                out=A[:, 1, :], in0=A[:, 2, :], scalar=-part, in1=A[:, 1, :], op0=ALU.mult, op1=ALU.add), t)
        t = dve.do(lambda e: e.tensor_scalar(A[:, 1, :], A[:, 1, :], 3.1415925, -3.1415925, ALU.min, ALU.max), t)
        t = dve.do(lambda e: e.scalar_tensor_tensor(out=A[:, 3, :], in0=A[:, 1, :], scalar=-1.0, in1=A[:, 1, :],
                                                    op0=ALU.mult, op1=ALU.max), t)
        t = dve.do(lambda e: e.tensor_scalar(A[:, 3, :], A[:, 3, :], -1.0, float(np.pi / 2), ALU.mult, ALU.add), t)
        act.do(lambda e: e.activation(m.rope[:, 0, :], A[:, 3, :], ACT.Sin), t)
        t = act.do(lambda e: e.activation(m.rope[:, 1, :], A[:, 1, :], ACT.Sin), t)
        rope_tok.append(t)
        tables(LNEXP)

    xhi, xlo = xn(0, S)
    w = T["attn_w_in"][0]
    scale = float(P) ** -0.5
    pb_free = [None, None]
    pt_free = [None, None]
    qk_free = [None, None]
    nrt = [0]
    otoks = [None] * KT

    def attend1(pair, qk_tok, v_tok):
        pbuf = pair % 2
        probs = {}

        def scores(h):
            hh = h % 2
            buf = h % 2
            q = [m.QK[:, pbuf, g, 0, hh, :] for g in range(3)]
            k = [m.QK[:, pbuf, g, 1, hh, :] for g in range(3)]
            parts = [[(q[0][:, P:S], k[0], 0, 256), (q[1][:, P:S], k[1], 256, 256)],
                     [(q[2][:, P:S], k[2], 0, 256)],
                     [(q[g][:, 0:P], k[g][:, 0:P], g * P, P) for g in range(3)]]
            st = m.stat[:, buf * 16:buf * 16 + 16]
            at = 0
            toks = []
            for n, part in enumerate(parts):
                b, acc = bank()
                for a, c, o, width in part:
                    tok = pe.do(lambda e: e.matmul(acc[:, o:o + width], a, c, start=True, stop=True), qk_tok)
                end = o + width
                t = dve.do(lambda e: e.tensor_tensor_reduce(
                    out=m.PB[:, buf, at:at + end], in0=acc[:, 0:end], in1=m.amask[:, at:at + end], scale=1.0,
                    scalar=-3.0e38, op0=ALU.add, op1=ALU.max, accum_out=st[:, n:n + 1]),
                    tok, pb_free[buf], loaded)
                bank_free[b] = t
                toks.append(t)
                at += end
            t = dve.do(lambda e: e.tensor_tensor(st[:, 3:4], st[:, 0:1], st[:, 1:2], ALU.max), toks)
            t = dve.do(lambda e: e.tensor_scalar(st[:, 4:6], st[:, 2:4], -scale, None, ALU.mult), t)
            rngs = ((768, 1152), (0, 768))
            ex = [act.do(lambda e: e.activation(
                m.PB[:, buf, r[0]:r[1]], m.PB[:, buf, r[0]:r[1]], ACT.Exp, bias=st[:, 4 + i:5 + i], scale=scale,
                accum_out=st[:, 6 + i:7 + i]), t) for i, r in enumerate(rngs)]
            t = dve.do(lambda e: e.reciprocal(st[:, 8:10], st[:, 6:8]), ex)
            probs[h] = [dve.do(lambda e: e.tensor_scalar(
                m.PB[:, buf, r[0]:r[1]], m.PB[:, buf, r[0]:r[1]], st[:, 8 + i:9 + i], None, ALU.mult), t)
                for i, r in enumerate(rngs)]

        got = {}

        def turn(h):
            buf = h % 2
            got[h] = []
            for g in range(3):
                b, acc = bank()
                for o, at in ((0, 768 + g * P), (P, g * 256), (2 * P, g * 256 + P)):
                    tok = pe.do(lambda e: e.transpose(acc[:, o:o + P], m.PB[:, buf, at:at + P], ident), probs[h])
                if g == 0:
                    t = dve.do(lambda e: e.tensor_copy(m.PT1[:, buf, g, :], acc[:, 0:384]), tok, pt_free[buf])
                else:
                    t = act.do(lambda e: e.activation(m.PT1[:, buf, g, :], acc[:, 0:384], ACT.Copy), tok,
                               pt_free[buf])
                bank_free[b] = t
                got[h].append(t)
            pb_free[buf] = tok

        def mix(h):
            hh = h % 2
            buf = h % 2
            b, acc = bank()
            plan = [(0, 0), (0, 1), (1, 1), (2, 1), (1, 0), (2, 0)]
            for i, (g, kt) in enumerate(plan):
                out = acc[:, 0:S] if kt == 0 else acc[:, P:S]
                prob = m.PT1[:, buf, g, 0:256] if kt == 0 else m.PT1[:, buf, g, 256:384]
                tok = pe.do(lambda e: e.matmul(out, m.V1[:, pbuf, kt, g, hh * P:(hh + 1) * P], prob, start=i == 0,
                                               stop=i == len(plan) - 1, skip_group_check=True), got[h], v_tok)
            pt_free[buf] = tok
            otoks[h] = halves(m.XN[:, 0, h, S:512], m.XN[:, 1, h, S:512], acc[:, 0:S], tok)
            bank_free[b] = otoks[h]
            qk_free[pbuf] = tok

        h0, h1 = 2 * pair, 2 * pair + 1
        for f, h, idle in ((scores, h0, 1), (scores, h1, 1), (turn, h0, 0), (mix, h0, 0), (turn, h1, 1),
                           (mix, h1, 0)):
            f(h)
            for _ in range(1 + idle):
                yield True

    for pair in range(4):
        pbuf = pair % 2
        qk_tok, v_tok = [], []
        for g in range(3):
            for which in range(2):
                col = ((g * 3 + which) * 8 + pair * 2) * P
                dst = m.QK[:, pbuf, g, which, :, :]
                got = []

                def evac(t, acc, tok):
                    r = act.do(lambda e: e.activation(dst[:, t, :], acc, ACT.Copy), tok, qk_free[pbuf])
                    got.append(r)
                    return r

                linear(w, 0, KT, col, 256, xhi, xlo, xt, evac, outer=pair + g + which == 0)

                if pair + g + which == 0:
                    pend.append(conditions)

                def rotate(dst=dst, got=got, qk_tok=qk_tok):
                    b, acc = bank()
                    buf = nrt[0] % 2
                    nrt[0] += 1
                    tok = pe.do(lambda e: e.matmul(acc[0:32, :], cst("rot", 32), dst[0:32, :, :],
                                                   start=True, stop=True), got, consts)
                    cos = m.rope[:, 0, :].unsqueeze(1).broadcast_to([32, 2, S])
                    sin = m.rope[:, 1, :].unsqueeze(1).broadcast_to([32, 2, S])
                    rt = m.RT[:, buf, :].rearrange("p (h t) -> p h t", h=2)
                    t1 = dve.do(lambda e: e.tensor_tensor(
                        rt, acc[0:32, :].rearrange("p (h t) -> p h t", h=2), sin, ALU.mult), tok, rope_tok)
                    bank_free[b] = t1
                    t2 = dve.do(lambda e: e.tensor_tensor(dst[0:32, :, :], dst[0:32, :, :], cos, ALU.mult),
                                tok, got)
                    qk_tok.append(dve.do(lambda e: e.tensor_tensor(dst[0:32, :, :], dst[0:32, :, :], rt,
                                                                   ALU.add), t1, t2))

                pend.append(rotate)
            col = ((g * 3 + 2) * 8 + pair * 2) * P

            def evac(t, acc, tok):
                r = act.do(lambda e: e.activation(m.V1[:, pbuf, t, g, :], acc, ACT.Copy), tok, qk_free[pbuf])
                v_tok.append(r)
                return r

            linear_tok(w, col, 256, 2, xt, evac)
        flush()
        assert not background
        background.append(attend1(pair, qk_tok, v_tok))
    def stages_for(done, mods=0):
        left = [mods, 0]

        def until(k):
            while background and not done(k):
                advance()
                left[1] += 1
                if left[0] and left[1] % 2 == 0:
                    left[0] -= 1
                    mod_unit()
                flush()

        return until

    def grow(xh, xl, xtok, n, gate, wsrc, until=None, adv=1):
        for c in range(4):
            def evac(t, acc, tok):
                return residual(c * 2 + t, n, gate, acc, tok, True)
            first = until if c == 0 else None
            linear(wsrc, 0, KT, c * 256, 256, xh, xl, xtok, evac, adv=adv if first else 1,
                   outer=bool(first), until=first)
            if first:
                drain()

    mh, ml = xn(S, 512)
    grow(mh, ml, otoks, S, None, T["attn_w_out"][0], stages_for(lambda k: otoks[k] is not None, 2), 3)

    def swiglu(layer):
        xt = norm(S, lambda k, s: pv("ffn_norm", k, layer))
        if layer == 1:
            pool.dma(m.X[:, :, S:512], T["ctx_2"], m.sem["ci"], xt)
        xhi, xlo = xn(0, S)
        w = T["ffn_w_in"][layer]
        wo = T["ffn_w_out"][layer]
        tables(SILU)
        htok = [None] * 22
        sg_free = [None] * 2
        sg_tok = {}
        for j in range(11):
            def evac_g(t, acc, tok):
                r = act.do(lambda e: e.activation(m.SG[:, j % 2, t, :], acc, ACT.Silu), tok, sg_free[j % 2])
                sg_tok[t] = r
                return r

            def evac_u(t, acc, tok):
                buf = j % 2
                r = dve.do(lambda e: e.tensor_tensor(m.SG[:, buf, t, :], acc, m.SG[:, buf, t, :], ALU.mult),
                           tok, sg_tok[t])
                i = 2 * j + t
                htok[i] = halves(m.HF[:, 0, i, :], m.HF[:, 1, i, :], m.SG[:, buf, t, :], r)
                if t == 1:
                    sg_free[buf] = [htok[i - 1], htok[i]]
                return r

            linear(w, 0, KT, j * 256, 256, xhi, xlo, xt, evac_g, outer=j == 0)
            linear(w, 0, KT, DFF + j * 256, 256, xhi, xlo, xt, evac_u)
        tables(LNEXP)
        for c in range(4):
            banks = [bank(), bank()]
            for part, (k0, kt) in enumerate(((0, 8), (8, 8), (16, 6))):
                j, hi, lo = take(weight(wo, k0 * P, kt, c * 256, 256), kt, 256)
                beside()
                for t in range(2):
                    acc = banks[t][1][:, 0:S]
                    for k in range(kt):
                        kk = k0 + k
                        pe.wait([htok[kk]])
                        ready(j, k, kt)
                        tok = mm3(acc, hi[:, k, t * P:(t + 1) * P], lo[:, k, t * P:(t + 1) * P],
                                  m.HF[:, 0, kk, :], m.HF[:, 1, kk, :], kk == 0, kk == 21, k == kt - 1)
                    if kk == 21:
                        if t == 0:
                            flush(True)
                        bank_free[banks[t][0]] = residual(c * 2 + t, S, None, acc, tok, True)
                used(j, tok)

    swiglu(0)

    xt = norm(S, lambda k, s: pv("mlstm_norm", k))
    xhi, xlo = xn(0, S)
    w = T["mlstm_w_in"][0]
    pads = pool.do(lambda e: e.memset(m.CB[:, :, 0:3], 0.0), xt)
    one8 = pool.do(lambda e: e.memset(m.G8[:, 7, :], 1.0), xt)
    vone = pool.do(lambda e: e.memset(m.VM[:, :, :, P:P + 1], 1.0), xt)
    j, hi, lo = take(weight(w, 0, KT, 3072, 16), KT, 16)
    beside()
    gbanks = []
    for i in range(2):
        b, acc = bank()
        for k in range(KT):
            pe.wait([xt[k]])
            ready(j, k, KT)
            tok = mm3(acc[0:8, 0:S], hi[:, k, i * 8:i * 8 + 8], lo[:, k, i * 8:i * 8 + 8], xhi(k), xlo(k),
                      k == 0, k == KT - 1)
        gbanks.append((b, acc, tok))
    used(j, tok)
    flush(True)
    G = m.G8
    z = dve.do(lambda e: e.tensor_scalar(G[:, 0, :], gbanks[1][1][0:8, 0:S], m.gb[:, 1:2], None, ALU.add),
               gbanks[1][2], loaded, xt[KT - 1])
    bank_free[gbanks[1][0]] = z
    az = dve.do(lambda e: e.scalar_tensor_tensor(out=G[:, 1, :], in0=G[:, 0, :], scalar=-1.0,
                                                 in1=G[:, 0, :], op0=ALU.mult, op1=ALU.max), z)
    t = act.do(lambda e: e.activation(G[:, 1, :], G[:, 1, :], ACT.Exp, scale=-1.0), az)
    t = act.do(lambda e: e.activation(G[:, 1, :], G[:, 1, :], ACT.Ln, bias=ones[0:8, 0:1]), t)
    t = dve.do(lambda e: e.scalar_tensor_tensor(out=G[:, 0, :], in0=G[:, 0, :], scalar=0.0,
                                                in1=G[:, 1, :], op0=ALU.min, op1=ALU.subtract), t)
    Bt = dve.do(lambda e: e.tensor_tensor_scan(G[:, 2, :], G[:, 7, :], G[:, 0, :], 0.0,
                                               ALU.mult, ALU.add), t, one8)
    At = dve.do(lambda e: e.scalar_tensor_tensor(out=G[:, 3, :], in0=gbanks[0][1][0:8, 0:S],
                                                 scalar=m.gb[:, 0:1], in1=G[:, 2, :],
                                                 op0=ALU.add, op1=ALU.subtract), Bt, gbanks[0][2])
    bank_free[gbanks[0][0]] = At
    Mt = dve.do(lambda e: e.tensor_tensor_scan(G[:, 4, :], G[:, 3, :], G[:, 3, :], 0.0,
                                               ALU.max, ALU.max), At)
    NMt = dve.do(lambda e: e.tensor_scalar(G[:, 5, :], G[:, 4, :], -1.0, None, ALU.mult), Mt)
    EMt = dve.do(lambda e: e.scalar_tensor_tensor(out=G[:, 6, :], in0=G[:, 2, :], scalar=-1.0,
                                                  in1=G[:, 4, :], op0=ALU.mult, op1=ALU.subtract), Mt)

    ac_tok = []

    def columns():
        b, acc = bank()
        for w8, row in enumerate((3, 6)):
            for i in range(2):
                o = w8 * 16 + i * 8
                tok = pe.do(lambda e: e.transpose(acc[:, o:o + 8], G[:, row, i * P:(i + 1) * P], ident[0:8, 0:8]),
                            At, EMt, consts)
        t = dve.do(lambda e: e.tensor_copy(m.AC[:, 0, :, :], acc[:, 0:16].rearrange("p (i h) -> p i h", i=2)), tok)
        t2 = act.do(lambda e: e.activation(m.AC[:, 1, :, :], acc[:, 16:32].rearrange("p (i h) -> p i h", i=2),
                                           ACT.Exp), tok, t)
        bank_free[b] = [t, t2]
        ac_tok.extend([t, t2])

    otoks[:] = [None] * KT
    qk_done = [None] * KT
    v_tok = []
    so_tok = [None] * KT
    mmask = cst("mmask")
    wt_free = [None, None]
    ht_free = [None, None]

    def cells():
        hot = {}

        def weights(h):
            buf = h % 2
            WT = m.WT[:, buf, :]
            b, acc = bank()
            tok = pe.do(lambda e: e.matmul(acc[:, 0:S], m.cst[0:8, h:h + 1].broadcast_to([8, P]), G[:, 5, :],
                                           start=True, stop=True), NMt, consts)
            t1 = dve.do(lambda e: e.tensor_tensor(WT[:, 0:S], acc[:, 0:S], mmask[:, 0:S], ALU.add), tok, wt_free[buf])
            t2 = dve.do(lambda e: e.tensor_tensor(WT[:, S:384], acc[:, P:S], mmask[:, S:384], ALU.add),
                        tok, wt_free[buf])
            bank_free[b] = [t1, t2]
            e2 = act.do(lambda e: e.activation(WT[:, 0:S], WT[:, 0:S], ACT.Exp, bias=m.AC[:, 0, 0, h:h + 1]),
                        t1, ac_tok)
            e3 = act.do(lambda e: e.activation(WT[:, S:384], WT[:, S:384], ACT.Exp, bias=m.AC[:, 0, 1, h:h + 1]), t2)
            hot[h] = [e2, e3]

        def products(h):
            WT = m.WT[:, h % 2, :]
            o = 64 * (h % 2)
            Q = m.QKM[o:o + 64, h // 2, :]
            K = m.QKM[o:o + 64, 4 + h // 2, :]
            b, acc = bank()
            pe.go(lambda e: e.matmul(acc[:, 0:S], K[:, 0:P], Q, start=True, stop=True),
                  qk_done[h // 2], qk_done[4 + h // 2])
            tok = pe.do(lambda e: e.matmul(acc[:, S:384], K[:, P:S], Q[:, P:S], start=True, stop=True))
            t = dve.do(lambda e: e.scalar_tensor_tensor(out=WT, in0=acc[:, 0:384], scalar=0.125, in1=WT,
                                                        op0=ALU.mult, op1=ALU.mult), tok, hot[h])
            bank_free[b] = t
            hot[h] = t

        def cell(h):
            buf = h % 2
            WT = m.WT[:, buf, :]
            b, acc = bank()
            V = m.VM[:, :, h, :]
            pe.go(lambda e: e.matmul(acc[:, 0:129], WT[:, 0:P], V[:, 0, :], start=True, stop=True),
                  hot[h], v_tok, vone)
            pe.go(lambda e: e.matmul(acc[:, 256:385], WT[:, P:S], V[:, 0, :], start=True, stop=False))
            tok = pe.do(lambda e: e.matmul(acc[:, 256:385], WT[:, S:384], V[:, 1, :], start=False, stop=True))
            wt_free[buf] = tok
            num = acc.rearrange("p (i v) -> p i v", i=2)
            st = m.stat[:, 32 + buf * 16:48 + buf * 16]
            t = act.do(lambda e: e.activation(st[:, 0:2], num[:, :, P:P + 1].rearrange("p i v -> p (i v)"), ACT.Abs),
                       tok)
            t = dve.do(lambda e: e.tensor_tensor(st[:, 2:4], st[:, 0:2], m.AC[:, 1, :, h], ALU.max), t, ac_tok)
            t = dve.do(lambda e: e.reciprocal(st[:, 4:6], st[:, 2:4]), t)
            sq = [act.do(lambda e: e.activation(m.HT[:, buf, i, :], num[:, i, 0:P], ACT.Square,
                                                scale=st[:, 4 + i:5 + i], accum_out=st[:, 6 + i:7 + i]),
                         t, ht_free[buf]) for i in range(2)]
            hot[h] = (b, num, t, sq)
            open_banks.add(b)

        def scale(h):
            buf = h % 2
            b, num, t, sq = hot[h]
            open_banks.discard(b)
            st = m.stat[:, 32 + buf * 16:48 + buf * 16]
            t2 = act.do(lambda e: e.activation(st[:, 8:10], st[:, 6:8], ACT.Ln, bias=m.eps[:, 0:1], scale=1.0 / P),
                        sq, eps_tok)
            t2 = act.do(lambda e: e.activation(st[:, 8:10], st[:, 8:10], ACT.Exp, scale=-0.5), t2)
            t = dve.do(lambda e: e.tensor_tensor(st[:, 10:12], st[:, 8:10], st[:, 4:6], ALU.mult), t2)
            last = [dve.do(lambda e: e.tensor_scalar(m.HT[:, buf, i, :], num[:, i, 0:P], st[:, 10 + i:11 + i], None,
                                                     ALU.mult), t, sq) for i in range(2)]
            bank_free[b] = last
            hot[h] = last

        def close(h):
            buf = h % 2
            b, acc = bank()
            for i in range(2):
                tok = pe.do(lambda e: e.transpose(acc[:, i * P:(i + 1) * P], m.HT[:, buf, i, :], ident), hot[h])
            ht_free[buf] = tok
            r = dve.do(lambda e: e.scalar_tensor_tensor(out=m.HS[:, buf, :], in0=acc[:, 0:S],
                                                        scalar=pv("mlstm_head_gain", h), in1=m.SO[:, h, :],
                                                        op0=ALU.mult, op1=ALU.mult), tok, so_tok[h], hs_free[buf])
            bank_free[b] = r
            otoks[h] = hs_free[buf] = halves(m.XN[:, 0, h, S:512], m.XN[:, 1, h, S:512], m.HS[:, buf, :], r)

        for f in (weights, products):
            for h in range(2):
                f(h)
                yield True
        for h in range(8):
            while len(v_tok) < 2 * (h // 2 + 1):
                yield True
            cell(h)
            yield True
            if h + 2 < 8:
                weights(h + 2)
                yield True
            scale(h)
            yield True
            if h + 2 < 8:
                while qk_done[h // 2 + 1] is None or qk_done[h // 2 + 5] is None:
                    yield True
                products(h + 2)
                yield True
            while h and so_tok[h - 1] is None:
                yield True
            if h:
                close(h - 1)
                yield True
        while so_tok[7] is None:
            yield True
        close(7)

    hs_free = [None, None]

    def convolved(c):
        got = {}

        def evac(t, acc, tok):
            r = act.do(lambda e: e.activation(m.CB[:, 2 * c + t, 3:3 + S], acc, ACT.Copy), tok)
            got[t] = r
            return r

        linear(w, 0, KT, c * 256, 256, xhi, xlo, xt, evac, adv=3)
        for t in range(2):
            k = 2 * c + t
            r = dve.do(lambda e: e.tensor_scalar(m.QKM[:, k, :], m.CB[:, k, 0:S], pv("mlstm_conv_w", k, 0),
                                                 pv("mlstm_conv_b", k), ALU.mult, ALU.add), got[t], pads)
            for i in range(1, 4):
                r = dve.do(lambda e: e.scalar_tensor_tensor(
                    out=m.QKM[:, k, :], in0=m.CB[:, k, i:i + S], scalar=pv("mlstm_conv_w", k, i),
                    in1=m.QKM[:, k, :], op0=ALU.mult, op1=ALU.add), r)
            conv_done[k] = r

    conv_done = [None] * KT

    def activate(tiles):
        tables(SILU)
        for k in tiles:
            qk_done[k] = act.do(lambda e: e.activation(m.QKM[:, k, :], m.QKM[:, k, :], ACT.Silu), conv_done[k])
        tables(LNEXP)

    def values(c):
        def evac(t, acc, tok):
            r = dve.do(lambda e: e.tensor_copy(m.VM[:, t, 2 * c:2 * c + 2, 0:P],
                                               acc.rearrange("p (h v) -> p h v", h=2)), tok)
            v_tok.append(r)
            return r

        linear_tok(w, 1024 + c * 256, 256, 2, xt, evac, adv=3)

    def outer_gate(c):
        def evac(t, acc, tok):
            k = 2 * c + t
            so, sg = m.SO[:, k, :], m.SG1[:, t, :]
            r = act.do(lambda e: e.activation(sg, acc, ACT.Abs), tok, sg_free[t])
            r = act.do(lambda e: e.activation(sg, sg, ACT.Exp, scale=-1.0), r)
            r = act.do(lambda e: e.activation(sg, sg, ACT.Ln, bias=ones[:, 0:1]), r)
            d = dve.do(lambda e: e.scalar_tensor_tensor(out=so, in0=acc, scalar=0.0, in1=sg,
                                                        op0=ALU.min, op1=ALU.subtract), tok, r)
            sg_free[t] = d
            so_tok[k] = act.do(lambda e: e.activation(so, so, ACT.Exp), d)
            return d

        linear(w, 0, KT, 2048 + c * 256, 256, xhi, xlo, xt, evac, adv=3)

    sg_free = [None, None]
    convolved(0)
    convolved(2)
    values(0)
    activate((0, 4, 1, 5))
    columns()
    background.append(cells())
    outer_gate(0)
    values(1)
    outer_gate(1)
    convolved(1)
    convolved(3)
    values(2)
    activate((2, 6, 3, 7))
    outer_gate(2)
    values(3)
    outer_gate(3)
    flush()
    grow(mh, ml, otoks, S, None, T["mlstm_w_out"][0], stages_for(lambda k: otoks[k] is not None, 1), 2)
    swiglu(1)
    fill(24 - mod_next[0])
    folds()
    state["until"], state["pace"] = 48, 0.0

    flush()
    r = rstd(S, D, m.RS[:, 0:S])
    for k in range(KT):
        t = dve.do(lambda e: e.scalar_tensor_tensor(out=m.X[:, k, 0:S], in0=m.X[:, k, 0:S],
                                                    scalar=pv("final_norm", k), in1=m.RS[:, 0:S],
                                                    op0=ALU.mult, op1=ALU.mult), r)
        sumsq(m.X[:, k, :], k, 512, [t, c_in], 1)
        flush()
    rs_free[0] = t

    def neighbourhood(layer, slot, ctx_out):
        n = 512 if ctx_out else S
        xt = norm(512, lambda k, s: m.gs[:, layer, 0, k, s:s + 1], modcol(layer, 0))
        w = T["na_wqkv_2"][slot]
        start = xt[KT - 1]
        tbs = [m.sem["tb0"], m.sem["tb1"]]
        tb_tok = [None] * 16
        tb_free = [None, None]
        nmask = cst("nmask").unsqueeze(1).broadcast_to([P, 4, 64])
        zero = pool.do(lambda e: e.memset(m.TB[:, :, :, S:512], 0.0), xt)

        def table(i):
            pair, qb = i // 2, i % 2
            buf = i % 2
            rpb = T["na_rpb_2"]
            for hh in range(2):
                h = pair * 2 + hh
                for rr in range(2):
                    base = slot * 7440 + h * 465 + (rr + 6 - 2 * qb) * 31 - 48
                    src = bass.AP(tensor=rpb.tensor, offset=base, ap=[[1, 64], [31, 4], [1, 64]])
                    dst = m.TB[rr * 64:rr * 64 + 64, buf, hh, 0:S].rearrange("p (a c) -> p a c", a=4)
                    pool.dma(dst, src, tbs[buf], start, tb_free[buf])
                    tb_count[buf] += 16
            got = []
            for hh in range(2):
                v = m.TB[:, buf, hh, 0:S].rearrange("p (a c) -> p a c", c=64)
                got.append(pool.do(lambda e: e.tensor_tensor(v, v, nmask, ALU.add),
                                   (tbs[buf], tb_count[buf]), consts))
            tb_tok[i] = got

        table(0)
        table(1)
        pb_free = [None, None]
        pt_free = [None]
        npb = [0]
        in_free = [None, None]
        otok = [[] for _ in range(KT)]

        def attend(group, qt, kt_, vt):
            gb = group % 2

            def softmax(buf, width, toks, st, pieces):
                ex = []
                for hh in range(2):
                    for i in range(pieces):
                        c = hh * pieces + i
                        v = m.PB2[:, buf, hh, i * width:(i + 1) * width]
                        ex.append((v, act.do(lambda e: e.activation(
                            v, toks[hh][1][:, i * width:(i + 1) * width], ACT.Exp, bias=st[:, c:c + 1],
                            accum_out=st[:, 4 + c:5 + c]), toks[hh][0], pb_free[buf]), c))
                n = 2 * pieces
                t = dve.do(lambda e: e.reciprocal(st[:, 8:8 + n], st[:, 4:4 + n]), [x[1] for x in ex])
                return [dve.do(lambda e: e.tensor_scalar(v, v, st[:, 8 + c:9 + c], None, ALU.mult), t)
                        for v, _, c in ex], [x[1] for x in ex]

            def lat_scores(p, qb):
                buf = npb[0] % 2
                npb[0] += 1
                i = (group * 2 + p) * 2 + qb
                st = m.stat[:, buf * 16:buf * 16 + 16]
                banks = [bank(), bank()]
                maxed = []
                for hh in range(2):
                    o = 64 * hh
                    acc = banks[hh][1]
                    tok = pe.do(lambda e: e.matmul(acc[:, :], m.QB[o:o + 64, gb, p, qb * P:(qb + 1) * P],
                                                   m.KB[o:o + 64, gb, p, :], start=True, stop=True), qt, kt_)
                    t = dve.do(lambda e: e.tensor_tensor_reduce(
                        out=m.PB2[:, buf, hh, :], in0=acc[:, :], in1=m.TB[:, qb, hh, :], scale=1.0, scalar=-3.0e38,
                        op0=ALU.add, op1=ALU.max, accum_out=st[:, 12 + hh:13 + hh]),
                        tok, tb_tok[i], zero, pb_free[buf])
                    bank_free[banks[hh][0]] = t
                    maxed.append(t)
                tb_free[qb] = maxed
                if i + 2 < 16:
                    table(i + 2)
                t = dve.do(lambda e: e.tensor_scalar(st[:, 0:2], st[:, 12:14], -1.0, None, ALU.mult), maxed)
                return buf, softmax(buf, 512, [(t, m.PB2[:, buf, hh, :]) for hh in range(2)], st, 1)[0]

            def ctx_scores(p):
                buf = npb[0] % 2
                npb[0] += 1
                st = m.stat[:, buf * 16:buf * 16 + 16]
                banks = [bank(), bank()]
                for qb in range(2):
                    for hh in range(2):
                        o = 64 * hh
                        acc = banks[hh][1]
                        tok = pe.do(lambda e: e.matmul(
                            acc[:, qb * S:(qb + 1) * S], m.QB[o:o + 64, gb, p, S + qb * P:S + (qb + 1) * P],
                            m.KB[o:o + 64, gb, p, S:512], start=True, stop=True), qt, kt_)
                ts = []
                for hh in range(2):
                    v = banks[hh][1].rearrange("p (i k) -> p i k", i=2)
                    ts.append(dve.do(lambda e: e.tensor_reduce(st[:, 2 * hh:2 * hh + 2], v, AX.X, ALU.max,
                                                               negate=True), tok, pb_free[buf]))
                done, ex = softmax(buf, S, [(ts[hh], banks[hh][1]) for hh in range(2)], st, 2)
                for hh in range(2):
                    bank_free[banks[hh][0]] = ex
                return buf, done

            def turn(buf, ready_, blocks, where):
                got = []
                for hh in range(2):
                    b, acc = bank()
                    for i, (col, kt, q) in enumerate(blocks):
                        tok = pe.do(lambda e: e.transpose(acc[:, i * P:(i + 1) * P],
                                                          m.PB2[:, buf, hh, col:col + P], ident), ready_)
                    dst = where(hh)
                    src = acc[:, :].rearrange("p (k q) -> p k q", q=P)[:, :, ::-1]
                    dst = dst.rearrange("p k (b q) -> p (k b) q", q=P) if dst.shape[2] > P else dst
                    if hh == 0:
                        c = act.do(lambda e: e.activation(dst, src, ACT.Copy), tok, pt_free[0])
                    else:
                        c = dve.do(lambda e: e.tensor_copy(dst, src), tok, pt_free[0])
                    bank_free[b] = c
                    got.append(c)
                pb_free[buf] = tok
                return got

            def mix(p, got, k0, nk, at):
                tile = group * 2 + p
                b, acc = bank()
                for kt in range(nk):
                    for hh in range(2):
                        o = 64 * hh
                        c = (2 * p + hh) * 64
                        tok = pe.do(lambda e: e.matmul(acc[o:o + 64, 0:S], m.VB[:, gb, k0 + kt, c:c + 64],
                                                       m.PT2[:, hh, kt, :], start=kt == 0, stop=kt == nk - 1),
                                    got, vt)
                pt_free[0] = tok
                r = halves(m.OB[:, 0, tile, at:at + S], m.OB[:, 1, tile, at:at + S], acc[:, 0:S], tok)
                bank_free[b] = r
                otok[tile].append(r)
                in_free[gb] = tok

            def lat_turn(s, qb):
                return turn(s[0], s[1], [(kt * P, kt, qb) for kt in range(4)],
                            lambda hh: m.PT2[:, hh, :, qb * P:(qb + 1) * P])

            def ctx_turn(s):
                return turn(s[0], s[1], [(qb * S + kt * P, kt, qb) for kt in range(2) for qb in range(2)],
                            lambda hh: m.PT2[:, hh, 0:2, :])

            s0 = lat_scores(0, 0)
            yield True
            s1 = lat_scores(0, 1)
            yield True
            for p in range(2):
                got = lat_turn(s0, 0)
                yield True
                if ctx_out:
                    sc = ctx_scores(p)
                    yield True
                got = got + lat_turn(s1, 1)
                yield True
                if p == 0:
                    s0 = lat_scores(1, 0)
                    yield True
                mix(p, got, 0, 4, 0)
                yield True
                if ctx_out:
                    got = ctx_turn(sc)
                    yield True
                if p == 0:
                    s1 = lat_scores(1, 1)
                    yield True
                if ctx_out:
                    mix(p, got, 2, 2, S)
                    yield True

        for group in range(4):
            gb = group % 2
            qt, kt_, vt = [], [], []

            def evac_q(t, acc, tok):
                while len(background) > 1:
                    advance()
                r = act.do(lambda e: e.activation(m.QB[:, gb, t, 0:n].rearrange("p (b q) -> p b q", q=P),
                                                  acc.rearrange("p (b q) -> p b q", q=P)[:, :, ::-1], ACT.Copy,
                                                  scale=0.125), tok, in_free[gb])
                qt.append(r)
                return r

            def evac_k(t, acc, tok):
                r = act.do(lambda e: e.activation(m.KB[:, gb, t, :], acc, ACT.Copy), tok, in_free[gb])
                kt_.append(r)
                return r

            def evac_v(t, acc, tok):
                r = act.do(lambda e: e.activation(m.VB[:, gb, t, :], acc, ACT.Copy), tok, in_free[gb])
                vt.append(r)
                return r

            xh, xl = xn(0, n)
            linear(w, 0, KT, group * 256, 256, xh, xl, xt, evac_q, adv=2 if ctx_out else 1, outer=group == 0)
            xh, xl = xn(0, 512)
            linear(w, 0, KT, 1024 + group * 256, 256, xh, xl, xt, evac_k, adv=2)
            linear_tok(w, 2048 + group * 256, 256, 4, xt, evac_v, adv=2)
            flush()
            while len(background) > 1:
                advance()
            background.append(attend(group, qt, kt_, vt))
        grow(lambda k: m.OB[:, 0, k, 0:n], lambda k: m.OB[:, 1, k, 0:n], otok, n, modcol(layer, 2),
             T["na_wo_2"][slot], stages_for(lambda k: len(otok[k]) == (2 if ctx_out else 1), 3 if ctx_out else 0), 6)

    tb_count = [0, 0]

    def conformer(layer):
        xt = norm(512, lambda k, s: m.gs[:, layer, 0, k, s:s + 1], modcol(layer, 0))
        xh, xl = xn(0, 512)
        w = T["cv_w1_2"][0]
        tables(SIGMOID)
        pads = [pool.do(lambda e, a=a: e.memset(m.U[:, :, :, a:a + 15], 0.0), xt[KT - 1]) for a in (0, 271)]
        ab_free = [None, None]
        cv_tok = [None] * KT
        ut = {}

        def shifted(k):
            return m.CV[:, k, :].rearrange("p (s t) -> p s t", s=2)

        def convolve(tiles):
            r = {}
            for i in range(31):
                for k in tiles:
                    out = shifted(k)
                    if i == 0:
                        r[k] = dve.do(lambda e: e.tensor_scalar(out, m.U[:, k, :, 0:S], pv("cv_dw_2", k, 0),
                                                                pv("cv_dwb_2", k), ALU.mult, ALU.add), ut[k], pads)
                    else:
                        r[k] = dve.do(lambda e: e.scalar_tensor_tensor(
                            out=out, in0=m.U[:, k, :, i:i + S], scalar=pv("cv_dw_2", k, i), in1=out,
                            op0=ALU.mult, op1=ALU.add), r[k])
                    if i == 30:
                        cv_tok[k] = r[k]
                        total(m.CV[:, k, :], k, 512, r[k])
                    yield True

        def convolve_apart(tiles):
            for k in tiles:
                while k not in ut:
                    yield True
                out = shifted(k)
                sums = act.do(lambda e: e.activation(out, m.U[:, k, :, 0:S], ACT.Identity, scale=pv("cv_dw_2", k, 0),
                                                     bias=pv("cv_dwb_2", k)), ut[k], pads)
                for i in range(1, 31):
                    buf = i % 4
                    tap = m.TAP[:, buf, :].rearrange("p (s t) -> p s t", s=2)
                    t = act.do(lambda e: e.activation(tap, m.U[:, k, :, i:i + S], ACT.Copy, scale=pv("cv_dw_2", k, i)),
                               tap_free[buf])
                    sums = tap_free[buf] = pool.do(lambda e: e.tensor_tensor(out, out, tap, ALU.add), t, sums)
                    if i == 30:
                        cv_tok[k] = sums
                        total(m.CV[:, k, :], k, 512, sums)
                    yield True

        tap_free = [None] * 4
        apart.append(convolve_apart((1, 3, 5)))
        state["pace"] = 1.0
        for c in range(4):
            at = {}

            def evac_a(t, acc, tok):
                at[t] = act.do(lambda e: e.activation(m.AB[:, c % 2, t, :], acc, ACT.Identity,
                                                      bias=pv("cv_b1_2", 2 * c + t, 0)), tok, ab_free[c % 2])
                return at[t]

            def evac_g(t, acc, tok):
                k = 2 * c + t
                r = act.do(lambda e: e.activation(m.SGM[:, t, :], acc, ACT.Sigmoid,
                                                  bias=pv("cv_b1_2", k, 1)), tok, sg_free[t])
                u = dve.do(lambda e: e.tensor_tensor(
                    m.U[:, k, :, 15:271], m.AB[:, c % 2, t, :].rearrange("p (s t) -> p s t", s=2),
                    m.SGM[:, t, :].rearrange("p (s t) -> p s t", s=2), ALU.mult), r, at[t], pads)
                sg_free[t] = u
                if t == 1:
                    ab_free[c % 2] = u
                ut[k] = u
                if c < 3 and t == 0:
                    background.append(convolve((k,)))
                elif c == 3 and t == 1:
                    background.append(convolve((k - 1, k)))
                return r

            if c == 0:
                sg_free = [None, None]
            linear(w, 0, KT, c * 256, 256, xh, xl, xt, evac_a, adv=7, outer=c == 0)
            linear(w, 0, KT, 1024 + c * 256, 256, xh, xl, xt, evac_g, adv=7)
        state["pace"] = state["credit"] = 0.0
        while mod_next[0] < 45:
            mod_unit()
            advance(8)
            flush()
        totals(4)
        folds()
        while apart:
            advance()
        drain()
        totals(KT)
        tables(LNEXP)
        r = act.do(lambda e: e.activation(m.RS[:, :], ps[6][:, :], ACT.Copy, scale=-1.0 / D), stat["tok"], rs_free[0])
        bank_free[6] = r
        for k in range(KT):
            cv_tok[k] = dve.do(lambda e: e.tensor_tensor(m.CV[:, k, :], m.CV[:, k, :], m.RS[:, :], ALU.add),
                               r, cv_tok[k])
            sumsq(m.CV[:, k, :], k, 512, cv_tok[k], 2)
            flush()
        flush()
        rs_free[0] = cv_tok[KT - 1]
        r = rstd(512, D, m.RS[:, :])
        free = (m.sem["pe"], pe.n)
        toks = []
        tables(SILU)
        scaled = []
        for k in range(KT + 2):
            if k < KT:
                scaled.append(dve.do(lambda e: e.scalar_tensor_tensor(
                    out=m.CV[:, k, :], in0=m.CV[:, k, :], scalar=pv("cv_ln_g_2", k), in1=m.RS[:, :],
                    op0=ALU.mult, op1=ALU.mult), r, cv_tok[k]))
            if k >= 2:
                i = k - 2
                t = act.do(lambda e: e.activation(m.CV[:, i, :], m.CV[:, i, :], ACT.Silu, bias=pv("cv_ln_b_2", i)),
                           scaled[i])
                toks.append(halves(m.XN[:, 0, i, :], m.XN[:, 1, i, :], m.CV[:, i, :], t, free))
        tables(LNEXP)
        rs_free[0] = toks[-1]
        gate = modcol(layer, 2)
        w2 = T["cv_w2_2"][0]
        for c in range(4):
            def evac(t, acc, tok):
                j = 2 * c + t
                buf = t
                y = act.do(lambda e: e.activation(m.AB[:, 0, buf, :], acc, ACT.Identity, bias=pv("cv_b2_2", j)),
                           tok, ab2_free[buf])
                ab2_free[buf] = residual(j, 512, gate, m.AB[:, 0, buf, :], y, True)
                return y
            if c == 0:
                ab2_free = [None, None]
            linear(w2, 0, KT, c * 256, 256, xh, xl, toks, evac, outer=c == 0)

    def shortconv(layer):
        xt = norm(512, lambda k, s: m.gs[:, layer, 0, k, s:s + 1], modcol(layer, 0))
        xh, xl = xn(0, 512)
        w = T["sc_win_2"][0]
        pads = [pool.do(lambda e, a=a: e.memset(m.UP[:, :, :, :, a:a + 1], 0.0), xt[KT - 1]) for a in (0, 257)]
        y = [None] * KT
        cgt, uft, cot = {}, {}, {}
        cg_free = [None, None]
        up_free = [None, None]
        co_free = [None, None]
        for c in range(4):
            buf = c % 2

            def evac_c(t, acc, tok):
                cgt[t] = act.do(lambda e: e.activation(m.CG[:, buf, t, :], acc, ACT.Copy), tok, cg_free[buf])
                return cgt[t]

            def evac_v(t, acc, tok):
                uft[t] = dve.do(lambda e: e.tensor_tensor(
                    m.UP[:, buf, t, :, 1:257], acc.rearrange("p (s t) -> p s t", s=2),
                    m.CG[:, buf, t, :].rearrange("p (s t) -> p s t", s=2), ALU.mult), tok, cgt[t], up_free[buf])
                if t == 1:
                    cg_free[buf] = uft[1]
                return uft[t]

            def evac_b(t, acc, tok):
                k = 2 * c + t
                r = dve.do(lambda e: e.tensor_tensor(m.CO[:, buf, t, :], acc, m.CO[:, buf, t, :], ALU.mult),
                           tok, cot[t])
                y[k] = (r, buf, t)
                return r

            linear(w, 0, KT, 1024 + c * 256, 256, xh, xl, xt, evac_c, outer=c == 0)
            linear(w, 0, KT, 2048 + c * 256, 256, xh, xl, xt, evac_v)
            for t in range(2):
                k = 2 * c + t
                out = m.CO[:, buf, t, :].rearrange("p (s t) -> p s t", s=2)
                r = dve.do(lambda e: e.tensor_scalar(out, m.UP[:, buf, t, :, 0:S], pv("sc_conv_2", k, 0), None,
                                                     ALU.mult), uft[t], pads, co_free[buf])
                for i in (1, 2):
                    r = dve.do(lambda e, i=i: e.scalar_tensor_tensor(
                        out=out, in0=m.UP[:, buf, t, :, i:i + S], scalar=pv("sc_conv_2", k, i), in1=out,
                        op0=ALU.mult, op1=ALU.add), r)
                cot[t] = r
            up_free[buf] = r
            linear(w, 0, KT, c * 256, 256, xh, xl, xt, evac_b)
            done = []
            for t in range(2):
                k = 2 * c + t
                r = y[k][0]
                y[k] = halves(m.YH[:, 0, k, :], m.YH[:, 1, k, :], m.CO[:, buf, t, :], r)
                done.append(y[k])
            co_free[buf] = done
        yh, yl = (lambda k: m.YH[:, 0, k, :]), (lambda k: m.YH[:, 1, k, :])
        grow(yh, yl, y, 512, modcol(layer, 2), T["sc_wout_2"][0])

    def mlp(layer, n):
        xt = norm(n, lambda k, s: m.gs[:, layer, 1, k, s:s + 1], modcol(layer, 3))
        xh, xl = xn(0, n)
        w1, w2 = T["mlp_w1_2"][layer], T["mlp_w2_2"][layer]
        gate = modcol(layer, 5)
        h_free = [None, None]
        htok = {}
        rl_free = [None] * 4
        nrl = [0]

        def up(q):
            buf = q % 2
            toks = [None] * KT
            for c in range(4):
                def evac(t, acc, tok):
                    r = nrl[0] % 4
                    nrl[0] += 1
                    a = act.do(lambda e: e.activation(m.RL[:, r, 0:n], acc, ACT.Relu), tok, rl_free[r])
                    d = dve.do(lambda e: e.tensor_tensor(m.RL[:, r, 0:n], acc, m.RL[:, r, 0:n], ALU.mult), a, tok)
                    k = 2 * c + t
                    toks[k] = halves(m.H2[:, buf, 0, k, 0:n], m.H2[:, buf, 1, k, 0:n], m.RL[:, r, 0:n], d, h_free[buf])
                    rl_free[r] = toks[k]
                    return d
                linear(w1, 0, KT, q * D + c * 256, 256, xh, xl, xt, evac, outer=q + c == 0)
            htok[q] = toks

        def down(q):
            buf = q % 2
            hh, hl = (lambda k: m.H2[:, buf, 0, k, 0:n]), (lambda k: m.H2[:, buf, 1, k, 0:n])
            for c in range(4):
                def evac(t, acc, tok):
                    h_free[buf] = tok
                    return residual(2 * c + t, n, gate, acc, tok, q == 3)
                linear(w2, q * D, KT, c * 256, 256, hh, hl, htok[q], evac)

        up(0)
        for q in range(4):
            if q + 1 < 4:
                up(q + 1)
            down(q)

    neighbourhood(0, 0, True)
    mlp(0, 512)
    conformer(1)
    mlp(1, 512)
    shortconv(2)
    mlp(2, 512)
    fill(48 - mod_next[0])
    folds()
    neighbourhood(3, 1, False)
    mlp(3, S)

    flush()
    r = rstd(S, D, m.RS[:, 0:S])
    for k in range(KT):
        t = dve.do(lambda e: e.scalar_tensor_tensor(out=m.X[:, k, 0:S], in0=m.X[:, k, 0:S], scalar=pv("final_g_2", k),
                                                    in1=m.RS[:, 0:S], op0=ALU.mult, op1=ALU.mult), r)
        half, end = divmod(k, KT // 2)
        if end == KT // 2 - 1:
            at = half * KT // 2
            sp.dma(T["out"][:, at:k + 1, :], m.X[:, at:k + 1, 0:S], m.sem["out"], t)
    sp.wait([(m.sem["out"], 32)])
    return order, {"pe": pe, "act": act, "dve": dve, "pool": pool, "sp": sp}


def build(nc, T):
    with ExitStack() as ctx:
        m = allocate(nc, ctx)
        units, _ = program(m, T, None)
        _, q = program(m, T, units)
        block = ctx.enter_context(nc.Block())

        @block.sync
        def _(e):
            for f in q["sp"].ops:
                f(e)

        @block.tensor
        def _(e):
            for f in q["pe"].ops:
                f(e)

        @block.scalar
        def _(e):
            for f in q["act"].ops:
                f(e)

        @block.vector
        def _(e):
            for f in q["dve"].ops:
                f(e)

        @block.gpsimd
        def _(e):
            for f in q["pool"].ops:
                f(e)


_INS = ["positions", "attn_w_in", "attn_w_out", "mlstm_w_in", "mlstm_w_out", "ffn_w_in", "ffn_w_out", "mod_w_2",
        "mlp_w1_2", "mlp_w2_2", "na_wqkv_2", "na_wo_2", "na_rpb_2", "cv_w1_2", "cv_w2_2", "sc_win_2", "sc_wout_2"]


def feature_major(a):
    return np.ascontiguousarray(np.asarray(a).reshape(-1, KT, P).transpose(2, 1, 0))


def lay_out(inputs):
    arrays = {name: np.ascontiguousarray(inputs[name]) for name in _INS}
    arrays["x"] = feature_major(inputs["x"])
    arrays["ctx_2"] = feature_major(inputs["ctx_2"])
    arrays["params"] = feature_major(np.concatenate([np.asarray(inputs[n]).reshape(k, D) for n, k in ROWS]))
    arrays["gate_bias"] = np.ascontiguousarray(np.concatenate([inputs["mlstm_ig_bias"], inputs["mlstm_fg_bias"]]).T)
    arrays["consts"] = constants()
    return arrays


def kernel(**inputs):
    import concourse.bacc as _bacc
    from concourse.bass_utils import run_bass_kernel_spmd as _run

    nc = _bacc.Bacc("TRN2", target_bir_lowering=False, num_devices=1)
    arrays = lay_out(inputs)
    T = {n: nc.dram_tensor(f"in_{n}", a.shape, mybir.dt.from_np(a.dtype), kind="ExternalInput").ap()
         for n, a in arrays.items()}
    T["out"] = nc.dram_tensor("out_0", (P, KT, S), F32, kind="ExternalOutput").ap()
    build(nc, T)
    r = _run(nc, [{f"in_{n}": a for n, a in arrays.items()}], core_ids=[0])
    return np.ascontiguousarray(r.results[0]["out_0"].transpose(2, 1, 0)).reshape(1, S, D)
```
